# Optimizing a Trainium2 kernel written in Bass

```python
import jax
import jax.numpy as jnp
from jax import lax
import numpy as np

D_MODEL = 1024
BATCH = 1
SEQ = 512
DEPTH = 1

EPS = 1e-6
GLA_HEADS = 4
GLA_DK = 64
GLA_DV = 128
GLA_GATE_RANK = 16
GLA_TAU = 16.0
GLA_CHUNK = 64
DSA_HEADS = 8
DSA_Q_RANK = 256
DSA_KV_RANK = 128
DSA_HEAD_DIM = 64
DSA_V_DIM = 64
IDX_HEADS = 8
IDX_DIM = 32
DSA_TOPK_MAX = 256
Q_BLOCK = 128
MLSTM_HEADS = 4
MLSTM_DQK = 64
MLSTM_DV = 128
MLSTM_CONV = 4
MLSTM_CHUNK = 64
N_EXPERTS = 64
TOP_K = 6
N_GROUPS = 8
TOPK_GROUPS = 4
EXPERT_FF = 256
SHARED_FF = 256
ROUTED_SCALE = 2.5
TOKEN_BLOCK = 128

GLA_QK = GLA_HEADS * GLA_DK
GLA_V = GLA_HEADS * GLA_DV
DSA_V = DSA_HEADS * DSA_V_DIM
MLSTM_QK = MLSTM_HEADS * MLSTM_DQK
MLSTM_V = MLSTM_HEADS * MLSTM_DV
IN_SIZES = (GLA_QK, GLA_QK, GLA_V, GLA_V, GLA_GATE_RANK,
            DSA_Q_RANK, DSA_KV_RANK, IDX_DIM, IDX_HEADS,
            MLSTM_QK, MLSTM_QK, MLSTM_V, MLSTM_HEADS, MLSTM_HEADS, MLSTM_V,
            3 * D_MODEL)
N_IN = sum(IN_SIZES)

kernel_name = 'hybrid_gla_dsa_mlstm_moe'

def _rms(x, g):
    xf = x.astype(jnp.float32)
    y = xf * lax.rsqrt(jnp.mean(xf * xf, axis=-1, keepdims=True) + EPS)
    return (y * g.astype(jnp.float32)).astype(x.dtype)

def _head_rms(x, g):
    xf = x.astype(jnp.float32)
    y = xf * lax.rsqrt(jnp.mean(xf * xf, axis=-1, keepdims=True) + EPS)
    return y.reshape(x.shape[0], x.shape[1], -1) * g.astype(jnp.float32)

def _to_chunks(t, L):
    b, s = t.shape[0], t.shape[1]
    return jnp.moveaxis(t.reshape((b, s // L, L) + t.shape[2:]), 1, 0)

def _from_chunks(t):
    t = jnp.moveaxis(t, 0, 1)
    return t.reshape((t.shape[0], t.shape[1] * t.shape[2]) + t.shape[3:])

def _causal_dwconv(x, w):
    K, C = w.shape
    return lax.conv_general_dilated(x, w[:, None, :].astype(x.dtype), window_strides=(1,),
                                    padding=[(K - 1, 0)], dimension_numbers=('NWC', 'WIO', 'NWC'),
                                    feature_group_count=C)

def _gla(q, k, v, log_a):
    f32 = jnp.float32
    b, s, nh, dk = q.shape
    dv = v.shape[-1]
    L = GLA_CHUNK
    causal = jnp.tril(jnp.ones((L, L), dtype=bool))[None, :, :, None, None]
    xs = tuple(_to_chunks(t.astype(f32), L) for t in (q * dk ** -0.5, k, v, log_a))

    def step(state, inp):
        qb, kb, vb, ab = inp
        cum = jnp.cumsum(ab, axis=1)
        inter = jnp.einsum('blhk,bhkv->blhv', qb * jnp.exp(cum), state)
        rel = jnp.exp(jnp.where(causal, cum[:, :, None] - cum[:, None, :], -jnp.inf))
        scores = jnp.einsum('bthk,btshk,bshk->btsh', qb, rel, kb)
        intra = jnp.einsum('btsh,bshv->bthv', scores, vb)
        tot = cum[:, -1]
        k_dec = kb * jnp.exp(tot[:, None] - cum)
        state = state * jnp.exp(tot)[..., None] + jnp.einsum('blhk,blhv->bhkv', k_dec, vb)
        return state, inter + intra

    _, out = lax.scan(step, jnp.zeros((b, nh, dk, dv), f32), xs)
    return _from_chunks(out)

def _mlstm(q, k, v, i_pre, log_f):
    f32 = jnp.float32
    b, s, nh, dk = q.shape
    dv = v.shape[-1]
    L = MLSTM_CHUNK
    causal = jnp.tril(jnp.ones((L, L), dtype=bool))[None, :, :, None]
    xs = tuple(_to_chunks(t.astype(f32), L) for t in (q * dk ** -0.5, k, v, i_pre, log_f))

    def step(carry, inp):
        C, n, m = carry
        qb, kb, vb, ib, fb = inp
        bcum = jnp.cumsum(fb, axis=1)
        dlog = jnp.where(causal, bcum[:, :, None] - bcum[:, None, :] + ib[:, None], -jnp.inf)
        inter_log = bcum + m[:, None]
        m_t = jnp.maximum(inter_log, jnp.max(dlog, axis=2))
        w_intra = jnp.exp(dlog - m_t[:, :, None])
        w_inter = jnp.exp(inter_log - m_t)
        qk = jnp.einsum('bthk,bshk->btsh', qb, kb) * w_intra
        num = jnp.einsum('btsh,bshv->bthv', qk, vb) + w_inter[..., None] * jnp.einsum('bthk,bhkv->bthv', qb, C)
        den = jnp.sum(qk, axis=2) + w_inter * jnp.einsum('bthk,bhk->bth', qb, n)
        h = num / jnp.maximum(jnp.abs(den), jnp.exp(-m_t))[..., None]
        tot = bcum[:, -1]
        g_log = tot[:, None] - bcum + ib
        m_new = jnp.maximum(tot + m, jnp.max(g_log, axis=1))
        w_s = jnp.exp(g_log - m_new[:, None])
        w_c = jnp.exp(tot + m - m_new)
        C = C * w_c[..., None, None] + jnp.einsum('blh,blhk,blhv->bhkv', w_s, kb, vb)
        n = n * w_c[..., None] + jnp.einsum('blh,blhk->bhk', w_s, kb)
        return (C, n, m_new), h

    init = (jnp.zeros((b, nh, dk, dv), f32), jnp.zeros((b, nh, dk), f32), jnp.zeros((b, nh), f32))
    _, out = lax.scan(step, init, xs)
    return _from_chunks(out)

def _dsa(cq, ckv, k_idx, w_idx, w_uq, w_uk, w_uv, w_qi):
    f32 = jnp.float32
    b, s, _ = cq.shape
    topk = min(DSA_TOPK_MAX, s // 4)
    q = jnp.einsum('bsr,rhd->bshd', cq, w_uq)
    q_lat = jnp.einsum('bshd,chd->bshc', q, w_uk) * DSA_HEAD_DIM ** -0.5
    q_idx = jnp.einsum('bsr,rhd->bshd', cq, w_qi) * IDX_DIM ** -0.5
    w_head = w_idx * IDX_HEADS ** -0.5
    slopes = 2.0 ** (-8.0 * jnp.arange(1, DSA_HEADS + 1, dtype=f32) / DSA_HEADS)
    key_pos = jnp.arange(s)

    def block(inp):
        ql, qi, wh, pos = inp
        idx_scores = jnp.einsum('bthd,bsd->bths', qi, k_idx)
        I = jnp.einsum('bth,bths->bts', wh, jax.nn.relu(idx_scores)).astype(f32)
        I = jnp.where((key_pos[None, :] <= pos[:, None])[None], I, -jnp.inf)
        _, sel = lax.top_k(I, topk)
        kv = jax.vmap(lambda cb, ib: cb[ib])(ckv, sel)
        dist = (pos[None, :, None] - sel).astype(f32)
        logits = jnp.einsum('bthr,btkr->bthk', ql, kv).astype(f32) - slopes[:, None] * dist[:, :, None, :]
        logits = jnp.where((dist >= 0)[:, :, None, :], logits, -jnp.inf)
        p = jax.nn.softmax(logits, axis=-1).astype(kv.dtype)
        return jnp.einsum('bthk,btkr->bthr', p, kv)

    xs = (_to_chunks(q_lat, Q_BLOCK), _to_chunks(q_idx, Q_BLOCK), _to_chunks(w_head, Q_BLOCK),
          key_pos.reshape(-1, Q_BLOCK))
    o_lat = _from_chunks(lax.map(block, xs))
    o = jnp.einsum('bshr,rhv->bshv', o_lat, w_uv)
    return o.reshape(b, s, -1)

def _hybrid_mixer(h, w_in, gla_w_a2, gla_b_a, gla_norm, dsa_norm_q, dsa_norm_kv, dsa_w_uq, dsa_w_uk,
                  dsa_w_uv, dsa_w_qi, mlstm_conv, mlstm_b_i, mlstm_b_f, mlstm_norm,
                  w_up_a, w_up_b, w_up_c, w_o):
    b, s, _ = h.shape
    f32 = jnp.float32
    split_points = [int(v) for v in np.cumsum(IN_SIZES)[:-1]]
    (qa, ka, va, ga, a_lr, cq, ckv, k_idx, w_idx,
     qc, kc, vc, ic, fc, oc, gates) = jnp.split(h @ w_in, split_points, axis=-1)

    log_a = jax.nn.log_sigmoid((a_lr @ gla_w_a2 + gla_b_a).astype(f32)) / GLA_TAU
    oa = _gla(qa.reshape(b, s, GLA_HEADS, GLA_DK), ka.reshape(b, s, GLA_HEADS, GLA_DK),
              va.reshape(b, s, GLA_HEADS, GLA_DV), log_a.reshape(b, s, GLA_HEADS, GLA_DK))
    ya = (_head_rms(oa, gla_norm) * jax.nn.silu(ga.astype(f32))).astype(h.dtype) @ w_up_a

    ob = _dsa(_rms(cq, dsa_norm_q), _rms(ckv, dsa_norm_kv), k_idx, w_idx,
              dsa_w_uq, dsa_w_uk, dsa_w_uv, dsa_w_qi)
    yb = ob @ w_up_b

    qk = jax.nn.silu(_causal_dwconv(jnp.concatenate([qc, kc], axis=-1), mlstm_conv))
    qc, kc = jnp.split(qk, 2, axis=-1)
    i_pre = (ic + mlstm_b_i).astype(f32)
    log_f = jax.nn.log_sigmoid((fc + mlstm_b_f).astype(f32))
    o_c = _mlstm(qc.reshape(b, s, MLSTM_HEADS, MLSTM_DQK), kc.reshape(b, s, MLSTM_HEADS, MLSTM_DQK),
                 vc.reshape(b, s, MLSTM_HEADS, MLSTM_DV), i_pre, log_f)
    yc = (_head_rms(o_c, mlstm_norm) * jax.nn.sigmoid(oc.astype(f32))).astype(h.dtype) @ w_up_c

    g_a, g_b, g_c = jnp.split(jax.nn.sigmoid(gates.astype(f32)).astype(h.dtype), 3, axis=-1)
    return (g_a * ya + g_b * yb + g_c * yc) @ w_o

def _moe(h, router_w, router_bias, w_gate, w_up, w_down, s_gate, s_up, s_down):
    b, s, d = h.shape
    t = h.reshape(-1, d)
    scores = jax.nn.sigmoid(jnp.einsum('td,de->te', t, router_w).astype(jnp.float32))
    sel = scores + router_bias.astype(jnp.float32)
    grp = sel.reshape(-1, N_GROUPS, N_EXPERTS // N_GROUPS)
    grp_score = jnp.sum(lax.top_k(grp, 2)[0], axis=-1)
    _, grp_idx = lax.top_k(grp_score, TOPK_GROUPS)
    grp_mask = jnp.sum(jax.nn.one_hot(grp_idx, N_GROUPS, dtype=jnp.float32), axis=1) > 0
    sel = jnp.where(jnp.repeat(grp_mask, N_EXPERTS // N_GROUPS, axis=1), sel, -jnp.inf)
    _, idx = lax.top_k(sel, TOP_K)
    w = jnp.take_along_axis(scores, idx, axis=1)
    w = w / jnp.sum(w, axis=-1, keepdims=True) * ROUTED_SCALE
    gates = jnp.sum(jax.nn.one_hot(idx, N_EXPERTS, dtype=jnp.float32) * w[..., None], axis=1)

    def block(inp):
        xb, gb = inp
        a = jnp.einsum('td,edf->tef', xb, w_gate)
        u = jnp.einsum('td,edf->tef', xb, w_up)
        return jnp.einsum('tef,efd->td', jax.nn.silu(a) * u * gb[..., None], w_down)

    xs = (t.reshape(-1, TOKEN_BLOCK, d), gates.astype(t.dtype).reshape(-1, TOKEN_BLOCK, N_EXPERTS))
    routed = lax.map(block, xs).reshape(-1, d)
    shared = (jax.nn.silu(t @ s_gate) * (t @ s_up)) @ s_down
    return (routed + shared).reshape(b, s, d)

def setup_inputs(seed: int = 0) -> dict:
    key = jax.random.key(seed)
    keys = jax.random.split(key, 40)
    cnt = [0]

    def nxt():
        cnt[0] += 1
        return keys[cnt[0] - 1]

    def nrm(shape, scale):
        return jax.random.normal(nxt(), shape, jnp.float32) * scale

    def gain(shape):
        return 1.0 + 0.05 * jax.random.normal(nxt(), shape, jnp.float32)

    D, L, E, F = D_MODEL, DEPTH, N_EXPERTS, EXPERT_FF
    return {
        'x': nrm((BATCH, SEQ, D), 1.0),
        'c': nrm((BATCH, D), 1.0),
        'ada_w': nrm((L, D, 6 * D), 0.3 * D ** -0.5),
        'ada_b': nrm((L, 6 * D), 0.02),
        'norm_mix': gain((L, D)),
        'norm_ffn': gain((L, D)),
        'w_in': nrm((L, D, N_IN), D ** -0.5),
        'gla_w_a2': nrm((L, GLA_GATE_RANK, GLA_QK), GLA_GATE_RANK ** -0.5),
        'gla_b_a': nrm((L, GLA_QK), 0.1),
        'gla_norm': gain((L, GLA_V)),
        'dsa_norm_q': gain((L, DSA_Q_RANK)),
        'dsa_norm_kv': gain((L, DSA_KV_RANK)),
        'dsa_w_uq': nrm((L, DSA_Q_RANK, DSA_HEADS, DSA_HEAD_DIM), DSA_Q_RANK ** -0.5),
        'dsa_w_uk': nrm((L, DSA_KV_RANK, DSA_HEADS, DSA_HEAD_DIM), DSA_KV_RANK ** -0.5),
        'dsa_w_uv': nrm((L, DSA_KV_RANK, DSA_HEADS, DSA_V_DIM), DSA_KV_RANK ** -0.5),
        'dsa_w_qi': nrm((L, DSA_Q_RANK, IDX_HEADS, IDX_DIM), DSA_Q_RANK ** -0.5),
        'mlstm_conv': nrm((L, MLSTM_CONV, 2 * MLSTM_QK), MLSTM_CONV ** -0.5),
        'mlstm_b_i': nrm((L, MLSTM_HEADS), 0.1),
        'mlstm_b_f': 3.0 + nrm((L, MLSTM_HEADS), 0.5),
        'mlstm_norm': gain((L, MLSTM_V)),
        'w_up_a': nrm((L, GLA_V, D), GLA_V ** -0.5),
        'w_up_b': nrm((L, DSA_V, D), DSA_V ** -0.5),
        'w_up_c': nrm((L, MLSTM_V, D), MLSTM_V ** -0.5),
        'w_o': nrm((L, D, D), D ** -0.5),
        'router_w': nrm((L, D, E), D ** -0.5),
        'router_bias': nrm((L, E), 0.01),
        'exp_w_gate': nrm((L, E, D, F), D ** -0.5),
        'exp_w_up': nrm((L, E, D, F), D ** -0.5),
        'exp_w_down': nrm((L, E, F, D), F ** -0.5),
        'sh_w_gate': nrm((L, D, SHARED_FF), D ** -0.5),
        'sh_w_up': nrm((L, D, SHARED_FF), D ** -0.5),
        'sh_w_down': nrm((L, SHARED_FF, D), SHARED_FF ** -0.5),
        'norm_final': gain((D,)),
    }

def reference(x, c, ada_w, ada_b, norm_mix, norm_ffn, w_in, gla_w_a2, gla_b_a, gla_norm,
              dsa_norm_q, dsa_norm_kv, dsa_w_uq, dsa_w_uk, dsa_w_uv, dsa_w_qi,
              mlstm_conv, mlstm_b_i, mlstm_b_f, mlstm_norm,
              w_up_a, w_up_b, w_up_c, w_o,
              router_w, router_bias, exp_w_gate, exp_w_up, exp_w_down,
              sh_w_gate, sh_w_up, sh_w_down, norm_final):
    cs = jax.nn.silu(c)
    for l in range(DEPTH):
        mod = cs @ ada_w[l] + ada_b[l]
        sh1, sc1, g1, sh2, sc2, g2 = jnp.split(mod[:, None, :], 6, axis=-1)
        h = _rms(x, norm_mix[l]) * (1 + sc1) + sh1
        x = x + g1 * _hybrid_mixer(h, w_in[l], gla_w_a2[l], gla_b_a[l], gla_norm[l],
                                   dsa_norm_q[l], dsa_norm_kv[l], dsa_w_uq[l], dsa_w_uk[l],
                                   dsa_w_uv[l], dsa_w_qi[l], mlstm_conv[l], mlstm_b_i[l],
                                   mlstm_b_f[l], mlstm_norm[l], w_up_a[l], w_up_b[l],
                                   w_up_c[l], w_o[l])
        h = _rms(x, norm_ffn[l]) * (1 + sc2) + sh2
        x = x + g2 * _moe(h, router_w[l], router_bias[l], exp_w_gate[l], exp_w_up[l],
                          exp_w_down[l], sh_w_gate[l], sh_w_up[l], sh_w_down[l])
    return _rms(x, norm_final)


_drawn_inputs = setup_inputs


def setup_inputs(seed=0):
    import zlib

    import numpy as np

    out = dict(_drawn_inputs(seed))
    spreads = {}
    factors = {'norm_mix': 3.093,
     'gla_w_a2': 4.289,
     'gla_b_a': 7.171,
     'gla_norm': 7.774,
     'dsa_norm_q': 4.47,
     'dsa_norm_kv': 6.565,
     'mlstm_b_i': 64.0,
     'mlstm_b_f': 2.824,
     'mlstm_norm': 33.679,
     'norm_ffn': 4.082,
     'router_bias': 4.384}
    for name, (base, spread) in spreads.items():
        noise = np.random.default_rng([zlib.crc32(name.encode()), seed]).standard_normal(out[name].shape)
        drawn = base * np.exp(spread * noise) if base else spread * noise
        out[name] = jnp.asarray(drawn.astype(out[name].dtype))
    for name, factor in factors.items():
        out[name] = (out[name] * factor).astype(out[name].dtype)
    return out
```

```python
from contextlib import ExitStack

import numpy as np

import concourse.bass as bass
from concourse import mybir

F32 = mybir.dt.float32
I32 = mybir.dt.int32
U32 = mybir.dt.uint32
ALU = mybir.AluOpType
ACT = mybir.ActivationFunctionType
AX = mybir.AxisListType.X

P = 128
BANKS = 8
EPS = 1e-6
NEG_MASK = -1e30
NEG_FUTURE = -1e38
NEG_TAKEN = -3e38

IN_SIZES = dict(qa=256, ka=256, va=512, ga=512, a_lr=16, cq=256, ckv=128, k_idx=32, w_idx=8,
                qc=256, kc=256, vc=512, ic=4, fc=4, oc=512, gates=3072)
COL = {}
_at = 0
for _n, _w in IN_SIZES.items():
    COL[_n] = _at
    _at += _w


def tile_cols(i, n=P):
    return slice(i * n, (i + 1) * n)


def product_order():
    out = [("params", "params_ready", 1)]
    out += [(f"mc{c}", "mc_ready", c + 1) for c in range(4)]
    out += [(f"xT{j}", "hT_ready", j + 1) for j in range(8)]
    out += [("small", "small_ready", 1)]
    out += [(f"la{f}", "z_ready", f + 1) for f in range(2)]
    out += [(f"qa{f}", "qa_ready", f + 1) for f in range(2)]
    out += [(f"ka{f}", "ka_ready", f + 1) for f in range(2)]
    out += [(f"va{i}", "v_ready", i + 1) for i in range(4)]
    out += [(f"kd{f}", "kdr_ready", f + 1) for f in range(2)]
    out += [(f"st{i}{f}", "state_ready", 2 * i + f + 1) for i in range(3) for f in range(2)]
    out += [(f"scA{l}{g}", "intra_done", 4 * l + g + 1) for l in range(8) for g in range(4)]
    out += [(f"ga{m}", "outgate_ready", m + 1) for m in range(4)]
    for h in range(5):
        out += [(f"oA{h}", "oA_read", h + 1)] if h < 4 else []
        out += [(f"msA{h - 1}", "root_ready", h)] if h >= 1 else []
    out += [(f"qk{f}", "qk_ready", f + 1) for f in range(4)]
    out += [("uT", "u_ready", 1)]
    out += [(f"vc{i}", "v_ready", i + 5) for i in range(4)]
    out += [(f"oc{m}", "outgate_ready", m + 5) for m in range(4)]
    for h in range(4):
        out += [(f"bm{h}", "SW_ready", 4 * h + 4), (f"bt{h}", "floor_ready", h + 1)]
        out += [(f"scC{h}{j}", "SW_ready", 4 * h + j + 1) for j in range(4)]
        out += [(f"num{h}", "hC_ready", h + 1), (f"den{h}", "den_read", h + 1)]
        out += [(f"msC{h}", "root_ready", h + 5)]
    out += [("kidx", "kidx_ready", 1)]
    out += [(f"cl{n}", "craw_ready", n + 1) for n in range(3)]
    out += [("msq", "root_ready", 9), ("mskv", "root_ready", 10)]
    out += [("wi", "wcol_ready", 1), ("uk", "ukT_ready", 1)]
    out += [("ckr", "ckr_ready", 1)]
    out += [(f"qi{m}", "qi_ready", m + 1) for m in range(2)]
    out += [(f"ix{i}{h}", "relu_ready", 8 * (i - 1) + h + 1) for i in range(1, 4) for h in range(8)]
    out += [(f"q{m}", "q_ready", m + 1) for m in range(4)]
    out += [(f"ql{h}", "ql_ready", h + 1) for h in range(8)]
    for i in range(4):
        out += [(f"lg{i}{h}", "L_ready", 8 * i + h + 1) for h in range(8)]
        for g in range(2):
            n = 2 * (i * (i + 1) // 2) + g * (i + 1)
            out += [(f"pt{i}{g}{j}", "PT_ready", n + j + 1) for j in range(i + 1)]
            out += [(f"ol{i}{g}", "ol_ready", 2 * i + g + 1)]
    out += [(f"ob{m}", "oTB_ready", m + 1) for m in range(4)]
    out += [(f"mb{c}", "mb_ready", c + 1) for c in range(8)]
    for m in range(8):
        for b in range(3):
            out += [(f"gate{m}{b}", "gate_ready", 3 * m + b + 1), (f"up{m}{b}", "up_read", 3 * m + b + 1)]
    out += [(f"wo{i}{n}", "wo_read", 2 * i + n + 1) for i in range(4) for n in range(2)]
    out += [(f"hT2{j}", "h2T_ready", j + 1) for j in range(8)]
    out += [(f"rt{i}", "rt_ready", i + 1) for i in range(4)]
    out += [(f"pos{i}", "slot_done", i + 1) for i in range(4)] + [("tot", "tot_read", 1), ("ue", "ue_ready", 1)]
    out += [("uc", "uc_ready", 1)]
    out += [(x, n, v) for m in range(2) for x, n, v in ((f"sg{m}", "sg_ready", m + 1), (f"su{m}", "actS_ready", m + 1))]
    out += [(f"sd{i}{n}", "sd_read", 2 * i + n + 1) for i in range(4) for n in range(2)]
    return out


def hybrid_kernel(nc, a, out):
    T, D = a["x"].shape[1:]
    TT, KT = T // P, D // P
    E = a["router_w"].shape[2]
    FF = a["exp_w_gate"].shape[3]
    TOPK, GROUPS, TOPG = 6, 8, 4
    KEYS = T // 4
    UNITS = E + T * TOPK // P
    assert (T, D, TT, KT, E, FF) == (512, 1024, 4, 8, 64, 256)

    products = product_order()
    number = {name: n for n, (name, _, _) in enumerate(products)}
    assert len(number) == len(products)

    ctx = ExitStack()
    with ctx:
        sems = {}

        def sem(name):
            if name not in sems:
                sems[name] = ctx.enter_context(nc.semaphore(name))
            return sems[name]

        def sb(name, shape, dt=F32):
            return ctx.enter_context(nc.sbuf_tensor(name, shape, dt))

        bank = [ctx.enter_context(nc.psum_tensor(f"bank{i}", [P, 512], F32)) for i in range(BANKS)]

        x = sb("x", [P, TT, D])
        hT = sb("hT", [P, KT, T])
        oT = [sb(f"oT{b}", [P, 4, T]) for b in "ABC"]
        RING = 3
        ring = sb("ring", [P, RING, 4096])
        arena = sb("arena", [P, 22528])
        ident = sb("ident", [P, P])
        ones = sb("ones", [P, P])
        causal = sb("causal", [P, P])
        before = sb("before", [P, P])
        future = sb("future", [P, P], I32)
        negc = sb("negc", [P, P])
        small = sb("small", [P, T])
        prow = sb("prow", [53, P])
        par = sb("par", [P, 53])
        stat = sb("stat", [P, 16])
        epsc = sb("epsc", [P, 1])
        cs = sb("cs", [P, 8])
        c_in = sb("c_in", [P, 8])
        mod1 = sb("mod1", [P, 16])
        bif = sb("bif", [4, 2])
        iota_e = sb("iota_e", [P, E])
        wcol = sb("wcol", [P, TT, 8])

        class Region:
            def __init__(self, tensor, start=0, end=None):
                self.t, self.at, self.end = tensor, start, end

            def take(self, *shape, dt=F32, parts=P):
                n = int(np.prod(shape))
                assert self.end is None or self.at + n <= self.end, (self.at, n, self.end)
                v = self.t[0:parts, self.at:self.at + n]
                if dt != F32:
                    v = v.bitcast(dt)
                self.at += n
                if len(shape) == 2:
                    v = v.rearrange("p (a b) -> p a b", a=shape[0])
                elif len(shape) == 3:
                    v = v.rearrange("p (a b c) -> p a b c", a=shape[0], b=shape[1])
                elif len(shape) == 4:
                    v = v.rearrange("p (a b c d) -> p a b c d", a=shape[0], b=shape[1], c=shape[2])
                return v

        END = 22528
        r0 = Region(arena, 0, END)
        xn = r0.take(TT, D)
        junk = r0.take(D)
        ra = Region(arena, 0, END)
        qT, kT, cum = ra.take(2, T), ra.take(2, T), ra.take(2, T)
        arg = [ra.take(2, T) for _ in range(2)]
        decay = ra.take(2, T)
        qE = [ra.take(2, T) for _ in range(2)]
        kE = [ra.take(2, T) for _ in range(2)]
        va = ra.take(TT, T)
        S = ra.take(2, TT, 2, P)
        sga = ra.take(4, T)
        qcz = [ra.take(2, T) for _ in range(2)]
        state = ra.take(3, 2, P)
        rsA = [ra.take(T) for _ in range(2)]
        hA = ra.take(T)
        ra2 = Region(oT[1][:].rearrange("p a b -> p (a b)"), 0, 2048)
        ecum, kdr = ra2.take(2, T), ra2.take(TT, 2, P)
        ra3 = Region(oT[2][:].rearrange("p a b -> p (a b)"), 0, 2048)
        level_mask = ra3.take(8, P, dt=I32)
        resets = ra3.take(T)
        sqA = ra3.take(T)
        w_a2 = sb("w_a2", [16, 256])
        rc = Region(arena, 0, END)
        raw = rc.take(4, 516)
        qkc = rc.take(4, T)
        vc, soc = rc.take(TT, T), rc.take(4, T)
        floor_, hC, sqC, rsC = rc.take(T), rc.take(T), rc.take(T), rc.take(T)
        argC = [rc.take(T) for _ in range(2)]
        W = [rc.take(T) for _ in range(2)]
        SW = rc.take(TT, T)
        sel4 = rc.take(4, P, parts=4)
        g4 = [rc.take(T, parts=4) for _ in range(8)]
        ones4 = rc.take(T, parts=4)
        ucol = rc.take(TT, 4)
        hD = rc.take(T)
        rb = Region(arena, 0, END)
        cn, kidxT, qlT, qiT = rb.take(3, T), rb.take(T), rb.take(8, T), rb.take(2, T)
        Dm, ckr, w_uv = rb.take(TT, T), rb.take(TT, P), rb.take(T)
        distv = rb.take(896)
        rb1 = Region(arena, rb.at, END)
        craw, sqB, rsB, qTb = rb1.take(3, T), rb1.take(3, T), rb1.take(2, T), rb1.take(4, T)
        w_uq, w_uk, w_qi, ukT = rb1.take(2, T), rb1.take(T), rb1.take(2, 256), rb1.take(4, P)
        rl = [rb1.take(T) for _ in range(2)]
        I_s = rb1.take(T)
        wki4 = rb1.take(8, 4, 32)
        selm = qTb[:, 0, :].bitcast(I32)
        wi0 = sb("wi0", [8, T])
        top8 = sb("top8", [P, 8])
        rb2 = Region(arena, rb.at, END)
        Pn, PT, olT = rb2.take(8, T), rb2.take(TT, T), rb2.take(8, T)
        L = [rb2.take(T) for _ in range(2)]
        nmax = sb("nmax", [P, 4])
        modB = arena[:, 18432:22528].rearrange("p (a b) -> p a b", a=4)
        mT = arena[:, 14336:18432].rearrange("p (a b) -> p a b", a=8)
        rm = Region(arena, 0, 14336)
        adab = rm.take(4096, parts=1)
        nffn = rm.take(D)
        csrep2 = rm.take(8, P)
        sgate = [rm.take(T) for _ in range(2)]
        mtmp = [rm.take(T) for _ in range(2)]
        wtmp = rm.take(T)
        h2 = rm.take(TT, D)
        sqx = rm.take(D)
        re = Region(arena, 0, 14336)
        wgu = [re.take(2, 8, FF) for _ in range(2)]
        wdn = [re.take(2, D) for _ in range(2)]
        nfin = re.take(D)
        rx = Region(arena, 14336, 18432)
        xg = [rx.take(D) for _ in range(2)]
        ys = [rx.take(D) for _ in range(2)]
        hTe = [oT[0][:].rearrange("p a b -> p (a b)")[:, 1024 * b:1024 * b + 1024].rearrange("p (j t) -> p j t", j=8)
               for b in range(2)]
        ro = Region(oT[1][:].rearrange("p a b -> p (a b)"), 0, 2048)
        sge = [ro.take(2, P) for _ in range(2)]
        acte = [ro.take(2, P) for _ in range(2)]
        rr = Region(oT[2][:].rearrange("p a b -> p (a b)"), 0, 2048)
        score, selr, mall = rr.take(TT, E), rr.take(TT, E), rr.take(TT, E)
        onehot = rr.take(6, E)
        rt_tmp, rt_tmp2 = rr.take(E), rr.take(E)
        base, ntile, uend = rr.take(E), rr.take(E), rr.take(E)
        slotA = rr.take(E)
        rbias = sb("rbias", [P, E])
        gtop = sb("gtop", [P, 8, 8])
        gsc, gm8, gmask = sb("gsc", [P, 8]), sb("gm8", [P, 8]), sb("gmask", [P, 8])
        gidx, eidx = sb("gidx", [P, 8], U32), sb("eidx", [P, 8], U32)
        gidf, eidf = sb("gidf", [P, 8]), sb("eidf", [P, 8])
        wk = sb("wk", [P, TT, 8])
        wsum = sb("wsum", [P, 1])
        slotf, sloti = sb("slotf", [P, TT, 8]), sb("sloti", [P, TT, 8], I32)
        tokid = sb("tokid", [P, TT, TOPK, 2], I32)
        oob = sb("oob", [P, 2 * (UNITS + 4)], I32)
        ucolf = sb("ucolf", [E, 1])
        ucmp = sb("ucmp", [E, 96])
        uexp = sb("uexp", [1, 96], I32)
        npair = sb("npair", [1, 1], I32)
        npf = sb("npf", [1, 64])
        npg = sb("npg", [1, 1])
        iota_u = sb("iota_u", [E, 96])
        tok_of = [sb(f"tok_of{b}", [P, 2], I32) for b in range(2)]
        row_of = [sb(f"row_of{b}", [P, 2], I32) for b in range(2)]
        eall = sb("eall", [P, TT, 8])
        sgS = [oT[1][:, 2 + m, :] for m in range(2)]
        rs = Region(arena, 16384, 18432)
        actS, wtmp2 = rs.take(2, T), rs.take(T)
        yk = [arena[:, 6144 * b:6144 * b + 6144].rearrange("p (k n) -> p k n", k=TOPK) for b in range(2)]
        routed = hT[:, 0:2, :].rearrange("p a b -> p (a b)")

        h_dram = nc.dram_tensor("h_dram", [T, D], F32).ap()
        y_dram = nc.dram_tensor("y_dram", [T * TOPK, D], F32).ap()
        list_dram = nc.dram_tensor("list_dram", [(UNITS + 4) * P, 2], I32).ap()

        w_in = a["w_in"][0].rearrange("(j p) n -> p j n", p=P)
        ada = a["ada_w"][0].rearrange("(p j) n -> p j n", j=8)
        loads = []

        def slot_view(n, off, *shape):
            v = ring[:, n % RING, off:off + int(np.prod(shape))]
            return v.rearrange("p (a b) -> p a b", a=shape[0])

        def load(name, parts, last):
            n = len(loads)
            loads.append((name, [(slot_view(n, off, *shape), src) for off, shape, src in parts], last))

        def cols(name, off=0, n=512):
            c = COL[name] + off
            return w_in[:, :, c:c + n]

        for c in range(4):
            load(f"ada{c}", [(0, (8, 512), ada[:, :, 512 * c:512 * c + 512])], f"mc{c}")
        load("w_qk", [(0, (8, 512), cols("qa"))], "ka1")
        load("w_va", [(0, (8, 512), cols("va"))], "va3")
        load("w_ga", [(0, (8, 512), cols("ga"))], "ga3")
        load("w_qkc", [(0, (8, 512), cols("qc"))], "qk3")
        load("w_vc", [(0, (8, 512), cols("vc"))], "vc3")
        load("w_oc", [(0, (8, 512), cols("oc"))], "oc3")
        load("w_cl", [(0, (8, 384), cols("cq", 0, 384))], "cl2")
        for c in range(8):
            load(f"adr{c}", [(0, (8, 512), ada[:, :, 2048 + 512 * c:2560 + 512 * c])], f"mb{c}")
        ups = [a[n][0].rearrange("(j p) n -> p j n", p=P) for n in ("w_up_a", "w_up_b", "w_up_c")]
        for m in range(0, 8, 2):
            for b in range(3):
                load(f"wm{m}{b}", [(0, (8, 256), cols("gates", D * b + P * m, 256)),
                                   (2048, (4, 256), ups[b][:, :, P * m:P * m + 256])], f"up{m + 1}{b}")
        wo_d = a["w_o"][0].rearrange("(j p) n -> p j n", p=P)
        for n in range(2):
            load(f"wo{n}", [(0, (8, 512), wo_d[:, :, 512 * n:512 * n + 512])], f"wo3{n}")
        load("w_sh", [(0, (8, 256), a["sh_w_gate"][0].rearrange("(p j) f -> p j f", j=8)),
                      (2048, (8, 256), a["sh_w_up"][0].rearrange("(p j) f -> p j f", j=8))], "su1")
        load("w_shd", [(0, (2, D), a["sh_w_down"][0].rearrange("(p m) n -> p m n", m=2)),
                       (2048, (8, E), a["router_w"][0].rearrange("(p j) e -> p j e", j=8))], "sd31")
        load_at = {name: n for n, (name, _, _) in enumerate(loads)}
        landed = {}
        count = [0] * RING
        for n, (name, parts, _) in enumerate(loads):
            count[n % RING] += 16 * len(parts)
            landed[name] = (n % RING, count[n % RING])

        def loaded(eng, name):
            s, v = landed[name]
            eng.wait_ge(sem(f"ring_loaded{s}"), v)

        def ring_view(name, off, *shape):
            return slot_view(load_at[name], off, *shape)

        def done(eng, name):
            n = number[name]
            eng.wait_ge(sem("products_done"), n + 1)
            return bank[n % BANKS]

        wsm = r0.take(8, P)
        wki = sb("wki", [P, 8, 32])
        GAPS = {"a_lr": 0, "w_idx": 32, "ic": 64, "fc": 96}

        for n in ("consts", "consts_loaded", "products_done", "dve_chain", "act_chain", "pool_chain",
                  *[f"ring_loaded{i}" for i in range(RING)], *sorted({s for _, s, _ in products})):
            sem(n)

        block = ctx.enter_context(nc.Block())
        NCONST = [0]

        @block.sync
        def _(sp):
            def const(dst, src):
                sp.dma_start(dst, src).then_inc(sem("consts_loaded"), 16)
                NCONST[0] += 16

            for b in range(2):
                for name in ("up_done", "y_done", "trans_done", "sge_ready", "acte_ready", "y_a", "y_v"):
                    sp.sem_inc(sem(f"{name}{b}"), 1)

            def rows(v, n):
                return v.rearrange("(r p) -> r p", p=P)[0:n]

            const(c_in[:, :], a["c"].rearrange("o (p j) -> (o p) j", j=8))
            sp.dma_start(x[:, :, :], a["x"][0].rearrange("(i p) d -> p i d", p=P)).then_inc(sem("x_loaded"), 16)
            const(prow[0:8, :], rows(a["norm_mix"][0], 8))
            const(prow[8:24, :], rows(a["ada_b"][0], 16))
            const(prow[24:26, :], rows(a["gla_b_a"][0], 2))
            const(prow[26:30, :], rows(a["gla_norm"][0], 4))
            const(prow[30:32, :], rows(a["dsa_norm_q"][0], 2))
            const(prow[32:33, :], rows(a["dsa_norm_kv"][0], 1))
            const(prow[33:37, :], rows(a["mlstm_norm"][0], 4))
            const(prow[37:53, :], a["mlstm_conv"][0].rearrange("k (r p) -> (k r) p", p=P))
            const(w_a2[:, :], a["gla_w_a2"][0])
            with nc.allow_non_contiguous_dma(reason="eight numbers"):
                const(bif[:, 0:1], a["mlstm_b_i"].rearrange("o h -> h o"))
                const(bif[:, 1:2], a["mlstm_b_f"].rearrange("o h -> h o"))
            sp.wait_ge(sem("small_cleared"), 1)
            for name, g in GAPS.items():
                const(wsm[:, :, g:g + IN_SIZES[name]], w_in[:, :, COL[name]:COL[name] + IN_SIZES[name]])
            const(wki[:, :, :], w_in[:, :, COL["k_idx"]:COL["k_idx"] + 32])
            const(rbias[:, :], a["router_bias"].to_broadcast([P, E]))

            def ring_load(n):
                name, parts, last = loads[n]
                if n >= RING:
                    sp.wait_ge(sem("products_done"), number[loads[n - RING][2]] + 1)
                for dst, src in parts:
                    sp.dma_start(dst, src).then_inc(sem(f"ring_loaded{n % RING}"), 16)

            n = 0
            while n < len(loads):
                name = loads[n][0]
                if name == "w_cl":
                    sp.wait_ge(sem("oTC_ready"), 4)
                    sp.dma_start(w_uq, a["dsa_w_uq"][0].rearrange("(k p) h d -> p k (h d)", p=P)).then_inc(sem("extra_loaded"), 16)
                    sp.dma_start(w_uk, a["dsa_w_uk"][0].rearrange("c h d -> c (h d)")).then_inc(sem("extra_loaded"), 16)
                    sp.dma_start(w_uv, a["dsa_w_uv"][0].rearrange("c h d -> c (h d)")).then_inc(sem("extra_loaded"), 16)
                    sp.dma_start(w_qi, a["dsa_w_qi"][0].rearrange("(k p) h d -> p k (h d)", p=P)).then_inc(sem("extra_loaded"), 16)
                if name == "adr0":
                    sp.wait_ge(sem("oTB_ready"), 4)
                    sp.dma_start(adab, a["ada_b"][0:1, 2048:6144]).then_inc(sem("extra_loaded"), 16)
                    sp.dma_start(nffn, a["norm_ffn"].to_broadcast([P, D])).then_inc(sem("extra_loaded"), 16)
                ring_load(n)
                n += 1

            for i in range(TT):
                sp.wait_ge(sem("h2_ready"), i + 1)
                sp.dma_start(h_dram[P * i:P * i + P, :], h2[:, i, :]).then_inc(sem("h_stored"), 16)
            sp.wait_ge(sem("consts"), 1)
            sp.dma_start(list_dram.rearrange("(p u) o -> p (u o)", p=P), oob[:, :]).then_inc(sem("list_cleared"), 16)
            sp.wait_ge(sem("h_stored"), 16 * TT)
            sp.wait_ge(sem("h2T_ready"), 8)
            sp.dma_start(nfin, a["norm_final"].rearrange("(o d) -> o d", o=1).to_broadcast([P, D])).then_inc(sem("extra_loaded"), 16)

            sp.wait_ge(sem("table_ready"), 1)
            pairs = sp.value_load(npair[0:1, 0:1], min_val=1, max_val=UNITS // 2)
            sp.wait_ge(sem("list_stored"), 16 * TT * TOPK)

            def unit_list(u, b):
                sp.dma_start(tok_of[b][:, :], list_dram[bass.ds(u * P, P), :]).then_inc(sem(f"list_loaded{b}"), 16)

            with sp.Fori(0, pairs) as i:
                for b in range(2):
                    u = 2 * i + b
                    e = sp.value_load(uexp[0:1, bass.ds(u, 1)], min_val=0, max_val=E - 1)
                    sp.wait_ge(sem(f"trans_done{b}"), 2 * i + 1)
                    unit_list(u, b)
                    sp.wait_ge(sem(f"up_done{b}"), i + 1)
                    for k, w in enumerate(("exp_w_gate", "exp_w_up")):
                        src = a[w][0][bass.ds(e, 1)].rearrange("e (p j) f -> (e p) j f", j=8)
                        sp.dma_start(wgu[b][:, k, :, :], src).then_inc(sem(f"wgu_loaded{b}"), 16)
                    sp.wait_ge(sem(f"y_done{b}"), 2 * i + 1)
                    src = a["exp_w_down"][0][bass.ds(e, 1)].rearrange("e (p m) n -> (e p) m n", m=2)
                    sp.dma_start(wdn[b][:, :, :], src).then_inc(sem(f"wdn_loaded{b}"), 16)
                    sp.wait_ge(sem(f"y_stored{b}"), 16 * i + 16)
                    sp.dma_start(row_of[b][:, :], list_dram[bass.ds(u * P, P), :]).then_inc(sem(f"rows_loaded{b}"), 16)
            sp.wait_ge(sem("trans_done0"), 2 * pairs + 1)
            unit_list(2 * pairs, 0)

            for b in range(2):
                sp.wait_ge(sem(f"y_stored{b}"), 16 * pairs + 16)
                sp.wait_ge(sem(f"y_done{b}"), 2 * pairs + 1)
            for i in range(TT):
                if i >= 2:
                    sp.wait_ge(sem("yk_used"), TOPK * (i - 1))
                sp.dma_start(yk[i % 2], y_dram[P * TOPK * i:P * TOPK * (i + 1), :].rearrange("(t k) n -> t k n", k=TOPK)
                             ).then_inc(sem(f"yk_loaded{i % 2}"), 16)
            for i in range(TT):
                sp.wait_ge(sem("out_ready"), i + 1)
                sp.dma_start(out[0, P * i:P * i + P, :], x[:, i, :]).then_inc(sem("out_stored"), 16)
            sp.wait_ge(sem("out_stored"), 16 * TT)

        @block.gpsimd
        def _(pool):
            g = nc.gpsimd
            chain = [0]

            def link(ins):
                chain[0] += 1
                ins.then_inc(sem("pool_chain"), 1)
                pool.wait_ge(sem("pool_chain"), chain[0])

            g.memset(wsm, 0.0).then_inc(sem("small_cleared"), 1)
            g.memset(epsc[:], EPS)
            link(g.memset(ident[:], 0.0))
            link(g.affine_select(out=ident[:], in_=ident[:], compare_op=ALU.not_equal, fill=1.0, base=0,
                                 pattern=[[-1, P]], channel_multiplier=1))
            link(g.memset(ones[:], 1.0))
            link(g.affine_select(out=causal[:], in_=ones[:], compare_op=ALU.is_ge, fill=0.0, base=0,
                                 pattern=[[1, P]], channel_multiplier=-1))
            link(g.affine_select(out=before[:], in_=ones[:], compare_op=ALU.is_gt, fill=0.0, base=0,
                                 pattern=[[1, P]], channel_multiplier=-1))
            link(g.memset(future[:], 1))
            link(g.affine_select(out=future[:], in_=future[:], compare_op=ALU.is_gt, fill=0.0, base=0,
                                 pattern=[[1, P]], channel_multiplier=-1))
            g.memset(negc[:], NEG_FUTURE)
            g.iota(iota_e[:], pattern=[[1, E]], base=0, channel_multiplier=0, allow_small_or_imprecise_dtypes=True)
            g.iota(iota_u[:], pattern=[[1, 96]], base=0, channel_multiplier=0, allow_small_or_imprecise_dtypes=True)
            g.iota(tokid[:, :, :, 0], pattern=[[P, TT], [0, TOPK]], base=0, channel_multiplier=1)
            g.iota(tokid[:, :, :, 1], pattern=[[P * TOPK, TT], [1, TOPK]], base=0, channel_multiplier=TOPK)
            g.memset(oob[:], T * TOPK)
            link(g.iota(level_mask[:, 0, :], pattern=[[1, P]], base=0, channel_multiplier=0))
            link(g.iota(level_mask[:, 1, :], pattern=[[0, P]], base=0, channel_multiplier=1))
            link(g.memset(resets, 1.0))
            link(g.memset(resets.rearrange("p (i t) -> p i t", i=TT)[:, :, 0:1], 0.0))
            g.memset(stat[:], 0.0).then_inc(sem("consts"), 1)

            pool.wait_ge(sem("hT_ready"), 8)
            pool.wait_ge(sem("small_ready"), 1)
            for t in (qE[0], qE[1], kE[0], kE[1], qcz[0], qcz[1], S):
                ins = g.memset(t, 0.0)
            ins.then_inc(sem("cleared"), 1)

            pool.wait_ge(sem("oTA_ready"), 4)
            g.memset(raw, 0.0)
            g.memset(ones4, 1.0)
            link(g.memset(sel4, 0.0))
            g.affine_select(out=sel4, in_=sel4, compare_op=ALU.not_equal, fill=1.0, base=0,
                            pattern=[[-1, 4], [0, P]], channel_multiplier=1).then_inc(sem("cleared"), 1)

            pool.wait_ge(sem("oTC_ready"), 4)
            g.iota(distv, pattern=[[1, 896]], base=-384, channel_multiplier=-1,
                   allow_small_or_imprecise_dtypes=True)
            g.memset(Dm, NEG_MASK).then_inc(sem("cleared"), 1)

            pool.wait_ge(sem("list_cleared"), 16)
            pool.wait_ge(sem("slots_ready"), TT)
            for i in range(TT):
                for k in range(TOPK):
                    g.indirect_dma_start(out=list_dram[:, :], out_offset=bass.IndirectOffsetOnAxis(ap=sloti[:, i, k:k + 1], axis=0),
                                         in_=tokid[:, i, k, :], in_offset=None).then_inc(sem("list_stored"), 16)
            pool.wait_ge(sem("x2_ready"), 4)
            pool.wait_ge(sem("products_done"), number["wo31"] + 1)
            for b in range(2):
                g.memset(row_of[b][:, :], T * TOPK)
                ins = g.memset(xg[b], 0.0)
            link(ins)
            pool.wait_ge(sem("h_stored"), 16 * TT)
            pool.wait_ge(sem("table_ready"), 1)
            pairs = pool.value_load(npair[0:1, 0:1], min_val=1, max_val=UNITS // 2)

            def gather(b):
                pool.sem_inc(sem("gathers_begun"), 1)
                g.indirect_dma_start(out=xg[b], out_offset=None, in_=h_dram[:, :],
                                     in_offset=bass.IndirectOffsetOnAxis(ap=tok_of[b][:, 0:1], axis=0),
                                     bounds_check=T - 1, oob_is_err=False).then_inc(sem(f"xg_loaded{b}"), 16)

            for b in range(2):
                g.indirect_dma_start(out=y_dram[:, :], out_offset=bass.IndirectOffsetOnAxis(ap=row_of[b][:, 1:2], axis=0),
                                     in_=xg[b], in_offset=None, bounds_check=T * TOPK - 1, oob_is_err=False
                                     ).then_inc(sem(f"y_stored{b}"), 16)
            pool.wait_ge(sem("list_loaded0"), 16)
            gather(0)
            with pool.Fori(0, pairs) as i:
                for b in range(2):
                    c = 1 - b
                    pool.wait_ge(sem(f"list_loaded{c}"), 16 * i + 16 * (b + 1))
                    pool.wait_ge(sem(f"trans_done{c}"), 2 * i + 2 * b + 1)
                    gather(c)
                    pool.wait_ge(sem(f"rows_loaded{b}"), 16 * i + 16)
                    pool.wait_ge(sem(f"y_a{b}"), i + 2)
                    pool.wait_ge(sem(f"y_v{b}"), i + 2)
                    pool.sem_inc(sem("gathers_begun"), 1)
                    g.indirect_dma_start(out=y_dram[:, :], out_offset=bass.IndirectOffsetOnAxis(ap=row_of[b][:, 1:2], axis=0),
                                         in_=ys[b], in_offset=None, bounds_check=T * TOPK - 1, oob_is_err=False
                                         ).then_inc(sem(f"y_stored{b}"), 16)

        @block.tensor
        def _(pe):
            mm = nc.tensor.matmul
            nxt = [0]

            def begin(name):
                n = nxt[0]
                assert products[n][0] == name, (products[n][0], name)
                nxt[0] += 1
                if n >= BANKS:
                    _, s, v = products[n - BANKS]
                    pe.wait_ge(sem(s), v)
                return bank[n % BANKS]

            def end(ins):
                ins.then_inc(sem("products_done"), 1)

            pe.wait_ge(sem("consts"), 1)
            pe.wait_ge(sem("consts_loaded"), NCONST[0])
            b = begin("params")
            end(nc.tensor.transpose(b[:, 0:53], prow[0:53, :], ident[0:53, 0:53]))
            pe.wait_ge(sem("cs_ready"), 1)
            for c in range(4):
                b = begin(f"mc{c}")
                loaded(pe, f"ada{c}")
                w = ring_view(f"ada{c}", 0, 8, 512)
                for m in range(4):
                    for j in range(8):
                        ins = mm(b[:, m:m + 1], w[:, j, tile_cols(m)], cs[:, j:j + 1],
                                 start=(j == 0), stop=(j == 7))
                end(ins)
            for j in range(8):
                pe.wait_ge(sem("xn_ready"), TT)
                b = begin(f"xT{j}")
                for i in range(TT):
                    ins = nc.tensor.transpose(b[:, tile_cols(i)], xn[:, i, tile_cols(j)], ident[:, :])
                end(ins)

            def project(name, w, m):
                b = begin(name)
                for j in range(8):
                    pe.wait_ge(sem("hT_ready"), j + 1)
                    ins = mm(b[:, :], w[:, j, tile_cols(m)], hT[:, j, :], start=(j == 0), stop=(j == 7))
                end(ins)

            def project_rows(name, w, i):
                b = begin(name)
                for j in range(8):
                    ins = mm(b[:, :], hT[:, j, tile_cols(i)], w[:, j, :], start=(j == 0), stop=(j == 7))
                end(ins)

            project("small", wsm, 0)
            pe.wait_ge(sem("small_ready"), 1)
            for f in range(2):
                b = begin(f"la{f}")
                end(mm(b[:, :], w_a2[:, tile_cols(f)], small[0:16, :], start=True, stop=True))
            loaded(pe, "w_qk")
            w = ring_view("w_qk", 0, 8, 512)
            for f in range(2):
                project(f"qa{f}", w, f)
            for f in range(2):
                project(f"ka{f}", w, 2 + f)
            loaded(pe, "w_va")
            w = ring_view("w_va", 0, 8, 512)
            for i in range(TT):
                project_rows(f"va{i}", w, i)
            pe.wait_ge(sem("kd_ready"), 1)
            kd = decay
            for f in range(2):
                b = begin(f"kd{f}")
                for i in range(TT):
                    ins = nc.tensor.transpose(b[:, tile_cols(i)], kd[:, f, tile_cols(i)], ident[:, :])
                end(ins)
            pe.wait_ge(sem("kdr_ready"), 2)
            pe.wait_ge(sem("v_ready"), 4)
            for i in range(3):
                for f in range(2):
                    b = begin(f"st{i}{f}")
                    end(mm(b[:, 0:256], kdr[:, i, f, :], va[:, i, 256 * f:256 * f + 256], start=True, stop=True))
            for l in range(8):
                if l < 7:
                    pe.wait_ge(sem("level_ready"), l + 1)
                    ksrc, qsrc = kE[l % 2], qE[l % 2]
                else:
                    ksrc, qsrc = kT, qT
                for g in range(4):
                    p0, tp = 64 * (g // 2), g % 2
                    b = begin(f"scA{l}{g}")
                    for ii in range(2):
                        for f in range(2):
                            t = tile_cols(2 * tp + ii)
                            ins = mm(b[:, tile_cols(2 * ii + f)], ksrc[p0:p0 + 64, f, t], qsrc[p0:p0 + 64, f, t],
                                     start=True, stop=True)
                    end(ins)
            loaded(pe, "w_ga")
            w = ring_view("w_ga", 0, 8, 512)
            for m in range(4):
                project(f"ga{m}", w, m)
            pe.wait_ge(sem("state_ready"), 6)
            pe.wait_ge(sem("intra_done"), 32)
            for h in range(5):
                if h < 4:
                    b = begin(f"oA{h}")
                    for i in range(TT):
                        if i:
                            mm(b[:, tile_cols(i)], state[:, i - 1, h // 2, :], qcz[h % 2][:, h // 2, tile_cols(i)],
                               start=True, stop=False)
                        ins = mm(b[:, tile_cols(i)], va[:, i, tile_cols(h)], S[:, h % 2, i, h // 2, :],
                                 start=(i == 0), stop=True)
                    end(ins)
                if h:
                    pe.wait_ge(sem("squares_ready"), h)
                    b = begin(f"msA{h - 1}")
                    end(mm(b[:, :], ones[:, :], sqA, start=True, stop=True))

            loaded(pe, "w_qkc")
            w = ring_view("w_qkc", 0, 8, 512)
            for f in range(4):
                project(f"qk{f}", w, f)
            pe.wait_ge(sem("scans_ready"), 1)
            b = begin("uT")
            for i in range(TT):
                ins = nc.tensor.transpose(b[:, 4 * i:4 * i + 4], g4[3][:, tile_cols(i)], ident[0:4, 0:4])
            end(ins)
            loaded(pe, "w_vc")
            w = ring_view("w_vc", 0, 8, 512)
            for i in range(TT):
                project_rows(f"vc{i}", w, i)
            loaded(pe, "w_oc")
            w = ring_view("w_oc", 0, 8, 512)
            for m in range(4):
                project(f"oc{m}", w, m)
            pe.wait_ge(sem("cleared"), 2)
            pe.wait_ge(sem("qkc_ready"), 4)
            pe.wait_ge(sem("v_ready"), 8)
            for h in range(4):
                p0, f = 64 * (h % 2), h // 2
                b = begin(f"bm{h}")
                end(mm(b[:, :], sel4[:, h, :], g4[4], start=True, stop=True))
                b = begin(f"bt{h}")
                end(mm(b[:, :], sel4[:, h, :], g4[5], start=True, stop=True))
                for j in range(TT):
                    b = begin(f"scC{h}{j}")
                    end(mm(b[:, P * j:T], qkc[p0:p0 + 64, 2 + f, tile_cols(j)], qkc[p0:p0 + 64, f, P * j:T],
                           start=True, stop=True))
                b = begin(f"num{h}")
                for j in range(TT):
                    pe.wait_ge(sem("SW_ready"), 4 * h + j + 1)
                    ins = mm(b[:, P * j:T], vc[:, j, tile_cols(h)], SW[:, j, P * j:T], start=(j == 0), stop=(j == 3))
                end(ins)
                b = begin(f"den{h}")
                for j in range(TT):
                    ins = mm(b[:, P * j:T], ones[:, :], SW[:, j, P * j:T], start=(j == 0), stop=(j == 3))
                end(ins)
                pe.wait_ge(sem("squares_ready"), h + 5)
                b = begin(f"msC{h}")
                end(mm(b[:, :], ones[:, :], sqC, start=True, stop=True))

            pe.wait_ge(sem("wki4_ready"), 1)
            b = begin("kidx")
            for j in range(8):
                ins = mm(b[:, :], wki4[:, j, :, :].rearrange("p g d -> p (g d)"), hT[:, j, :],
                         start=(j == 0), stop=(j == 7))
            end(ins)
            loaded(pe, "w_cl")
            w = ring_view("w_cl", 0, 8, 384)
            for n in range(3):
                project(f"cl{n}", w, n)
            pe.wait_ge(sem("squares_ready"), 11)
            b = begin("msq")
            for k in range(2):
                ins = mm(b[:, :], ones[:, :], sqB[:, k, :], start=(k == 0), stop=(k == 1))
            end(ins)
            b = begin("mskv")
            end(mm(b[:, :], ones[:, :], sqB[:, 2, :], start=True, stop=True))
            pe.wait_ge(sem("wi0_ready"), 1)
            b = begin("wi")
            for i in range(TT):
                ins = nc.tensor.transpose(b[:, 8 * i:8 * i + 8], wi0[:, tile_cols(i)], ident[0:8, 0:8])
            end(ins)
            pe.wait_ge(sem("extra_loaded"), 64)
            b = begin("uk")
            for m in range(4):
                ins = nc.tensor.transpose(b[:, tile_cols(m)], w_uk[:, tile_cols(m)], ident[:, :])
            end(ins)
            pe.wait_ge(sem("cn_ready"), 2)
            b = begin("ckr")
            for i in range(TT):
                ins = nc.tensor.transpose(b[:, tile_cols(i)], cn[:, 2, tile_cols(i)], ident[:, :])
            end(ins)
            for m in range(2):
                b = begin(f"qi{m}")
                for k in range(2):
                    ins = mm(b[:, :], w_qi[:, k, tile_cols(m)], cn[:, k, :], start=(k == 0), stop=(k == 1))
                end(ins)
            pe.wait_ge(sem("qi_ready"), 2)
            pe.wait_ge(sem("kidx_ready"), 1)
            for i in range(1, TT):
                for h in range(8):
                    p0 = 32 * (h % 4)
                    b = begin(f"ix{i}{h}")
                    end(mm(b[:, 0:P * (i + 1)], qiT[p0:p0 + 32, h // 4, tile_cols(i)],
                           kidxT[p0:p0 + 32, 0:P * (i + 1)], start=True, stop=True))
            for m in range(4):
                b = begin(f"q{m}")
                for k in range(2):
                    ins = mm(b[:, :], w_uq[:, k, tile_cols(m)], cn[:, k, :], start=(k == 0), stop=(k == 1))
                end(ins)
            pe.wait_ge(sem("ukT_ready"), 1)
            for h in range(8):
                p0 = 64 * (h % 2)
                pe.wait_ge(sem("q_ready"), h // 2 + 1)
                b = begin(f"ql{h}")
                end(mm(b[:, :], ukT[p0:p0 + 64, h // 2, :], qTb[p0:p0 + 64, h // 2, :], start=True, stop=True))
            npt = 0
            for i in range(TT):
                for h in range(8):
                    pe.wait_ge(sem("ql_ready"), h + 1)
                    b = begin(f"lg{i}{h}")
                    end(mm(b[:, 0:P * (i + 1)], qlT[:, h, tile_cols(i)], cn[:, 2, 0:P * (i + 1)],
                           start=True, stop=True))
                for g in range(2):
                    pe.wait_ge(sem("P_ready"), 8 * i + 4 * g + 4)
                    for j in range(i + 1):
                        b = begin(f"pt{i}{g}{j}")
                        for h in range(4):
                            ins = nc.tensor.transpose(b[:, tile_cols(h)], Pn[:, 4 * g + h, tile_cols(j)], ident[:, :])
                        end(ins)
                    b = begin(f"ol{i}{g}")
                    for j in range(i + 1):
                        npt += 1
                        pe.wait_ge(sem("PT_ready"), npt)
                        ins = mm(b[:, :], ckr[:, j, :], PT[:, j, :], start=(j == 0), stop=(j == i))
                    end(ins)
            pe.wait_ge(sem("ol_ready"), 8)
            for m in range(4):
                b = begin(f"ob{m}")
                for q in range(2):
                    h = 2 * m + q
                    ins = mm(b[64 * q:64 * q + 64, :], w_uv[:, 64 * h:64 * h + 64], olT[:, h, :], start=True, stop=True)
                end(ins)

            pe.wait_ge(sem("csrep_ready"), 1)
            pe.wait_ge(sem("extra_loaded"), 96)
            for c in range(8):
                loaded(pe, f"adr{c}")
                w = ring_view(f"adr{c}", 0, 8, 512)
                b = begin(f"mb{c}")
                for j in range(8):
                    mm(b[:, :], csrep2[:, j, :], w[:, j, :], start=(j == 0), stop=False)
                end(mm(b[:, :], ones[0:1, :], adab[:, 512 * c:512 * c + 512], start=False, stop=True))
            for m in range(8):
                for br in range(3):
                    name = f"wm{m - m % 2}{br}"
                    loaded(pe, name)
                    wg, wu = ring_view(name, 0, 8, 256), ring_view(name, 2048, 4, 256)
                    project(f"gate{m}{br}", wg, m % 2)
                    b = begin(f"up{m}{br}")
                    for j in range(4):
                        ins = mm(b[:, :], wu[:, j, tile_cols(m % 2)], oT[br][:, j, :], start=(j == 0), stop=(j == 3))
                    end(ins)
            loaded(pe, "wo0")
            loaded(pe, "wo1")
            pe.wait_ge(sem("mT_ready"), 8)
            for i in range(TT):
                for n in range(2):
                    w = ring_view(f"wo{n}", 0, 8, 512)
                    b = begin(f"wo{i}{n}")
                    for j in range(8):
                        ins = mm(b[:, :], mT[:, j, tile_cols(i)], w[:, j, :], start=(j == 0), stop=(j == 7))
                    end(ins)

            pe.wait_ge(sem("h2_ready"), TT)
            for j in range(8):
                b = begin(f"hT2{j}")
                for i in range(TT):
                    src = h2[:, i, :].rearrange("t (p j) -> t j p", j=8)[:, j, :]
                    ins = nc.tensor.transpose(b[:, tile_cols(i)], src, ident[:, :])
                end(ins)
            loaded(pe, "w_shd")
            rw = ring_view("w_shd", 2048, 8, E)
            pe.wait_ge(sem("h2T_ready"), 8)
            for i in range(TT):
                b = begin(f"rt{i}")
                for j in range(8):
                    ins = mm(b[:, 0:E], hT[:, j, tile_cols(i)], rw[:, j, :], start=(j == 0), stop=(j == 7))
                end(ins)
            for i in range(TT):
                pe.wait_ge(sem("mall_ready"), TT)
                b = begin(f"pos{i}")
                for q in range(i + 1):
                    ins = mm(b[:, 0:E], before[:, :] if q == i else ones[:, :], mall[:, q, :],
                             start=(q == 0), stop=(q == i))
                end(ins)
            b = begin("tot")
            for q in range(TT):
                ins = mm(b[:, 0:E], ones[:, :], mall[:, q, :], start=(q == 0), stop=(q == TT - 1))
            end(ins)
            pe.wait_ge(sem("uend_ready"), 1)
            b = begin("ue")
            end(nc.tensor.transpose(b[0:E, 0:P], uend, ident[:, :]))
            pe.wait_ge(sem("ucmp_ready"), 1)
            b = begin("uc")
            end(mm(b[0:1, 0:96], ones[0:E, 0:1], ucmp[:, :], start=True, stop=True))
            loaded(pe, "w_sh")
            wg, wu = ring_view("w_sh", 0, 8, 256), ring_view("w_sh", 2048, 8, 256)
            for m in range(2):
                for name, w in ((f"sg{m}", wg), (f"su{m}", wu)):
                    b = begin(name)
                    for j in range(8):
                        ins = mm(b[:, :], w[:, j, :].rearrange("p (f m) -> p m f", m=2)[:, m, :], hT[:, j, :],
                                 start=(j == 0), stop=(j == 7))
                    end(ins)
            wd = ring_view("w_shd", 0, 2, D)
            pe.wait_ge(sem("actS_ready"), 2)
            for i in range(TT):
                for n in range(2):
                    b = begin(f"sd{i}{n}")
                    for m in range(2):
                        ins = mm(b[:, :], actS[:, m, tile_cols(i)], wd[:, m, 512 * n:512 * n + 512],
                                 start=(m == 0), stop=(m == 1))
                    end(ins)
            assert nxt[0] == len(products)

            for _, s, v in products[-BANKS:]:
                pe.wait_ge(sem(s), v)
            pe.wait_ge(sem("table_ready"), 1)
            pairs = pe.value_load(npair[0:1, 0:1], min_val=1, max_val=UNITS // 2)

            def transpose_rows(c):
                for half in range(2):
                    for q in range(4):
                        j = 4 * half + q
                        src = xg[c].rearrange("t (p j) -> t j p", j=8)[:, j, :]
                        ins = nc.tensor.transpose(bank[half][:, tile_cols(q)], src, ident[:, :])
                    ins.then_inc(sem(f"trans_done{c}"), 1)

            pe.wait_ge(sem("xg_loaded0"), 16)
            transpose_rows(0)
            with pe.Fori(0, pairs) as i:
                for b in range(2):
                    c = 1 - b
                    pe.wait_ge(sem(f"hTe_a{b}"), i + 1)
                    pe.wait_ge(sem(f"hTe_v{b}"), i + 1)
                    pe.wait_ge(sem(f"wgu_loaded{b}"), 32 * i + 32)
                    pe.wait_ge(sem(f"sge_ready{c}"), i + b + 1)
                    for m in range(2):
                        for j in range(8):
                            w = wgu[b][:, 0, j, :].rearrange("p (f m) -> p m f", m=2)[:, m, :]
                            ins = mm(bank[2][:, tile_cols(m)], w, hTe[b][:, j, :], start=(j == 0), stop=(j == 7))
                    ins.then_inc(sem(f"gate_done{b}"), 1)
                    pe.wait_ge(sem(f"acte_ready{c}"), i + b + 1)
                    for m in range(2):
                        for j in range(8):
                            w = wgu[b][:, 1, j, :].rearrange("p (f m) -> p m f", m=2)[:, m, :]
                            ins = mm(bank[3][:, tile_cols(m)], w, hTe[b][:, j, :], start=(j == 0), stop=(j == 7))
                    ins.then_inc(sem(f"up_done{b}"), 1)
                    pe.wait_ge(sem(f"xg_loaded{c}"), 16 * (i + b + 1))
                    transpose_rows(c)
                    pe.wait_ge(sem(f"acte_ready{b}"), i + 2)
                    pe.wait_ge(sem(f"wdn_loaded{b}"), 16 * i + 16)
                    pe.wait_ge(sem(f"y_a{b}"), i + 1)
                    pe.wait_ge(sem(f"y_v{b}"), i + 1)
                    for n in range(2):
                        for m in range(2):
                            ins = mm(bank[4 + 2 * b + n][:, :], acte[b][:, m, :], wdn[b][:, m, 512 * n:512 * n + 512],
                                     start=(m == 0), stop=(m == 1))
                        ins.then_inc(sem(f"y_done{b}"), 1)

        @block.scalar
        def _(act):
            A = nc.scalar.activation
            chain = [0]

            def link(ins):
                chain[0] += 1
                ins.then_inc(sem("act_chain"), 1)
                act.wait_ge(sem("act_chain"), chain[0])

            act.wait_ge(sem("consts"), 1)
            act.wait_ge(sem("consts_loaded"), NCONST[0])
            A(cs[:, :], c_in[:, :], ACT.Silu).then_inc(sem("cs_ready"), 1)
            act.wait_ge(sem("x_loaded"), 16)
            for i in range(TT):
                link(A(junk, x[:, i, :], ACT.Square, accum_out=stat[:, i:i + 1]))
            A(stat[:, 4:8], stat[:, 0:4], ACT.Sqrt, scale=1.0 / D, bias=epsc[:, 0:1]).then_inc(sem("rms_ready"), 1)
            act.wait_ge(sem("mod1_ready"), 1)
            for j in range(8):
                b = done(act, f"xT{j}")
                A(hT[:, j, :], b[:, :], ACT.Identity, scale=mod1[:, j:j + 1], bias=mod1[:, 8 + j:9 + j]
                  ).then_inc(sem("hT_ready"), 1)
            b = done(act, "small")
            A(small[:, :], b[:, :], ACT.Copy).then_inc(sem("small_ready"), 1)
            for f in range(2):
                act.wait_ge(sem("z_ready"), f + 1)
                link(A(decay[:, f, :], arg[0][:, f, :], ACT.Abs))
                link(A(decay[:, f, :], decay[:, f, :], ACT.Exp, scale=-1.0))
                A(decay[:, f, :], decay[:, f, :], ACT.Ln, bias=1.0).then_inc(sem("lnz_ready"), 1)
            for f in range(2):
                b = done(act, f"qa{f}")
                A(qT[:, f, :], b[:, :], ACT.Copy, scale=0.125).then_inc(sem("qa_ready"), 1)
            act.wait_ge(sem("cum_ready"), 1)
            A(ecum, cum, ACT.Exp).then_inc(sem("ecum_ready"), 1)
            act.wait_ge(sem("kdarg_ready"), 1)
            A(decay, arg[0], ACT.Exp).then_inc(sem("kdE_ready"), 1)
            for f in range(2):
                b = done(act, f"kd{f}")
                A(kdr[:, :, f, :], b[:, :].rearrange("p (i k) -> p i k", i=TT), ACT.Copy).then_inc(sem("kdr_ready"), 1)
            for l in range(7):
                act.wait_ge(sem("arg_ready"), l + 1)
                if l:
                    act.wait_ge(sem("level_ready"), l)
                else:
                    act.wait_ge(sem("products_done"), number["kd1"] + 1)
                A(decay, arg[l % 2], ACT.Exp).then_inc(sem("E_ready"), 1)
            for m in range(4):
                b = done(act, f"ga{m}")
                A(sga[:, m, :], b[:, :], ACT.Silu).then_inc(sem("outgate_ready"), 1)
            for h in range(5):
                if h < 4:
                    b = done(act, f"oA{h}")
                    if h:
                        b1 = done(act, f"msA{h - 1}")
                        if h == 3:
                            act.wait_ge(sem("oA_read"), 1)
                        A(rsA[(h - 1) % 2], b1[:, :], ACT.Sqrt, scale=1.0 / P,
                          bias=epsc[:, 0:1]).then_inc(sem("root_ready"), 1)
                    A(sqA, b[:, :], ACT.Square).then_inc(sem("squares_ready"), 1)
                else:
                    b = done(act, "msA3")
                    act.wait_ge(sem("oA_read"), 2)
                    A(rsA[1], b[:, :], ACT.Sqrt, scale=1.0 / P, bias=epsc[:, 0:1]).then_inc(sem("root_ready"), 1)

            act.wait_ge(sem("oTA_ready"), 4)
            act.wait_ge(sem("fb_ready"), 1)
            link(A(g4[1], g4[0], ACT.Abs))
            link(A(g4[1], g4[1], ACT.Exp, scale=-1.0))
            A(g4[1], g4[1], ACT.Ln, bias=1.0).then_inc(sem("lnf_ready"), 1)
            for f in range(4):
                act.wait_ge(sem("conv_ready"), f + 1)
                A(qkc[:, f, :], qkc[:, f, :], ACT.Silu).then_inc(sem("qkc_ready"), 1)
            for m in range(4):
                b = done(act, f"oc{m}")
                A(soc[:, m, :], b[:, :], ACT.Sigmoid).then_inc(sem("outgate_ready"), 1)
            for h in range(4):
                b = done(act, f"bt{h}")
                if h:
                    act.wait_ge(sem("den_read"), h)
                A(floor_, b[:, :], ACT.Exp, scale=-1.0).then_inc(sem("floor_ready"), 1)
                for j in range(TT):
                    n = 4 * h + j
                    act.wait_ge(sem("argC_ready"), n + 1)
                    if n >= 2:
                        act.wait_ge(sem("SW_ready"), n - 1)
                    A(W[n % 2][:, 0:T - P * j], argC[n % 2][:, 0:T - P * j], ACT.Exp, scale=-1.0).then_inc(sem("W_ready"), 1)
                act.wait_ge(sem("hC_ready"), h + 1)
                if h:
                    act.wait_ge(sem("products_done"), number[f"msC{h - 1}"] + 1)
                A(sqC, hC, ACT.Square).then_inc(sem("squares_ready"), 1)
                b = done(act, f"msC{h}")
                A(rsC, b[:, :], ACT.Sqrt, scale=1.0 / P, bias=epsc[:, 0:1]).then_inc(sem("root_ready"), 1)

            act.wait_ge(sem("oTC_ready"), 4)
            b = done(act, "kidx")
            A(kidxT, b[:, :], ACT.Copy).then_inc(sem("kidx_ready"), 1)
            for n in range(3):
                act.wait_ge(sem("craw_ready"), n + 1)
                A(sqB[:, n, :], craw[:, n, :], ACT.Square).then_inc(sem("squares_ready"), 1)
            for n, name in enumerate(("msq", "mskv")):
                b = done(act, name)
                A(rsB[:, n, :], b[:, :], ACT.Sqrt, scale=1.0 / (256, 128)[n], bias=epsc[:, 0:1]).then_inc(sem("root_ready"), 1)
            b = done(act, "ckr")
            A(ckr, b[:, :].rearrange("p (i k) -> p i k", i=TT), ACT.Copy).then_inc(sem("ckr_ready"), 1)
            for m in range(2):
                b = done(act, f"qi{m}")
                A(qiT[:, m, :], b[:, :], ACT.Copy, scale=float(32 ** -0.5)).then_inc(sem("qi_ready"), 1)
            for i in range(1, TT):
                for h in range(8):
                    n = 8 * (i - 1) + h
                    b = done(act, f"ix{i}{h}")
                    if n >= 2:
                        act.wait_ge(sem("relu_used"), n - 1)
                    A(rl[n % 2][:, 0:P * (i + 1)], b[:, 0:P * (i + 1)], ACT.Relu).then_inc(sem("relu_ready"), 1)
            for m in range(4):
                b = done(act, f"q{m}")
                if m == 0:
                    act.wait_ge(sem("D_ready"), 4)
                A(qTb[:, m, :], b[:, :], ACT.Copy).then_inc(sem("q_ready"), 1)
            for h in range(8):
                b = done(act, f"ql{h}")
                A(qlT[:, h, :], b[:, :], ACT.Copy, scale=0.125).then_inc(sem("ql_ready"), 1)
            npt = 0
            for i in range(TT):
                for h in range(8):
                    n = 8 * i + h
                    act.wait_ge(sem("nmax_ready"), n + 1)
                    if i:
                        act.wait_ge(sem("products_done"), number[f"pt{i - 1}{h // 4}{i - 1}"] + 1)
                    A(Pn[:, h, 0:P * (i + 1)], L[n % 2][:, 0:P * (i + 1)], ACT.Exp, bias=nmax[:, n % 2:n % 2 + 1],
                      accum_out=nmax[:, 2 + n % 2:3 + n % 2]).then_inc(sem("exp_ready"), 1)
                for g in range(2):
                    for j in range(i + 1):
                        b = done(act, f"pt{i}{g}{j}")
                        if i or g:
                            act.wait_ge(sem("products_done"), number[f"ol{i - (g == 0)}{1 - g}"] + 1)
                        A(PT[:, j, :], b[:, :], ACT.Copy).then_inc(sem("PT_ready"), 1)
            for m in range(4):
                b = done(act, f"ob{m}")
                A(oT[1][:, m, :], b[:, :], ACT.Copy).then_inc(sem("oTB_ready"), 1)

            for m in range(8):
                for br in range(3):
                    n = 3 * m + br
                    b = done(act, f"gate{m}{br}")
                    if n >= 2:
                        act.wait_ge(sem("up_read"), n - 1)
                    A(sgate[n % 2], b[:, :], ACT.Sigmoid).then_inc(sem("gate_ready"), 1)
            for i in range(TT):
                act.wait_ge(sem("x2_ready"), i + 1)
                link(A(sqx, x[:, i, :], ACT.Square, accum_out=stat[:, 8 + i:9 + i]))
                A(stat[:, 12 + i:13 + i], stat[:, 8 + i:9 + i], ACT.Sqrt, scale=1.0 / D, bias=epsc[:, 0:1]).then_inc(sem("rms_ready"), 1)
            for j in range(8):
                b = done(act, f"hT2{j}")
                A(hT[:, j, :], b[:, :], ACT.Copy).then_inc(sem("h2T_ready"), 1)
            for i in range(TT):
                b = done(act, f"rt{i}")
                A(score[:, i, :], b[:, 0:E], ACT.Sigmoid).then_inc(sem("rt_ready"), 1)
            for m in range(2):
                b = done(act, f"sg{m}")
                A(sgS[m], b[:, :], ACT.Silu).then_inc(sem("sg_ready"), 1)

            act.wait_ge(sem("table_ready"), 1)
            act.wait_ge(sem("x_added"), 8)
            pairs = act.value_load(npair[0:1, 0:1], min_val=1, max_val=UNITS // 2)

            def turn(c):
                A(hTe[c][:, 0:4, :], bank[0][:, :].rearrange("p (j t) -> p j t", j=4), ACT.Copy
                  ).then_inc(sem(f"hTe_a{c}"), 1)

            act.wait_ge(sem("trans_done0"), 2)
            turn(0)
            with act.Fori(0, pairs) as i:
                for b in range(2):
                    c = 1 - b
                    act.wait_ge(sem(f"gate_done{b}"), i + 1)
                    act.wait_ge(sem(f"acte_ready{b}"), i + 1)
                    A(sge[b], bank[2][:, 0:256].rearrange("p (m t) -> p m t", m=2), ACT.Silu).then_inc(sem(f"sge_ready{b}"), 1)
                    act.wait_ge(sem(f"trans_done{c}"), 2 * (i + b + 1))
                    act.wait_ge(sem(f"up_done{c}"), i + b + 1)
                    turn(c)
                    act.wait_ge(sem(f"y_done{b}"), 2 * i + 2)
                    act.wait_ge(sem(f"y_stored{b}"), 16 * i + 16)
                    A(ys[b][:, 0:512], bank[4 + 2 * b][:, :], ACT.Copy).then_inc(sem(f"y_a{b}"), 1)
            for i in range(TT):
                act.wait_ge(sem("x4_ready"), i + 1)
                link(A(ring[:, 0, 0:D], x[:, i, :], ACT.Square, accum_out=stat[:, i:i + 1]))
                A(stat[:, 4 + i:5 + i], stat[:, i:i + 1], ACT.Sqrt, scale=1.0 / D, bias=epsc[:, 0:1]).then_inc(sem("rms_ready"), 1)

        @block.vector
        def _(dve):
            v = nc.vector
            chain = [0]

            def link(ins):
                chain[0] += 1
                ins.then_inc(sem("dve_chain"), 1)
                dve.wait_ge(sem("dve_chain"), chain[0])

            dve.wait_ge(sem("consts"), 1)
            link(v.tensor_tensor(level_mask[:, 7, :], level_mask[:, 0, :], level_mask[:, 1, :], ALU.bitwise_xor))
            b = level_mask[:, 0, :]
            link(v.tensor_copy(b, before[:, :]))
            link(v.memset(level_mask[:, 6, :], 1000))
            link(v.copy_predicated(level_mask[:, 6, :], b, level_mask[:, 7, :]))
            for l in range(6):
                v.tensor_scalar(level_mask[:, l, :], level_mask[:, 6, :], float(P >> l), None, ALU.is_lt)
            link(v.tensor_scalar(level_mask[:, 7, :], level_mask[:, 7, :], 0.0, None, ALU.is_equal))
            link(v.tensor_scalar(level_mask[:, 6, :], level_mask[:, 6, :], 2.0, None, ALU.is_lt))

            dve.wait_ge(sem("consts_loaded"), NCONST[0])
            b = done(dve, "params")
            v.tensor_copy(par[:, :], b[:, 0:53]).then_inc(sem("params_ready"), 1)
            dve.wait_ge(sem("params_ready"), 1)
            dve.wait_ge(sem("rms_ready"), 1)
            link(v.reciprocal(stat[:, 8:12], stat[:, 4:8]))
            for i in range(TT):
                v.tensor_scalar(xn[:, i, :], x[:, i, :], stat[:, 8 + i:9 + i], None, ALU.mult).then_inc(sem("xn_ready"), 1)
            for c in range(4):
                b = done(dve, f"mc{c}")
                d0 = (8, 12, 0, 4)[c]
                v.tensor_tensor(mod1[:, d0:d0 + 4], b[:, 0:4], par[:, 8 + 4 * c:12 + 4 * c], ALU.add
                                ).then_inc(sem("mc_ready"), 1)
            dve.wait_ge(sem("mc_ready"), 4)
            v.scalar_tensor_tensor(out=mod1[:, 0:8], in0=mod1[:, 0:8], scalar=1.0, in1=par[:, 0:8], op0=ALU.add,
                                   op1=ALU.mult).then_inc(sem("mod1_ready"), 1)

            dve.wait_ge(sem("small_ready"), 1)
            for f in range(2):
                b = done(dve, f"la{f}")
                v.tensor_scalar(arg[0][:, f, :], b[:, :], par[:, 24 + f:25 + f], None, ALU.add).then_inc(sem("z_ready"), 1)
            dve.wait_ge(sem("z_ready"), 2)
            for f in range(2):
                dve.wait_ge(sem("lnz_ready"), f + 1)
                link(v.scalar_tensor_tensor(out=arg[1][:, f, :], in0=arg[0][:, f, :], scalar=0.0, in1=decay[:, f, :],
                                            op0=ALU.min, op1=ALU.subtract))
                link(v.tensor_scalar(arg[1][:, f, :], arg[1][:, f, :], 1.0 / 16.0, None, ALU.mult))
                ins = v.tensor_tensor_scan(cum[:, f, :], resets, arg[1][:, f, :], 0.0, ALU.mult, ALU.add)
                if f == 0:
                    link(ins)
            ins.then_inc(sem("cum_ready"), 1)
            dve.wait_ge(sem("cum_ready"), 1)
            for f in range(2):
                b = done(dve, f"ka{f}")
                v.tensor_copy(kT[:, f, :], b[:, :]).then_inc(sem("ka_ready"), 1)
            c8 = cum.rearrange("p f (i t) -> p (f i) t", t=P)
            a8 = arg[0].rearrange("p f (i t) -> p (f i) t", t=P)
            v.tensor_tensor(a8, c8[:, :, P - 1:P].to_broadcast([P, 8, P]), c8, ALU.subtract).then_inc(sem("kdarg_ready"), 1)
            for i in range(TT):
                b = done(dve, f"va{i}")
                v.tensor_copy(va[:, i, :], b[:, :]).then_inc(sem("v_ready"), 1)
            dve.wait_ge(sem("cleared"), 1)
            dve.wait_ge(sem("ecum_ready"), 1)
            dve.wait_ge(sem("qa_ready"), 2)
            for p in range(2):
                r = slice(64 * p, 64 * p + 64)
                v.tensor_tensor(qcz[p][r], qT[r], ecum[r], ALU.mult)
            dve.wait_ge(sem("ka_ready"), 2)
            dve.wait_ge(sem("kdE_ready"), 1)
            v.tensor_tensor(decay, decay, kT, ALU.mult).then_inc(sem("kd_ready"), 1)

            def level_arg(l):
                h = (P // 2) >> l
                cv = cum.rearrange("p f t -> p (f t)").rearrange("p (n b) -> p n b", b=2 * h)
                av = arg[l % 2].rearrange("p f t -> p (f t)").rearrange("p (n b) -> p n b", b=2 * h)
                ref = cv[:, :, h - 1:h].to_broadcast([P, 1024 // (2 * h), h])
                if l == 0:
                    dve.wait_ge(sem("kdE_ready"), 1)
                v.tensor_tensor(av[:, :, 0:h], ref, cv[:, :, 0:h], ALU.subtract)
                v.tensor_tensor(av[:, :, h:2 * h], cv[:, :, h:2 * h], ref, ALU.subtract).then_inc(sem("arg_ready"), 1)

            def level_mul(l):
                h = (P // 2) >> l
                dve.wait_ge(sem("E_ready"), l + 1)
                if l >= 2:
                    dve.wait_ge(sem("products_done"), number[f"scA{l - 2}3"] + 1)

                def halves(t):
                    return t.rearrange("p f t -> p (f t)").rearrange("p (n b) -> p n b", b=2 * h)

                v.tensor_tensor(halves(kE[l % 2])[:, :, 0:h], halves(kT)[:, :, 0:h], halves(decay)[:, :, 0:h], ALU.mult)
                v.tensor_tensor(halves(qE[l % 2])[:, :, h:2 * h], halves(qT)[:, :, h:2 * h],
                                halves(decay)[:, :, h:2 * h], ALU.mult).then_inc(sem("level_ready"), 1)

            def level_merge(l):
                m = level_mask[:, l:l + 1, :].to_broadcast([P, 4, P])
                for g in range(4):
                    b = done(dve, f"scA{l}{g}")
                    if l:
                        dve.wait_ge(sem("intra_done"), 4 * (l - 1) + g + 1)
                    tp = g % 2
                    v.copy_predicated(S[:, g // 2, 2 * tp:2 * tp + 2, :, :].rearrange("p i f t -> p (i f) t"), m,
                                      b[:, :].rearrange("p (n t) -> p n t", t=P)).then_inc(sem("intra_done"), 1)

            level_arg(0)
            for i in range(3):
                for f in range(2):
                    b = done(dve, f"st{i}{f}")
                    for p in range(2):
                        r = slice(64 * p, 64 * p + 64)
                        if i == 0:
                            ins = v.tensor_copy(state[r, i, f, :], b[r, tile_cols(p)])
                        else:
                            ins = v.scalar_tensor_tensor(out=state[r, i, f, :], in0=state[r, i - 1, f, :],
                                                         scalar=ecum[r, f, P * i + P - 1:P * i + P],
                                                         in1=b[r, tile_cols(p)], op0=ALU.mult, op1=ALU.add)
                    ins.then_inc(sem("state_ready"), 1)
                dve.wait_ge(sem("state_ready"), 2 * i + 2)
            for l in range(7):
                level_mul(l)
                if l < 6:
                    level_arg(l + 1)
                if l:
                    level_merge(l - 1)
            level_merge(6)
            level_merge(7)
            dve.wait_ge(sem("outgate_ready"), 4)
            for h in range(4):
                dve.wait_ge(sem("root_ready"), h + 1)
                if h:
                    dve.wait_ge(sem("oTA_ready"), h)
                link(v.reciprocal(hA, rsA[h % 2]))
                b = done(dve, f"oA{h}")
                v.scalar_tensor_tensor(out=hA, in0=b[:, :], scalar=par[:, 26 + h:27 + h], in1=hA, op0=ALU.mult,
                                       op1=ALU.mult).then_inc(sem("oA_read"), 1)
                dve.wait_ge(sem("oA_read"), h + 1)
                v.tensor_tensor(oT[0][:, h, :], hA, sga[:, h, :], ALU.mult).then_inc(sem("oTA_ready"), 1)
            dve.wait_ge(sem("oTA_ready"), 4)

            fb, lnf, G, u, M, mt, ib, lf = g4
            link(v.tensor_copy(fb, small[96:100, :]))
            link(v.tensor_copy(ib, small[64:68, :]))
            v.tensor_scalar(fb, fb, bif[:, 1:2], None, ALU.add).then_inc(sem("fb_ready"), 1)
            dve.wait_ge(sem("fb_ready"), 1)
            link(v.tensor_scalar(ib, ib, bif[:, 0:1], None, ALU.add))
            dve.wait_ge(sem("cleared"), 2)
            dve.wait_ge(sem("lnf_ready"), 1)
            link(v.scalar_tensor_tensor(out=lf, in0=fb, scalar=0.0, in1=lnf, op0=ALU.min, op1=ALU.subtract))
            link(v.tensor_tensor_scan(G, ones4, lf, 0.0, ALU.mult, ALU.add))
            link(v.tensor_tensor(u, ib, G, ALU.subtract))
            link(v.tensor_tensor_scan(M, ones4, u, 0.0, ALU.mult, ALU.max))
            v.tensor_tensor(mt, G, M, ALU.add).then_inc(sem("scans_ready"), 1)
            for f in range(4):
                b = done(dve, f"qk{f}")
                v.tensor_copy(raw[:, f, 3:515], b[:, :]).then_inc(sem("qk_ready"), 1)
                dve.wait_ge(sem("qk_ready"), f + 1)
                link(v.tensor_scalar(qkc[:, f, :], raw[:, f, 0:512], par[:, 37 + f:38 + f], None, ALU.mult))
                for k in range(1, 4):
                    ins = v.scalar_tensor_tensor(out=qkc[:, f, :], in0=raw[:, f, k:k + 512],
                                                 scalar=par[:, 37 + 4 * k + f:38 + 4 * k + f], in1=qkc[:, f, :],
                                                 op0=ALU.mult, op1=ALU.add)
                    if k < 3:
                        link(ins)
                ins.then_inc(sem("conv_ready"), 1)
            b = done(dve, "uT")
            v.tensor_copy(ucol, b[:, 0:16].rearrange("p (i h) -> p i h", i=TT)).then_inc(sem("u_ready"), 1)
            for i in range(TT):
                b = done(dve, f"vc{i}")
                v.tensor_copy(vc[:, i, :], b[:, :]).then_inc(sem("v_ready"), 1)
            dve.wait_ge(sem("u_ready"), 1)
            for h in range(4):
                def arg_c(j):
                    n = 4 * h + j
                    bm = done(dve, f"bm{h}")
                    if n >= 2:
                        dve.wait_ge(sem("W_ready"), n - 1)
                    v.tensor_scalar(argC[n % 2][:, 0:T - P * j], bm[:, P * j:T], ucol[:, j, h:h + 1], 0.0,
                                    ALU.subtract, ALU.max).then_inc(sem("argC_ready"), 1)

                arg_c(0)
                if h:
                    dve.wait_ge(sem("products_done"), number[f"den{h - 1}"] + 1)
                for j in range(TT):
                    if j < 3:
                        arg_c(j + 1)
                    n = 4 * h + j
                    dve.wait_ge(sem("W_ready"), n + 1)
                    link(v.tensor_tensor(W[n % 2][:, 0:P], W[n % 2][:, 0:P], causal[:, :], ALU.mult))
                    b = done(dve, f"scC{h}{j}")
                    v.scalar_tensor_tensor(out=SW[:, j, P * j:T], in0=b[:, P * j:T], scalar=0.125,
                                           in1=W[n % 2][:, 0:T - P * j], op0=ALU.mult, op1=ALU.mult
                                           ).then_inc(sem("SW_ready"), 1)
                dve.wait_ge(sem("floor_ready"), h + 1)
                if h:
                    dve.wait_ge(sem("oTC_ready"), h)
                b = done(dve, f"den{h}")
                link(v.scalar_tensor_tensor(out=hD, in0=b[:, :], scalar=-1.0, in1=floor_, op0=ALU.mult, op1=ALU.max))
                v.tensor_tensor(hD, b[:, :], hD, ALU.max).then_inc(sem("den_read"), 1)
                dve.wait_ge(sem("den_read"), h + 1)
                link(v.reciprocal(hD, hD))
                b = done(dve, f"num{h}")
                v.tensor_tensor(hC, b[:, :], hD, ALU.mult).then_inc(sem("hC_ready"), 1)
                dve.wait_ge(sem("hC_ready"), h + 1)
                dve.wait_ge(sem("root_ready"), h + 5)
                link(v.reciprocal(hD, rsC))
                link(v.scalar_tensor_tensor(out=hD, in0=hC, scalar=par[:, 33 + h:34 + h], in1=hD, op0=ALU.mult,
                                            op1=ALU.mult))
                dve.wait_ge(sem("outgate_ready"), h + 5)
                v.tensor_tensor(oT[2][:, h, :], hD, soc[:, h, :], ALU.mult).then_inc(sem("oTC_ready"), 1)
            dve.wait_ge(sem("oTC_ready"), 4)

            v.tensor_copy(wki4, wki[:, :, :].rearrange("p j (o d) -> p j o d", o=1).to_broadcast([P, 8, 4, 32])
                          ).then_inc(sem("wki4_ready"), 1)
            v.tensor_copy(wi0[:, :], small[32:40, :]).then_inc(sem("wi0_ready"), 1)
            for n in range(3):
                b = done(dve, f"cl{n}")
                v.tensor_copy(craw[:, n, :], b[:, :]).then_inc(sem("craw_ready"), 1)
            b = done(dve, "wi")
            v.tensor_scalar(wcol[:, :, :], b[:, 0:32].rearrange("p (i h) -> p i h", i=TT), float(8 ** -0.5), None,
                            ALU.mult).then_inc(sem("wcol_ready"), 1)
            b = done(dve, "uk")
            v.tensor_copy(ukT, b[:, :].rearrange("p (i h) -> p i h", i=4)).then_inc(sem("ukT_ready"), 1)
            dve.wait_ge(sem("craw_ready"), 3)
            for n in range(2):
                dve.wait_ge(sem("root_ready"), n + 9)
                link(v.reciprocal(rsB[:, n, :], rsB[:, n, :]))
                for k in (0, 1) if n == 0 else (2,):
                    ins = v.scalar_tensor_tensor(out=cn[:, k, :], in0=craw[:, k, :], scalar=par[:, 30 + k:31 + k],
                                                 in1=rsB[:, n, :], op0=ALU.mult, op1=ALU.mult)
                ins.then_inc(sem("cn_ready"), 1)
            dve.wait_ge(sem("wcol_ready"), 1)
            dve.wait_ge(sem("cleared"), 3)
            link(v.tensor_scalar(selm[:, 0:P], future[:, :], 0.0, None, ALU.is_equal))
            v.copy_predicated(Dm[:, 0, 0:P], selm[:, 0:P], distv[:, 384:384 + P]).then_inc(sem("D_ready"), 1)
            for i in range(1, TT):
                N = P * (i + 1)
                for h in range(8):
                    n = 8 * (i - 1) + h
                    dve.wait_ge(sem("relu_ready"), n + 1)
                    if h == 0:
                        ins = v.tensor_scalar(I_s[:, 0:N], rl[n % 2][:, 0:N], wcol[:, i, 0:1], None, ALU.mult)
                    else:
                        ins = v.scalar_tensor_tensor(out=I_s[:, 0:N], in0=rl[n % 2][:, 0:N], scalar=wcol[:, i, h:h + 1],
                                                     in1=I_s[:, 0:N], op0=ALU.mult, op1=ALU.add)
                    ins.then_inc(sem("relu_used"), 1)
                    dve.wait_ge(sem("relu_used"), n + 1)
                link(v.copy_predicated(I_s[:, P * i:N], future[:, :], negc[:, :]))
                for _ in range(KEYS // 8):
                    link(v.max(top8[:, :], I_s[:, 0:N]))
                    link(v.match_replace(I_s[:, 0:N], top8[:, :], I_s[:, 0:N], NEG_TAKEN))
                link(v.tensor_scalar(selm[:, 0:N], I_s[:, 0:N], -2e38, None, ALU.is_lt))
                off = 384 - P * i
                v.copy_predicated(Dm[:, i, 0:N], selm[:, 0:N], distv[:, off:off + N]).then_inc(sem("D_ready"), 1)
            dve.wait_ge(sem("D_ready"), 4)
            def logits(i, h):
                n, N = 8 * i + h, P * (i + 1)
                b = done(dve, f"lg{i}{h}")
                if n >= 2:
                    dve.wait_ge(sem("exp_ready"), n - 1)
                v.scalar_tensor_tensor(out=L[n % 2][:, 0:N], in0=Dm[:, i, 0:N], scalar=float(2.0 ** -(h + 1)),
                                       in1=b[:, 0:N], op0=ALU.mult, op1=ALU.add).then_inc(sem("L_ready"), 1)
                dve.wait_ge(sem("L_ready"), n + 1)
                if n >= 2:
                    dve.wait_ge(sem("P_ready"), n - 1)
                v.tensor_reduce(nmax[:, n % 2:n % 2 + 1], L[n % 2][:, 0:N], AX, ALU.max, negate=True
                                ).then_inc(sem("nmax_ready"), 1)

            def normalise(i, h):
                n, N = 8 * i + h, P * (i + 1)
                dve.wait_ge(sem("exp_ready"), n + 1)
                link(v.reciprocal(top8[:, n % 2:n % 2 + 1], nmax[:, 2 + n % 2:3 + n % 2]))
                v.tensor_scalar(Pn[:, h, 0:N], Pn[:, h, 0:N], top8[:, n % 2:n % 2 + 1], None, ALU.mult
                                ).then_inc(sem("P_ready"), 1)

            for i in range(TT):
                for h in range(8):
                    logits(i, h)
                    if h:
                        normalise(i, h - 1)
                normalise(i, 7)
                for g in range(2):
                    b = done(dve, f"ol{i}{g}")
                    v.tensor_copy(olT[:, 4 * g:4 * g + 4, tile_cols(i)], b[:, :].rearrange("p (h t) -> p h t", h=4)
                                  ).then_inc(sem("ol_ready"), 1)

            dve.wait_ge(sem("oTB_ready"), 4)
            v.tensor_copy(csrep2, cs[:, :].rearrange("p (j o) -> p j o", o=1).to_broadcast([P, 8, P])
                          ).then_inc(sem("csrep_ready"), 1)
            dve.wait_ge(sem("extra_loaded"), 96)
            for c in range(8):
                b = done(dve, f"mb{c}")
                dst = modB[:, c // 2, 512 * (c % 2):512 * (c % 2) + 512]
                if c // 2 == 2:
                    ins = v.scalar_tensor_tensor(out=dst, in0=b[:, :], scalar=1.0, in1=nffn[:, 512 * (c % 2):512 * (c % 2) + 512],
                                                 op0=ALU.add, op1=ALU.mult)
                else:
                    ins = v.tensor_copy(dst, b[:, :])
                ins.then_inc(sem("mb_ready"), 1)
            dve.wait_ge(sem("mb_ready"), 8)
            for m in range(8):
                for br in range(3):
                    n = 3 * m + br
                    dve.wait_ge(sem("gate_ready"), n + 1)
                    b = done(dve, f"up{m}{br}")
                    dst = mT[:, m, :] if br == 0 else mtmp[n % 2]
                    v.tensor_tensor(dst, b[:, :], sgate[n % 2], ALU.mult).then_inc(sem("up_read"), 1)
                    dve.wait_ge(sem("up_read"), n + 1)
                    if br:
                        ins = v.tensor_tensor(mT[:, m, :], mT[:, m, :], mtmp[n % 2], ALU.add)
                        if br == 1:
                            link(ins)
                        else:
                            ins.then_inc(sem("mT_ready"), 1)
            for i in range(TT):
                for n in range(2):
                    b = done(dve, f"wo{i}{n}")
                    v.tensor_tensor(wtmp, b[:, :], modB[:, 0, 512 * n:512 * n + 512], ALU.mult).then_inc(sem("wo_read"), 1)
                    dve.wait_ge(sem("wo_read"), 2 * i + n + 1)
                    dst = x[:, i, 512 * n:512 * n + 512]
                    ins = v.tensor_tensor(dst, dst, wtmp, ALU.add)
                    if n:
                        ins.then_inc(sem("x2_ready"), 1)
                    else:
                        link(ins)
                dve.wait_ge(sem("x2_ready"), i + 1)
                dve.wait_ge(sem("rms_ready"), i + 2)
                link(v.reciprocal(stat[:, 12 + i:13 + i], stat[:, 12 + i:13 + i]))
                link(v.scalar_tensor_tensor(out=h2[:, i, :], in0=x[:, i, :], scalar=stat[:, 12 + i:13 + i],
                                            in1=modB[:, 2, :], op0=ALU.mult, op1=ALU.mult))
                v.tensor_tensor(h2[:, i, :], h2[:, i, :], modB[:, 1, :], ALU.add).then_inc(sem("h2_ready"), 1)

            for i in range(TT):
                dve.wait_ge(sem("rt_ready"), i + 1)
                sel = selr[:, i, :]
                link(v.tensor_tensor(sel, score[:, i, :], rbias[:, :], ALU.add))
                for g in range(GROUPS):
                    ins = v.max(gtop[:, g, :], sel[:, 8 * g:8 * g + 8])
                link(ins)
                link(v.tensor_tensor(gsc[:, :], gtop[:, :, 0], gtop[:, :, 1], ALU.add))
                link(v.max(gm8[:, :], gsc[:, :]))
                link(v.max_index(gidx[:, :], gm8[:, :], gsc[:, :]))
                link(v.tensor_copy(gidf[:, :], gidx[:, :]))
                link(v.tensor_scalar(gmask[:, :], iota_e[:, 0:8], gidf[:, 0:1], None, ALU.is_equal))
                for k in range(1, TOPG):
                    link(v.scalar_tensor_tensor(out=gmask[:, :], in0=iota_e[:, 0:8], scalar=gidf[:, k:k + 1],
                                                in1=gmask[:, :], op0=ALU.is_equal, op1=ALU.add))
                gb = gmask[:, :].rearrange("p (g o) -> p g o", o=1).to_broadcast([P, 8, 8])
                s3 = sel.rearrange("p (g e) -> p g e", g=8)
                link(v.tensor_tensor(s3, s3, gb, ALU.mult))
                link(v.tensor_scalar(gmask[:, :], gmask[:, :], 1.0, 1e30, ALU.subtract, ALU.mult))
                link(v.tensor_tensor(s3, s3, gb, ALU.add))
                link(v.max(gm8[:, :], sel))
                link(v.max_index(eidx[:, :], gm8[:, :], sel))
                link(v.tensor_copy(eidf[:, :], eidx[:, :]))
                for k in range(TOPK):
                    ins = v.tensor_scalar(onehot[:, k, :], iota_e[:, :], eidf[:, k:k + 1], None, ALU.is_equal)
                link(ins)
                for k in range(TOPK):
                    ins = v.tensor_tensor_reduce(rt_tmp, onehot[:, k, :], score[:, i, :], 1.0, 0.0, ALU.mult,
                                                 ALU.add, wk[:, i, k:k + 1])
                    link(ins)
                link(v.tensor_copy(eall[:, i, :], eidf[:, :]))
                link(v.tensor_reduce(wsum[:, :], wk[:, i, 0:TOPK], AX, ALU.add))
                link(v.reciprocal(wsum[:, :], wsum[:, :]))
                v.tensor_scalar(wk[:, i, 0:TOPK], wk[:, i, 0:TOPK], wsum[:, 0:1], 2.5, ALU.mult, ALU.mult)
                v.tensor_reduce(mall[:, i, :], onehot[:, 0:TOPK, :].rearrange("p k e -> p e k"), AX, ALU.add
                                ).then_inc(sem("mall_ready"), 1)
                dve.wait_ge(sem("mall_ready"), i + 1)
            b = done(dve, "tot")
            link(v.tensor_scalar(ntile, b[:, 0:E], 0.0, None, ALU.is_gt))
            for q in range(1, TT - 1):
                link(v.scalar_tensor_tensor(out=ntile, in0=b[:, 0:E], scalar=float(P * q), in1=ntile, op0=ALU.is_gt,
                                            op1=ALU.add))
            v.scalar_tensor_tensor(out=ntile, in0=b[:, 0:E], scalar=float(P * (TT - 1)), in1=ntile, op0=ALU.is_gt,
                                   op1=ALU.add).then_inc(sem("tot_read"), 1)
            dve.wait_ge(sem("tot_read"), 1)
            link(v.memset(rt_tmp, 1.0))
            link(v.tensor_tensor_scan(uend, rt_tmp, ntile, 0.0, ALU.mult, ALU.add))
            link(v.tensor_tensor(base, uend, ntile, ALU.subtract))
            v.tensor_scalar(base, base, float(P), None, ALU.mult).then_inc(sem("uend_ready"), 1)
            dve.wait_ge(sem("uend_ready"), 1)
            for i in range(TT):
                b = done(dve, f"pos{i}")
                v.tensor_tensor(slotA, b[:, 0:E], base, ALU.add).then_inc(sem("slot_done"), 1)
                dve.wait_ge(sem("slot_done"), i + 1)
                for k in range(TOPK):
                    link(v.tensor_scalar(rt_tmp2, iota_e[:, :], eall[:, i, k:k + 1], None, ALU.is_equal))
                    link(v.tensor_tensor_reduce(rt_tmp2, rt_tmp2, slotA, 1.0, 0.0, ALU.mult, ALU.add,
                                                slotf[:, i, k:k + 1]))
                v.tensor_copy(sloti[:, i, 0:TOPK], slotf[:, i, 0:TOPK]).then_inc(sem("slots_ready"), 1)
            b = done(dve, "ue")
            v.tensor_copy(ucolf[:, :], b[0:E, 0:1]).then_inc(sem("ue_ready"), 1)
            dve.wait_ge(sem("ue_ready"), 1)
            v.tensor_scalar(ucmp[:, :], iota_u[:, :], ucolf[:, 0:1], None, ALU.is_ge).then_inc(sem("ucmp_ready"), 1)
            b = done(dve, "uc")
            v.tensor_scalar(uexp[:, :], b[0:1, 0:96], float(E - 1), None, ALU.min).then_inc(sem("uc_ready"), 1)
            link(v.tensor_scalar(npf[:, :], iota_e[0:1, :], 2.0, uend[0:1, E - 1:E], ALU.mult, ALU.is_lt))
            link(v.tensor_reduce(npg[:, :], npf[:, :], AX, ALU.add))
            v.tensor_copy(npair[:, :], npg[:, :]).then_inc(sem("table_ready"), 1)
            for m in range(2):
                dve.wait_ge(sem("sg_ready"), m + 1)
                b = done(dve, f"su{m}")
                v.tensor_tensor(actS[:, m, :], b[:, :], sgS[m], ALU.mult).then_inc(sem("actS_ready"), 1)
            for i in range(TT):
                for n in range(2):
                    b = done(dve, f"sd{i}{n}")
                    v.tensor_tensor(wtmp2, b[:, :], modB[:, 3, 512 * n:512 * n + 512], ALU.mult).then_inc(sem("sd_read"), 1)
                    dve.wait_ge(sem("sd_read"), 2 * i + n + 1)
                    dst = x[:, i, 512 * n:512 * n + 512]
                    v.tensor_tensor(dst, dst, wtmp2, ALU.add).then_inc(sem("x_added"), 1)
                    dve.wait_ge(sem("x_added"), 2 * i + n + 1)
            dve.wait_ge(sem("table_ready"), 1)
            dve.wait_ge(sem("x_added"), 8)
            pairs = dve.value_load(npair[0:1, 0:1], min_val=1, max_val=UNITS // 2)

            def turn(c):
                v.tensor_copy(hTe[c][:, 4:8, :], bank[1][:, :].rearrange("p (j t) -> p j t", j=4)
                              ).then_inc(sem(f"hTe_v{c}"), 1)

            dve.wait_ge(sem("trans_done0"), 3)
            turn(0)
            with dve.Fori(0, pairs) as i:
                for b in range(2):
                    c = 1 - b
                    dve.wait_ge(sem(f"up_done{b}"), i + 2)
                    dve.wait_ge(sem(f"sge_ready{b}"), i + 2)
                    dve.wait_ge(sem(f"y_done{b}"), 2 * i + 1)
                    v.tensor_tensor(acte[b], bank[3][:, 0:256].rearrange("p (m t) -> p m t", m=2), sge[b],
                                    ALU.mult).then_inc(sem(f"acte_ready{b}"), 1)
                    dve.wait_ge(sem(f"trans_done{c}"), 2 * (i + b) + 3)
                    turn(c)
                    dve.wait_ge(sem(f"y_done{b}"), 2 * i + 3)
                    dve.wait_ge(sem(f"y_stored{b}"), 16 * i + 16)
                    v.tensor_copy(ys[b][:, 512:1024], bank[5 + 2 * b][:, :]).then_inc(sem(f"y_v{b}"), 1)
            dve.wait_ge(sem("extra_loaded"), 112)
            for i in range(TT):
                for k in range(TOPK):
                    n = TOPK * i + k
                    dve.wait_ge(sem(f"yk_loaded{i % 2}"), 16 * (i // 2 + 1))
                    if k == 0:
                        ins = v.tensor_scalar(routed, yk[i % 2][:, k, :], wk[:, i, 0:1], None, ALU.mult)
                    else:
                        ins = v.scalar_tensor_tensor(out=routed, in0=yk[i % 2][:, k, :], scalar=wk[:, i, k:k + 1], in1=routed,
                                                     op0=ALU.mult, op1=ALU.add)
                    ins.then_inc(sem("yk_used"), 1)
                    dve.wait_ge(sem("yk_used"), n + 1)
                link(v.tensor_tensor(routed, routed, modB[:, 3, :], ALU.mult))
                v.tensor_tensor(x[:, i, :], x[:, i, :], routed, ALU.add).then_inc(sem("x4_ready"), 1)
                dve.wait_ge(sem("x4_ready"), i + 1)
                dve.wait_ge(sem("rms_ready"), i + 6)
                link(v.reciprocal(stat[:, 4 + i:5 + i], stat[:, 4 + i:5 + i]))
                v.scalar_tensor_tensor(out=x[:, i, :], in0=x[:, i, :], scalar=stat[:, 4 + i:5 + i], in1=nfin,
                                       op0=ALU.mult, op1=ALU.mult).then_inc(sem("out_ready"), 1)


_INS = ['x', 'c', 'ada_w', 'ada_b', 'norm_mix', 'norm_ffn', 'w_in', 'gla_w_a2', 'gla_b_a', 'gla_norm',
        'dsa_norm_q', 'dsa_norm_kv', 'dsa_w_uq', 'dsa_w_uk', 'dsa_w_uv', 'dsa_w_qi', 'mlstm_conv', 'mlstm_b_i',
        'mlstm_b_f', 'mlstm_norm', 'w_up_a', 'w_up_b', 'w_up_c', 'w_o', 'router_w', 'router_bias', 'exp_w_gate',
        'exp_w_up', 'exp_w_down', 'sh_w_gate', 'sh_w_up', 'sh_w_down', 'norm_final']


def kernel(**inputs):
    import numpy as _np
    import concourse.bacc as _bacc
    from concourse import mybir as _mybir
    from concourse.bass_utils import run_bass_kernel_spmd as _run

    nc = _bacc.Bacc("TRN2", target_bir_lowering=False, num_devices=1)
    arrays, aps = {}, {}
    for name in _INS:
        v = _np.ascontiguousarray(inputs[name])
        arrays[f"in_{name}"] = v
        aps[name] = nc.dram_tensor(f"in_{name}", v.shape, _mybir.dt.from_np(v.dtype), kind="ExternalInput").ap()
    shape = inputs["x"].shape
    out = nc.dram_tensor("out_0", shape, _mybir.dt.float32, kind="ExternalOutput").ap()
    hybrid_kernel(nc, aps, out)
    r = _run(nc, [arrays], core_ids=[0])
    return r.results[0]["out_0"]
```

```python
from contextlib import ExitStack

import numpy as np

import concourse.bass as bass
from concourse import mybir

F32 = mybir.dt.float32
F32R = mybir.dt.float32r
I32 = mybir.dt.int32
U32 = mybir.dt.uint32
ALU = mybir.AluOpType
ACT = mybir.ActivationFunctionType
AX = mybir.AxisListType.X

P = 128
BANKS = 8
EPS = 1e-6
NEG_MASK = -1e30
NEG_FUTURE = -1e38
NEG_TAKEN = -3e38

IN_SIZES = dict(qa=256, ka=256, va=512, ga=512, a_lr=16, cq=256, ckv=128, k_idx=32, w_idx=8,
                qc=256, kc=256, vc=512, ic=4, fc=4, oc=512, gates=3072)
COL = {}
_at = 0
for _n, _w in IN_SIZES.items():
    COL[_n] = _at
    _at += _w


def tile_cols(i, n=P):
    return slice(i * n, (i + 1) * n)


def merge_steps():
    return [(m + r, b) for m in range(0, 8, 2) for b in range(3) for r in range(2)]


def product_order():
    out = [("params", "params_ready", 1)]
    out += [(f"mc{c}", "mc_ready", c + 1) for c in range(4)]
    out += [(f"xT{j}", "hT_ready", j + 1) for j in range(8)]
    out += [("small", "small_ready", 1)]
    out += [(f"la{f}", "z_ready", f + 1) for f in range(2)]
    out += [(f"qa{f}", "qa_ready", f + 1) for f in range(2)]
    out += [(f"ka{f}", "ka_ready", f + 1) for f in range(2)]
    out += [(f"va{i}", "v_ready", i + 1) for i in range(4)]
    out += [(f"kd{f}", "kdr_ready", f + 1) for f in range(2)]
    out += [(f"st{i}{f}", "state_ready", 2 * i + f + 1) for i in range(3) for f in range(2)]
    out += [(f"scA{l}{g}", "intra_done", 4 * l + g + 1) for l in range(8) for g in range(4)]
    out += [(f"ga{m}", "outgate_ready", m + 1) for m in range(4)]
    for h in range(5):
        out += [(f"oA{h}", "oA_read", h + 1)] if h < 4 else []
        out += [(f"msA{h - 1}", "root_ready", h)] if h >= 1 else []
    out += [(f"qk{f}", "qk_ready", f + 1) for f in range(4)]
    out += [("uT", "u_ready", 1)]
    out += [(f"vc{i}", "v_ready", i + 5) for i in range(4)]
    out += [(f"oc{m}", "outgate_ready", m + 5) for m in range(4)]
    for h in range(4):
        out += [(f"bm{h}", "SW_ready", 4 * h + 4), (f"bt{h}", "floor_ready", h + 1)]
        out += [(f"scC{h}{j}", "SW_ready", 4 * h + j + 1) for j in range(4)]
        out += [(f"num{h}", "hC_ready", h + 1), (f"den{h}", "den_read", h + 1)]
        out += [(f"msC{h}", "root_ready", h + 5)]
    out += [("kidx", "kidx_ready", 1)]
    out += [(f"cl{n}", "craw_ready", n + 1) for n in range(3)]
    out += [("msq", "root_ready", 9), ("mskv", "root_ready", 10)]
    out += [("wi", "wcol_ready", 1), ("uk", "ukT_ready", 1)]
    out += [("ckr", "ckr_ready", 1)]
    out += [(f"qi{m}", "qi_ready", m + 1) for m in range(2)]
    out += [(f"ix{i}{h}", "relu_ready", 8 * (i - 1) + h + 1) for i in range(1, 4) for h in range(8)]
    out += [(f"q{m}", "q_ready", m + 1) for m in range(4)]
    out += [(f"ql{h}", "ql_ready", h + 1) for h in range(8)]
    for i in range(4):
        out += [(f"lg{i}{h}", "L_ready", 8 * i + h + 1) for h in range(8)]
        for g in range(2):
            n = 2 * (i * (i + 1) // 2) + g * (i + 1)
            out += [(f"pt{i}{g}{j}", "PT_ready", n + j + 1) for j in range(i + 1)]
            out += [(f"ol{i}{g}", "ol_ready", 2 * i + g + 1)]
    out += [(f"ob{m}", "oTB_ready", m + 1) for m in range(4)]
    for n, (m, b) in enumerate(merge_steps()):
        out += [(f"gate{m}{b}", "gate_ready", n + 1), (f"up{m}{b}", "up_read", n + 1)]
        if n % 2 and n // 2 < 8:
            out += [(f"mb{n // 2}", "mb_ready", n // 2 + 1)]
    out += [(f"wo{i}{n}", "wo_read", 2 * i + n + 1) for i in range(4) for n in range(2)]
    out += [(f"hT2{j}", "h2T_ready", j + 1) for j in range(8)]
    out += [(f"rt{i}", "rt_ready", i + 1) for i in range(4)]
    out += [(f"pos{i}", "slot_done", i + 1) for i in range(4)] + [("tot", "tot_read", 1), ("ue", "ue_ready", 1)]
    out += [("uc", "uc_ready", 1)]
    out += [(x, n, v) for m in range(2) for x, n, v in ((f"sg{m}", "sg_ready", m + 1), (f"su{m}", "actS_ready", m + 1))]
    out += [(f"sd{i}{n}", "sd_read", 2 * i + n + 1) for i in range(4) for n in range(2)]
    return out


def hybrid_kernel(nc, a, out):
    T, D = a["x"].shape[1:]
    TT, KT = T // P, D // P
    E = a["router_w"].shape[2]
    FF = a["exp_w_gate"].shape[3]
    TOPK, GROUPS, TOPG = 6, 8, 4
    KEYS = T // 4
    UNITS = E + T * TOPK // P
    assert (T, D, TT, KT, E, FF) == (512, 1024, 4, 8, 64, 256)

    products = product_order()
    number = {name: n for n, (name, _, _) in enumerate(products)}
    assert len(number) == len(products)

    ctx = ExitStack()
    with ctx:
        sems = {}

        def sem(name):
            if name not in sems:
                sems[name] = ctx.enter_context(nc.semaphore(name))
            return sems[name]

        def sb(name, shape, dt=F32):
            return ctx.enter_context(nc.sbuf_tensor(name, shape, dt))

        def sb_two(name, shape):
            with nc.sbuf_tensor(name, shape, F32) as plain:
                pass
            parts = sb(name + "_parts", shape, F32R)
            return plain, parts

        bank = [ctx.enter_context(nc.psum_tensor(f"bank{i}", [P, 512], F32)) for i in range(BANKS)]

        x = sb("x", [P, TT, D])
        hT = sb("hT", [P, KT, T])
        oT, oTp = zip(*[sb_two(f"oT{b}", [P, 4, T]) for b in "ABC"])
        RING = 3
        ring, ringp = sb_two("ring", [P, RING, 4096])
        arena, arenap = sb_two("arena", [P, 22528])
        ident = sb("ident", [P, P])
        ones = sb("ones", [P, P])
        causal = sb("causal", [P, P])
        before = sb("before", [P, P])
        future = sb("future", [P, P], I32)
        negc = sb("negc", [P, P])
        small = sb("small", [P, T])
        prow = sb("prow", [53, P])
        par = sb("par", [P, 53])
        stat = sb("stat", [P, 16])
        epsc = sb("epsc", [P, 1])
        cs = sb("cs", [P, 8])
        c_in = sb("c_in", [P, 8])
        mod1 = sb("mod1", [P, 16])
        bif = sb("bif", [4, 2])
        iota_e = sb("iota_e", [P, E])
        wcol = sb("wcol", [P, TT, 8])

        class Region:
            def __init__(self, tensor, start=0, end=None):
                self.t, self.at, self.end = tensor, start, end

            def take(self, *shape, dt=F32, parts=P):
                n = int(np.prod(shape))
                assert self.end is None or self.at + n <= self.end, (self.at, n, self.end)
                v = self.t[0:parts, self.at:self.at + n]
                if dt not in (F32, F32R):
                    v = v.bitcast(dt)
                self.at += n
                if len(shape) == 2:
                    v = v.rearrange("p (a b) -> p a b", a=shape[0])
                elif len(shape) == 3:
                    v = v.rearrange("p (a b c) -> p a b c", a=shape[0], b=shape[1])
                elif len(shape) == 4:
                    v = v.rearrange("p (a b c d) -> p a b c d", a=shape[0], b=shape[1], c=shape[2])
                return v

        END = 22528
        r0 = Region(arena, 0, END)
        xn = r0.take(TT, D)
        junk = r0.take(D)
        ra = Region(arena, 0, END)
        qT, kT, cum = ra.take(2, T), ra.take(2, T), ra.take(2, T)
        arg = [ra.take(2, T) for _ in range(2)]
        decay = ra.take(2, T)
        qE = [ra.take(2, T) for _ in range(2)]
        kE = [ra.take(2, T) for _ in range(2)]
        va = ra.take(TT, T)
        S = ra.take(2, TT, 2, P)
        sga = ra.take(4, T)
        qcz = [ra.take(2, T) for _ in range(2)]
        state = ra.take(3, 2, P)
        rsA = [ra.take(T) for _ in range(2)]
        hA = ra.take(T)
        ra2 = Region(oT[1][:].rearrange("p a b -> p (a b)"), 0, 2048)
        ecum, kdr = ra2.take(2, T), ra2.take(TT, 2, P)
        ra3 = Region(oT[2][:].rearrange("p a b -> p (a b)"), 0, 2048)
        level_mask = ra3.take(8, P, dt=I32)
        resets = ra3.take(T)
        sqA = ra3.take(T)
        w_a2 = sb("w_a2", [16, 256])
        rc = Region(arena, 0, END)
        raw = rc.take(4, 516)
        qkc = rc.take(4, T)
        vc, soc = rc.take(TT, T), rc.take(4, T)
        floor_, hC, sqC, rsC = rc.take(T), rc.take(T), rc.take(T), rc.take(T)
        argC = [rc.take(T) for _ in range(2)]
        W = [rc.take(T) for _ in range(2)]
        SW = rc.take(TT, T)
        sel4 = rc.take(4, P, parts=4)
        g4 = [rc.take(T, parts=4) for _ in range(8)]
        ones4 = rc.take(T, parts=4)
        ucol = rc.take(TT, 4)
        hD = rc.take(T)
        rb = Region(arena, 0, END)
        cn, kidxT, qlT, qiT = rb.take(3, T), rb.take(T), rb.take(8, T), rb.take(2, T)
        Dm, ckr, w_uv = rb.take(TT, T), rb.take(TT, P), rb.take(T)
        distv = rb.take(896)
        rb1 = Region(arena, rb.at, END)
        craw, sqB, rsB, qTb = rb1.take(3, T), rb1.take(3, T), rb1.take(2, T), rb1.take(4, T)
        w_uq, w_uk, w_qi, ukT = rb1.take(2, T), rb1.take(T), rb1.take(2, 256), rb1.take(4, P)
        rl = [rb1.take(T) for _ in range(2)]
        I_s = rb1.take(T)
        wki4 = rb1.take(8, 4, 32)
        selm = qTb[:, 0, :].bitcast(I32)
        wi0 = sb("wi0", [8, T])
        top8 = sb("top8", [P, 8])
        rb2 = Region(arena, rb.at, END)
        Pn, PT, olT = rb2.take(8, T), rb2.take(TT, T), rb2.take(8, T)
        L = [rb2.take(T) for _ in range(2)]
        nmax = sb("nmax", [P, 4])
        modB = arena[:, 18432:22528].rearrange("p (a b) -> p a b", a=4)
        mT = arena[:, 14336:18432].rearrange("p (a b) -> p a b", a=8)
        rm = Region(arena, 0, 14336)
        adab = rm.take(4096, parts=1)
        nffn = rm.take(D)
        sgate = [rm.take(T) for _ in range(2)]
        mtmp = [rm.take(T) for _ in range(2)]
        wtmp = rm.take(T)
        cond_merge = [rm.take(T) for _ in range(2)]
        h2 = rm.take(TT, D)
        sqx = rm.take(D)
        re = Region(arena, 0, 14336)
        ringf = ring[:].rearrange("p s n -> p (s n)")
        rw_ = Region(ringf, 0, 12288)
        w_at = [None, None]
        for b in (1, 0):
            w_at[b] = rw_.at
            rw_.at += 6144

        def pieces(t, at):
            return [t[:, at + 2048 * k:at + 2048 * k + 2048] for k in range(3)]

        w_raw = [pieces(ringf, w_at[b]) for b in range(2)]
        w_lo = [pieces(ringp[:].rearrange("p s n -> p (s n)"), w_at[b]) for b in range(2)]
        w_hi = [pieces(arenap, 6144 * b) for b in range(2)]
        re.at = 12288
        nfin = re.take(D)
        rx = Region(arena, 14336, 18432)
        xg = [rx.take(D) for _ in range(2)]
        ys = [rx.take(D) for _ in range(2)]
        xe_hi, xe_lo = ([t[:].rearrange("p a b -> p (a b)")[:, D * b:D * b + D]
                         for b in range(2)] for t in (oTp[0], oTp[2]))
        ro = Region(oT[1][:].rearrange("p a b -> p (a b)"), 0, 2048)
        sge = [ro.take(FF) for _ in range(2)]
        acte = [ro.take(FF) for _ in range(2)]
        rp = Region(oTp[1][:].rearrange("p a b -> p (a b)"), ro.at, 2048)
        ae_hi = [rp.take(2, P, dt=F32R) for _ in range(2)]
        ae_lo = [rp.take(2, P, dt=F32R) for _ in range(2)]
        rr = Region(oT[2][:].rearrange("p a b -> p (a b)"), 0, 2048)
        score, selr, mall = rr.take(TT, E), rr.take(TT, E), rr.take(TT, E)
        onehot = rr.take(6, E)
        rt_tmp, rt_tmp2 = rr.take(E), rr.take(E)
        base, ntile, uend = rr.take(E), rr.take(E), rr.take(E)
        slotA = rr.take(E)
        rbias = sb("rbias", [P, E])
        gtop = sb("gtop", [P, 8, 8])
        gsc, gm8, gmask = sb("gsc", [P, 8]), sb("gm8", [P, 8]), sb("gmask", [P, 8])
        gidx, eidx = sb("gidx", [P, 8], U32), sb("eidx", [P, 8], U32)
        gidf, eidf = sb("gidf", [P, 8]), sb("eidf", [P, 8])
        wk = sb("wk", [P, TT, 8])
        wsum = sb("wsum", [P, 1])
        slotf, sloti = sb("slotf", [P, TT, 8]), sb("sloti", [P, TT, 8], I32)
        tokid = sb("tokid", [P, TT, TOPK, 2], I32)
        oob = sb("oob", [P, 2 * (UNITS + 4)], I32)
        ucolf = sb("ucolf", [E, 1])
        ucmp = sb("ucmp", [E, 96])
        uexp = sb("uexp", [1, 96], I32)
        npair = sb("npair", [1, 1], I32)
        npf = sb("npf", [1, 64])
        npg = sb("npg", [1, 1])
        iota_u = sb("iota_u", [E, 96])
        tok_of = [sb(f"tok_of{b}", [P, 2], I32) for b in range(2)]
        row_of = [sb(f"row_of{b}", [P, 2], I32) for b in range(2)]
        eall = sb("eall", [P, TT, 8])
        sgS = [oT[1][:, 2 + m, :] for m in range(2)]
        rs = Region(arena, 16384, 18432)
        actS, wtmp2 = rs.take(2, T), rs.take(T)
        yk = [arena[:, 6144 * b:6144 * b + 6144].rearrange("p (k n) -> p k n", k=TOPK) for b in range(2)]
        routed = hT[:, 0:2, :].rearrange("p a b -> p (a b)")

        h_dram = nc.dram_tensor("h_dram", [T, D], F32).ap()
        y_dram = nc.dram_tensor("y_dram", [T * TOPK, D], F32).ap()
        list_dram = nc.dram_tensor("list_dram", [(UNITS + 4) * P, 2], I32).ap()

        w_in = a["w_in"][0].rearrange("(j p) n -> p j n", p=P)
        ada = a["ada_w"][0].rearrange("(p j) n -> p j n", j=8)
        loads = []

        def slot_view(n, off, *shape):
            v = ring[:, n % RING, off:off + int(np.prod(shape))]
            return v.rearrange("p (a b) -> p a b", a=shape[0])

        def load(name, parts, last):
            n = len(loads)
            loads.append((name, [(slot_view(n, off, *shape), src) for off, shape, src in parts], last))

        def cols(name, off=0, n=512):
            c = COL[name] + off
            return w_in[:, :, c:c + n]

        for c in range(4):
            load(f"ada{c}", [(0, (8, 512), ada[:, :, 512 * c:512 * c + 512])], f"mc{c}")
        load("w_qk", [(0, (8, 512), cols("qa"))], "ka1")
        load("w_va", [(0, (8, 512), cols("va"))], "va3")
        load("w_ga", [(0, (8, 512), cols("ga"))], "ga3")
        load("w_qkc", [(0, (8, 512), cols("qc"))], "qk3")
        load("w_vc", [(0, (8, 512), cols("vc"))], "vc3")
        load("w_oc", [(0, (8, 512), cols("oc"))], "oc3")
        load("w_cl", [(0, (8, 384), cols("cq", 0, 384))], "cl2")
        ups = [a[n][0].rearrange("(j p) n -> p j n", p=P) for n in ("w_up_a", "w_up_b", "w_up_c")]
        for m in range(0, 8, 2):
            for b in range(3):
                load(f"wm{m}{b}", [(0, (8, 256), cols("gates", D * b + P * m, 256)),
                                   (2048, (4, 256), ups[b][:, :, P * m:P * m + 256])], f"up{m + 1}{b}")
                c = 3 * m // 2 + b
                if c < 8:
                    load(f"adr{c}", [(0, (8, 512), ada[:, :, 2048 + 512 * c:2560 + 512 * c])], f"mb{c}")
        wo_d = a["w_o"][0].rearrange("(j p) n -> p j n", p=P)
        for n in range(2):
            load(f"wo{n}", [(0, (8, 512), wo_d[:, :, 512 * n:512 * n + 512])], f"wo3{n}")
        load("w_sh", [(0, (8, 256), a["sh_w_gate"][0].rearrange("(p j) f -> p j f", j=8)),
                      (2048, (8, 256), a["sh_w_up"][0].rearrange("(p j) f -> p j f", j=8))], "su1")
        load("w_shd", [(0, (2, D), a["sh_w_down"][0].rearrange("(p m) n -> p m n", m=2)),
                       (2048, (8, E), a["router_w"][0].rearrange("(p j) e -> p j e", j=8))], "sd31")
        load_at = {name: n for n, (name, _, _) in enumerate(loads)}
        landed = {}
        count = [0] * RING
        for n, (name, parts, _) in enumerate(loads):
            count[n % RING] += 16 * len(parts)
            landed[name] = (n % RING, count[n % RING])

        def loaded(eng, name):
            s, v = landed[name]
            eng.wait_ge(sem(f"ring_loaded{s}"), v)

        def ring_view(name, off, *shape):
            return slot_view(load_at[name], off, *shape)

        def done(eng, name):
            n = number[name]
            eng.wait_ge(sem("products_done"), n + 1)
            return bank[n % BANKS]

        wsm = r0.take(8, P)
        cond = [r0.take(T), r0.take(T), *cond_merge]
        cond = [cond[c % 2 + (2 if c >= 4 else 0)] for c in range(12)]
        wki = sb("wki", [P, 8, 32])
        GAPS = {"a_lr": 0, "w_idx": 32, "ic": 64, "fc": 96}

        for n in ("consts", "consts_loaded", "products_done", "dve_chain", "act_chain", "pool_chain",
                  *[f"ring_loaded{i}" for i in range(RING)], *sorted({s for _, s, _ in products})):
            sem(n)

        block = ctx.enter_context(nc.Block())
        NCONST = [0]

        @block.sync
        def _(sp):
            def const(dst, src):
                sp.dma_start(dst, src).then_inc(sem("consts_loaded"), 16)
                NCONST[0] += 16

            for name, n in (("piece_used", 6), ("turned", 1), ("y_read", 4)):
                sp.sem_inc(sem(name), n)

            def rows(v, n):
                return v.rearrange("(r p) -> r p", p=P)[0:n]

            const(c_in[:, :], a["c"].rearrange("o (p j) -> (o p) j", j=8))
            sp.dma_start(x[:, :, :], a["x"][0].rearrange("(i p) d -> p i d", p=P)).then_inc(sem("x_loaded"), 16)
            const(prow[0:8, :], rows(a["norm_mix"][0], 8))
            const(prow[8:24, :], rows(a["ada_b"][0], 16))
            const(prow[24:26, :], rows(a["gla_b_a"][0], 2))
            const(prow[26:30, :], rows(a["gla_norm"][0], 4))
            const(prow[30:32, :], rows(a["dsa_norm_q"][0], 2))
            const(prow[32:33, :], rows(a["dsa_norm_kv"][0], 1))
            const(prow[33:37, :], rows(a["mlstm_norm"][0], 4))
            const(prow[37:53, :], a["mlstm_conv"][0].rearrange("k (r p) -> (k r) p", p=P))
            const(w_a2[:, :], a["gla_w_a2"][0])
            with nc.allow_non_contiguous_dma(reason="eight numbers"):
                const(bif[:, 0:1], a["mlstm_b_i"].rearrange("o h -> h o"))
                const(bif[:, 1:2], a["mlstm_b_f"].rearrange("o h -> h o"))
            sp.wait_ge(sem("small_cleared"), 1)
            for name, g in GAPS.items():
                const(wsm[:, :, g:g + IN_SIZES[name]], w_in[:, :, COL[name]:COL[name] + IN_SIZES[name]])
            const(wki[:, :, :], w_in[:, :, COL["k_idx"]:COL["k_idx"] + 32])
            const(rbias[:, :], a["router_bias"].to_broadcast([P, E]))

            def ring_load(n):
                name, parts, last = loads[n]
                if n >= RING:
                    sp.wait_ge(sem("products_done"), number[loads[n - RING][2]] + 1)
                for dst, src in parts:
                    sp.dma_start(dst, src).then_inc(sem(f"ring_loaded{n % RING}"), 16)

            n = 0
            while n < len(loads):
                name = loads[n][0]
                if name == "w_cl":
                    sp.wait_ge(sem("oTC_ready"), 4)
                    sp.dma_start(w_uq, a["dsa_w_uq"][0].rearrange("(k p) h d -> p k (h d)", p=P)).then_inc(sem("extra_loaded"), 16)
                    sp.dma_start(w_uk, a["dsa_w_uk"][0].rearrange("c h d -> c (h d)")).then_inc(sem("extra_loaded"), 16)
                    sp.dma_start(w_uv, a["dsa_w_uv"][0].rearrange("c h d -> c (h d)")).then_inc(sem("extra_loaded"), 16)
                    sp.dma_start(w_qi, a["dsa_w_qi"][0].rearrange("(k p) h d -> p k (h d)", p=P)).then_inc(sem("extra_loaded"), 16)
                if name == "wm00":
                    sp.wait_ge(sem("oTB_ready"), 4)
                    sp.dma_start(adab, a["ada_b"][0:1, 2048:6144]).then_inc(sem("extra_loaded"), 16)
                    sp.dma_start(nffn, a["norm_ffn"].to_broadcast([P, D])).then_inc(sem("extra_loaded"), 16)
                ring_load(n)
                n += 1

            for i in range(TT):
                sp.wait_ge(sem("h2_ready"), i + 1)
                sp.dma_start(h_dram[P * i:P * i + P, :], h2[:, i, :]).then_inc(sem("h_stored"), 16)
            sp.wait_ge(sem("consts"), 1)
            sp.dma_start(list_dram.rearrange("(p u) o -> p (u o)", p=P), oob[:, :]).then_inc(sem("list_cleared"), 16)
            sp.wait_ge(sem("h_stored"), 16 * TT)
            sp.wait_ge(sem("h2T_ready"), 8)
            sp.dma_start(nfin, a["norm_final"].rearrange("(o d) -> o d", o=1).to_broadcast([P, D])).then_inc(sem("extra_loaded"), 16)

            sp.wait_ge(sem("table_ready"), 1)
            pairs = sp.value_load(npair[0:1, 0:1], min_val=1, max_val=UNITS // 2)
            sp.wait_ge(sem("list_stored"), 16 * TT * TOPK)

            def unit_list(u, b):
                sp.dma_start(tok_of[b][:, :], list_dram[bass.ds(u * P, P), :]).then_inc(sem(f"list_loaded{b}"), 16)

            def load_piece(e, b, k):
                if k < 2:
                    dst = w_raw[b][k].rearrange("p (g j f) -> p g j f", g=2, j=4)
                    for g, w in enumerate(("exp_w_gate", "exp_w_up")):
                        src = a[w][0][bass.ds(e, 1)].rearrange("e (p j) f -> (e p) j f", j=8)[:, 4 * k:4 * k + 4, :]
                        sp.dma_start(dst[:, g, :, :], src).then_inc(sem(f"w_loaded{b}{k}"), 16)
                else:
                    src = a["exp_w_down"][0][bass.ds(e, 1)].rearrange("e (p m) n -> (e p) m n", m=2)
                    sp.dma_start(w_raw[b][2].rearrange("p (m n) -> p m n", m=2), src).then_inc(sem(f"w_loaded{b}2"), 16)

            unit_list(0, 0)
            unit_list(1, 1)
            e = sp.value_load(uexp[0:1, 0:1], min_val=0, max_val=E - 1)
            for k in range(3):
                load_piece(e, 0, k)
            sp.wait_ge(sem("products_done"), len(products))
            with sp.Fori(0, pairs) as i:
                for b in range(2):
                    c, u = 1 - b, 2 * i + b
                    e = sp.value_load(uexp[0:1, bass.ds(u + 1, 1)], min_val=0, max_val=E - 1)
                    for k in range(3):
                        if k == 2:
                            sp.wait_ge(sem("turned"), 2 * u + 3)
                            unit_list(u + 2, b)
                        sp.wait_ge(sem("piece_used"), 3 * u + k + 4)
                        load_piece(e, c, k)
                    sp.wait_ge(sem(f"y_stored{b}"), 16 * i + 16)
                    sp.dma_start(row_of[b][:, :], list_dram[bass.ds(u * P, P), :]).then_inc(sem(f"rows_loaded{b}"), 16)

            for b in range(2):
                sp.wait_ge(sem(f"y_stored{b}"), 16 * pairs + 16)
            sp.wait_ge(sem("lo_ready"), 6 * pairs + 3)
            for i in range(TT):
                if i >= 2:
                    sp.wait_ge(sem("yk_used"), TOPK * (i - 1))
                sp.dma_start(yk[i % 2], y_dram[P * TOPK * i:P * TOPK * (i + 1), :].rearrange("(t k) n -> t k n", k=TOPK)
                             ).then_inc(sem(f"yk_loaded{i % 2}"), 16)
            for i in range(TT):
                sp.wait_ge(sem("out_ready"), i + 1)
                sp.dma_start(out[0, P * i:P * i + P, :], x[:, i, :]).then_inc(sem("out_stored"), 16)
            sp.wait_ge(sem("out_stored"), 16 * TT)

        @block.gpsimd
        def _(pool):
            g = nc.gpsimd
            chain = [0]

            def link(ins):
                chain[0] += 1
                ins.then_inc(sem("pool_chain"), 1)
                pool.wait_ge(sem("pool_chain"), chain[0])

            g.memset(wsm, 0.0).then_inc(sem("small_cleared"), 1)
            g.memset(epsc[:], EPS)
            link(g.memset(ident[:], 0.0))
            link(g.affine_select(out=ident[:], in_=ident[:], compare_op=ALU.not_equal, fill=1.0, base=0,
                                 pattern=[[-1, P]], channel_multiplier=1))
            link(g.memset(ones[:], 1.0))
            link(g.affine_select(out=causal[:], in_=ones[:], compare_op=ALU.is_ge, fill=0.0, base=0,
                                 pattern=[[1, P]], channel_multiplier=-1))
            link(g.affine_select(out=before[:], in_=ones[:], compare_op=ALU.is_gt, fill=0.0, base=0,
                                 pattern=[[1, P]], channel_multiplier=-1))
            link(g.memset(future[:], 1))
            link(g.affine_select(out=future[:], in_=future[:], compare_op=ALU.is_gt, fill=0.0, base=0,
                                 pattern=[[1, P]], channel_multiplier=-1))
            g.memset(negc[:], NEG_FUTURE)
            g.iota(iota_e[:], pattern=[[1, E]], base=0, channel_multiplier=0, allow_small_or_imprecise_dtypes=True)
            g.iota(iota_u[:], pattern=[[1, 96]], base=0, channel_multiplier=0, allow_small_or_imprecise_dtypes=True)
            g.iota(tokid[:, :, :, 0], pattern=[[P, TT], [0, TOPK]], base=0, channel_multiplier=1)
            g.iota(tokid[:, :, :, 1], pattern=[[P * TOPK, TT], [1, TOPK]], base=0, channel_multiplier=TOPK)
            g.memset(oob[:], T * TOPK)
            link(g.iota(level_mask[:, 0, :], pattern=[[1, P]], base=0, channel_multiplier=0))
            link(g.iota(level_mask[:, 1, :], pattern=[[0, P]], base=0, channel_multiplier=1))
            link(g.memset(resets, 1.0))
            link(g.memset(resets.rearrange("p (i t) -> p i t", i=TT)[:, :, 0:1], 0.0))
            g.memset(stat[:], 0.0).then_inc(sem("consts"), 1)

            pool.wait_ge(sem("hT_ready"), 8)
            pool.wait_ge(sem("small_ready"), 1)
            for t in (qE[0], qE[1], kE[0], kE[1], qcz[0], qcz[1], S):
                ins = g.memset(t, 0.0)
            ins.then_inc(sem("cleared"), 1)

            pool.wait_ge(sem("oTA_ready"), 4)
            g.memset(raw, 0.0)
            g.memset(ones4, 1.0)
            link(g.memset(sel4, 0.0))
            g.affine_select(out=sel4, in_=sel4, compare_op=ALU.not_equal, fill=1.0, base=0,
                            pattern=[[-1, 4], [0, P]], channel_multiplier=1).then_inc(sem("cleared"), 1)

            pool.wait_ge(sem("oTC_ready"), 4)
            g.iota(distv, pattern=[[1, 896]], base=-384, channel_multiplier=-1,
                   allow_small_or_imprecise_dtypes=True)
            g.memset(Dm, NEG_MASK).then_inc(sem("cleared"), 1)

            pool.wait_ge(sem("list_cleared"), 16)
            pool.wait_ge(sem("slots_ready"), TT)
            for i in range(TT):
                for k in range(TOPK):
                    g.indirect_dma_start(out=list_dram[:, :], out_offset=bass.IndirectOffsetOnAxis(ap=sloti[:, i, k:k + 1], axis=0),
                                         in_=tokid[:, i, k, :], in_offset=None).then_inc(sem("list_stored"), 16)
            pool.wait_ge(sem("x2_ready"), 4)
            pool.wait_ge(sem("products_done"), number["wo31"] + 1)
            for b in range(2):
                g.memset(row_of[b][:, :], T * TOPK)
                ins = g.memset(xg[b], 0.0)
            link(ins)
            pool.wait_ge(sem("h_stored"), 16 * TT)
            pool.wait_ge(sem("table_ready"), 1)
            pairs = pool.value_load(npair[0:1, 0:1], min_val=1, max_val=UNITS // 2)

            def gather(b):
                pool.sem_inc(sem("gathers_begun"), 1)
                g.indirect_dma_start(out=xg[b], out_offset=None, in_=h_dram[:, :],
                                     in_offset=bass.IndirectOffsetOnAxis(ap=tok_of[b][:, 0:1], axis=0),
                                     bounds_check=T - 1, oob_is_err=False).then_inc(sem(f"xg_loaded{b}"), 16)

            for b in range(2):
                g.indirect_dma_start(out=y_dram[:, :], out_offset=bass.IndirectOffsetOnAxis(ap=row_of[b][:, 1:2], axis=0),
                                     in_=xg[b], in_offset=None, bounds_check=T * TOPK - 1, oob_is_err=False
                                     ).then_inc(sem(f"y_stored{b}"), 16)
            for b in range(2):
                pool.wait_ge(sem(f"list_loaded{b}"), 16)
                gather(b)
            with pool.Fori(0, pairs) as i:
                for b in range(2):
                    pool.wait_ge(sem(f"list_loaded{b}"), 16 * i + 32)
                    pool.wait_ge(sem("turned"), 4 * i + 2 * b + 3)
                    gather(b)
                    pool.wait_ge(sem(f"rows_loaded{b}"), 16 * i + 16)
                    pool.wait_ge(sem("y_read"), 4 * i + 2 * b + 6)
                    pool.sem_inc(sem("gathers_begun"), 1)
                    g.indirect_dma_start(out=y_dram[:, :], out_offset=bass.IndirectOffsetOnAxis(ap=row_of[b][:, 1:2], axis=0),
                                         in_=ys[b], in_offset=None, bounds_check=T * TOPK - 1, oob_is_err=False
                                         ).then_inc(sem(f"y_stored{b}"), 16)

        @block.tensor
        def _(pe):
            mm = nc.tensor.matmul
            nxt = [0]

            def begin(name):
                n = nxt[0]
                assert products[n][0] == name, (products[n][0], name)
                nxt[0] += 1
                if n >= BANKS:
                    _, s, v = products[n - BANKS]
                    pe.wait_ge(sem(s), v)
                return bank[n % BANKS]

            def end(ins):
                ins.then_inc(sem("products_done"), 1)

            pe.wait_ge(sem("consts"), 1)
            pe.wait_ge(sem("consts_loaded"), NCONST[0])
            b = begin("params")
            end(nc.tensor.transpose(b[:, 0:53], prow[0:53, :], ident[0:53, 0:53]))
            for c in range(4):
                b = begin(f"mc{c}")
                pe.wait_ge(sem("cond_ready"), c + 1)
                for m in range(4):
                    ins = mm(b[:, m:m + 1], cond[c][:, tile_cols(m)], ones[:, 0:1], start=True, stop=True)
                end(ins)
            for j in range(8):
                pe.wait_ge(sem("xn_ready"), TT)
                b = begin(f"xT{j}")
                for i in range(TT):
                    ins = nc.tensor.transpose(b[:, tile_cols(i)], xn[:, i, tile_cols(j)], ident[:, :])
                end(ins)

            def project(name, w, m):
                b = begin(name)
                for j in range(8):
                    pe.wait_ge(sem("hT_ready"), j + 1)
                    ins = mm(b[:, :], w[:, j, tile_cols(m)], hT[:, j, :], start=(j == 0), stop=(j == 7))
                end(ins)

            def project_rows(name, w, i):
                b = begin(name)
                for j in range(8):
                    ins = mm(b[:, :], hT[:, j, tile_cols(i)], w[:, j, :], start=(j == 0), stop=(j == 7))
                end(ins)

            project("small", wsm, 0)
            pe.wait_ge(sem("small_ready"), 1)
            for f in range(2):
                b = begin(f"la{f}")
                end(mm(b[:, :], w_a2[:, tile_cols(f)], small[0:16, :], start=True, stop=True))
            loaded(pe, "w_qk")
            w = ring_view("w_qk", 0, 8, 512)
            for f in range(2):
                project(f"qa{f}", w, f)
            for f in range(2):
                project(f"ka{f}", w, 2 + f)
            loaded(pe, "w_va")
            w = ring_view("w_va", 0, 8, 512)
            for i in range(TT):
                project_rows(f"va{i}", w, i)
            pe.wait_ge(sem("kd_ready"), 1)
            kd = decay
            for f in range(2):
                b = begin(f"kd{f}")
                for i in range(TT):
                    ins = nc.tensor.transpose(b[:, tile_cols(i)], kd[:, f, tile_cols(i)], ident[:, :])
                end(ins)
            pe.wait_ge(sem("kdr_ready"), 2)
            pe.wait_ge(sem("v_ready"), 4)
            for i in range(3):
                for f in range(2):
                    b = begin(f"st{i}{f}")
                    end(mm(b[:, 0:256], kdr[:, i, f, :], va[:, i, 256 * f:256 * f + 256], start=True, stop=True))
            for l in range(8):
                if l < 7:
                    pe.wait_ge(sem("level_ready"), l + 1)
                    ksrc, qsrc = kE[l % 2], qE[l % 2]
                else:
                    ksrc, qsrc = kT, qT
                for g in range(4):
                    p0, tp = 64 * (g // 2), g % 2
                    b = begin(f"scA{l}{g}")
                    for ii in range(2):
                        for f in range(2):
                            t = tile_cols(2 * tp + ii)
                            ins = mm(b[:, tile_cols(2 * ii + f)], ksrc[p0:p0 + 64, f, t], qsrc[p0:p0 + 64, f, t],
                                     start=True, stop=True)
                    end(ins)
            loaded(pe, "w_ga")
            w = ring_view("w_ga", 0, 8, 512)
            for m in range(4):
                project(f"ga{m}", w, m)
            pe.wait_ge(sem("state_ready"), 6)
            pe.wait_ge(sem("intra_done"), 32)
            for h in range(5):
                if h < 4:
                    b = begin(f"oA{h}")
                    for i in range(TT):
                        if i:
                            mm(b[:, tile_cols(i)], state[:, i - 1, h // 2, :], qcz[h % 2][:, h // 2, tile_cols(i)],
                               start=True, stop=False)
                        ins = mm(b[:, tile_cols(i)], va[:, i, tile_cols(h)], S[:, h % 2, i, h // 2, :],
                                 start=(i == 0), stop=True)
                    end(ins)
                if h:
                    pe.wait_ge(sem("squares_ready"), h)
                    b = begin(f"msA{h - 1}")
                    end(mm(b[:, :], ones[:, :], sqA, start=True, stop=True))

            loaded(pe, "w_qkc")
            w = ring_view("w_qkc", 0, 8, 512)
            for f in range(4):
                project(f"qk{f}", w, f)
            pe.wait_ge(sem("scans_ready"), 1)
            b = begin("uT")
            for i in range(TT):
                ins = nc.tensor.transpose(b[:, 4 * i:4 * i + 4], g4[3][:, tile_cols(i)], ident[0:4, 0:4])
            end(ins)
            loaded(pe, "w_vc")
            w = ring_view("w_vc", 0, 8, 512)
            for i in range(TT):
                project_rows(f"vc{i}", w, i)
            loaded(pe, "w_oc")
            w = ring_view("w_oc", 0, 8, 512)
            for m in range(4):
                project(f"oc{m}", w, m)
            pe.wait_ge(sem("cleared"), 2)
            pe.wait_ge(sem("qkc_ready"), 4)
            pe.wait_ge(sem("v_ready"), 8)
            for h in range(4):
                p0, f = 64 * (h % 2), h // 2
                b = begin(f"bm{h}")
                end(mm(b[:, :], sel4[:, h, :], g4[4], start=True, stop=True))
                b = begin(f"bt{h}")
                end(mm(b[:, :], sel4[:, h, :], g4[5], start=True, stop=True))
                for j in range(TT):
                    b = begin(f"scC{h}{j}")
                    end(mm(b[:, P * j:T], qkc[p0:p0 + 64, 2 + f, tile_cols(j)], qkc[p0:p0 + 64, f, P * j:T],
                           start=True, stop=True))
                b = begin(f"num{h}")
                for j in range(TT):
                    pe.wait_ge(sem("SW_ready"), 4 * h + j + 1)
                    ins = mm(b[:, P * j:T], vc[:, j, tile_cols(h)], SW[:, j, P * j:T], start=(j == 0), stop=(j == 3))
                end(ins)
                b = begin(f"den{h}")
                for j in range(TT):
                    ins = mm(b[:, P * j:T], ones[:, :], SW[:, j, P * j:T], start=(j == 0), stop=(j == 3))
                end(ins)
                pe.wait_ge(sem("squares_ready"), h + 5)
                b = begin(f"msC{h}")
                end(mm(b[:, :], ones[:, :], sqC, start=True, stop=True))

            pe.wait_ge(sem("wki4_ready"), 1)
            b = begin("kidx")
            for j in range(8):
                ins = mm(b[:, :], wki4[:, j, :, :].rearrange("p g d -> p (g d)"), hT[:, j, :],
                         start=(j == 0), stop=(j == 7))
            end(ins)
            loaded(pe, "w_cl")
            w = ring_view("w_cl", 0, 8, 384)
            for n in range(3):
                project(f"cl{n}", w, n)
            pe.wait_ge(sem("squares_ready"), 11)
            b = begin("msq")
            for k in range(2):
                ins = mm(b[:, :], ones[:, :], sqB[:, k, :], start=(k == 0), stop=(k == 1))
            end(ins)
            b = begin("mskv")
            end(mm(b[:, :], ones[:, :], sqB[:, 2, :], start=True, stop=True))
            pe.wait_ge(sem("wi0_ready"), 1)
            b = begin("wi")
            for i in range(TT):
                ins = nc.tensor.transpose(b[:, 8 * i:8 * i + 8], wi0[:, tile_cols(i)], ident[0:8, 0:8])
            end(ins)
            pe.wait_ge(sem("extra_loaded"), 64)
            b = begin("uk")
            for m in range(4):
                ins = nc.tensor.transpose(b[:, tile_cols(m)], w_uk[:, tile_cols(m)], ident[:, :])
            end(ins)
            pe.wait_ge(sem("cn_ready"), 2)
            b = begin("ckr")
            for i in range(TT):
                ins = nc.tensor.transpose(b[:, tile_cols(i)], cn[:, 2, tile_cols(i)], ident[:, :])
            end(ins)
            for m in range(2):
                b = begin(f"qi{m}")
                for k in range(2):
                    ins = mm(b[:, :], w_qi[:, k, tile_cols(m)], cn[:, k, :], start=(k == 0), stop=(k == 1))
                end(ins)
            pe.wait_ge(sem("qi_ready"), 2)
            pe.wait_ge(sem("kidx_ready"), 1)
            for i in range(1, TT):
                for h in range(8):
                    p0 = 32 * (h % 4)
                    b = begin(f"ix{i}{h}")
                    end(mm(b[:, 0:P * (i + 1)], qiT[p0:p0 + 32, h // 4, tile_cols(i)],
                           kidxT[p0:p0 + 32, 0:P * (i + 1)], start=True, stop=True))
            for m in range(4):
                b = begin(f"q{m}")
                for k in range(2):
                    ins = mm(b[:, :], w_uq[:, k, tile_cols(m)], cn[:, k, :], start=(k == 0), stop=(k == 1))
                end(ins)
            pe.wait_ge(sem("ukT_ready"), 1)
            for h in range(8):
                p0 = 64 * (h % 2)
                pe.wait_ge(sem("q_ready"), h // 2 + 1)
                b = begin(f"ql{h}")
                end(mm(b[:, :], ukT[p0:p0 + 64, h // 2, :], qTb[p0:p0 + 64, h // 2, :], start=True, stop=True))
            npt = 0
            for i in range(TT):
                for h in range(8):
                    pe.wait_ge(sem("ql_ready"), h + 1)
                    b = begin(f"lg{i}{h}")
                    end(mm(b[:, 0:P * (i + 1)], qlT[:, h, tile_cols(i)], cn[:, 2, 0:P * (i + 1)],
                           start=True, stop=True))
                for g in range(2):
                    pe.wait_ge(sem("P_ready"), 8 * i + 4 * g + 4)
                    for j in range(i + 1):
                        b = begin(f"pt{i}{g}{j}")
                        for h in range(4):
                            ins = nc.tensor.transpose(b[:, tile_cols(h)], Pn[:, 4 * g + h, tile_cols(j)], ident[:, :])
                        end(ins)
                    b = begin(f"ol{i}{g}")
                    for j in range(i + 1):
                        npt += 1
                        pe.wait_ge(sem("PT_ready"), npt)
                        ins = mm(b[:, :], ckr[:, j, :], PT[:, j, :], start=(j == 0), stop=(j == i))
                    end(ins)
            pe.wait_ge(sem("ol_ready"), 8)
            for m in range(4):
                b = begin(f"ob{m}")
                for q in range(2):
                    h = 2 * m + q
                    ins = mm(b[64 * q:64 * q + 64, :], w_uv[:, 64 * h:64 * h + 64], olT[:, h, :], start=True, stop=True)
                end(ins)

            for n, (m, br) in enumerate(merge_steps()):
                name = f"wm{m - m % 2}{br}"
                loaded(pe, name)
                wg, wu = ring_view(name, 0, 8, 256), ring_view(name, 2048, 4, 256)
                project(f"gate{m}{br}", wg, m % 2)
                b = begin(f"up{m}{br}")
                for j in range(4):
                    ins = mm(b[:, :], wu[:, j, tile_cols(m % 2)], oT[br][:, j, :], start=(j == 0), stop=(j == 3))
                end(ins)
                if n % 2 and n // 2 < 8:
                    c = n // 2
                    b = begin(f"mb{c}")
                    pe.wait_ge(sem("cond_ready"), 5 + c)
                    mm(b[:, :], ones[:, :], cond[4 + c], start=True, stop=False)
                    pe.wait_ge(sem("extra_loaded"), 96)
                    end(mm(b[:, :], ones[0:1, :], adab[:, 512 * c:512 * c + 512], start=False, stop=True))
            loaded(pe, "wo0")
            loaded(pe, "wo1")
            pe.wait_ge(sem("mT_ready"), 8)
            for i in range(TT):
                for n in range(2):
                    w = ring_view(f"wo{n}", 0, 8, 512)
                    b = begin(f"wo{i}{n}")
                    for j in range(8):
                        ins = mm(b[:, :], mT[:, j, tile_cols(i)], w[:, j, :], start=(j == 0), stop=(j == 7))
                    end(ins)

            pe.wait_ge(sem("h2_ready"), TT)
            for j in range(8):
                b = begin(f"hT2{j}")
                for i in range(TT):
                    src = h2[:, i, :].rearrange("t (p j) -> t j p", j=8)[:, j, :]
                    ins = nc.tensor.transpose(b[:, tile_cols(i)], src, ident[:, :])
                end(ins)
            loaded(pe, "w_shd")
            rw = ring_view("w_shd", 2048, 8, E)
            pe.wait_ge(sem("h2T_ready"), 8)
            for i in range(TT):
                b = begin(f"rt{i}")
                for j in range(8):
                    ins = mm(b[:, 0:E], hT[:, j, tile_cols(i)], rw[:, j, :], start=(j == 0), stop=(j == 7))
                end(ins)
            for i in range(TT):
                pe.wait_ge(sem("mall_ready"), TT)
                b = begin(f"pos{i}")
                for q in range(i + 1):
                    ins = mm(b[:, 0:E], before[:, :] if q == i else ones[:, :], mall[:, q, :],
                             start=(q == 0), stop=(q == i))
                end(ins)
            b = begin("tot")
            for q in range(TT):
                ins = mm(b[:, 0:E], ones[:, :], mall[:, q, :], start=(q == 0), stop=(q == TT - 1))
            end(ins)
            pe.wait_ge(sem("uend_ready"), 1)
            b = begin("ue")
            end(nc.tensor.transpose(b[0:E, 0:P], uend, ident[:, :]))
            pe.wait_ge(sem("ucmp_ready"), 1)
            b = begin("uc")
            end(mm(b[0:1, 0:96], ones[0:E, 0:1], ucmp[:, :], start=True, stop=True))
            loaded(pe, "w_sh")
            wg, wu = ring_view("w_sh", 0, 8, 256), ring_view("w_sh", 2048, 8, 256)
            for m in range(2):
                for name, w in ((f"sg{m}", wg), (f"su{m}", wu)):
                    b = begin(name)
                    for j in range(8):
                        ins = mm(b[:, :], w[:, j, :].rearrange("p (f m) -> p m f", m=2)[:, m, :], hT[:, j, :],
                                 start=(j == 0), stop=(j == 7))
                    end(ins)
            wd = ring_view("w_shd", 0, 2, D)
            pe.wait_ge(sem("actS_ready"), 2)
            for i in range(TT):
                for n in range(2):
                    b = begin(f"sd{i}{n}")
                    for m in range(2):
                        ins = mm(b[:, :], actS[:, m, tile_cols(i)], wd[:, m, 512 * n:512 * n + 512],
                                 start=(m == 0), stop=(m == 1))
                    end(ins)
            assert nxt[0] == len(products)

            for _, s, v in products[-BANKS:]:
                pe.wait_ge(sem(s), v)
            pe.wait_ge(sem("table_ready"), 1)
            pairs = pe.value_load(npair[0:1, 0:1], min_val=1, max_val=UNITS // 2)

            def turn(c, half):
                rows = xg[c].rearrange("t (p j) -> t j p", j=8)
                for q in range(4):
                    ins = nc.tensor.transpose(bank[half][:, tile_cols(q)], rows[:, 4 * half + q, :], ident[:, :])
                ins.then_inc(sem("turned"), 1)

            pe.wait_ge(sem("xg_loaded0"), 16)
            turn(0, 0)
            turn(0, 1)
            with pe.Fori(0, pairs) as i:
                for b in range(2):
                    c, u = 1 - b, 2 * i + b
                    out_gu = bank[2][:, :].rearrange("p (g f) -> p g f", g=2)
                    for k in range(2):
                        hi, lo = (w[b][k].rearrange("p (g j f) -> p g j f", g=2, j=4) for w in (w_hi, w_lo))
                        pe.wait_ge(sem("xe_hi_ready"), 2 * u + k + 1)
                        pe.wait_ge(sem("xe_lo_ready"), 2 * u + k + 1)
                        pe.wait_ge(sem("hi_ready"), 3 * u + k + 1)
                        for j in range(4):
                            for x_, t in enumerate((xe_hi, xe_lo)):
                                mm(out_gu, t[b][:, tile_cols(4 * k + j)], hi[:, :, j, :],
                                   start=(k == 0 and j == 0 and x_ == 0), stop=False)
                        pe.wait_ge(sem("lo_ready"), 3 * u + k + 1)
                        for j in range(4):
                            ins = mm(out_gu, xe_hi[b][:, tile_cols(4 * k + j)], lo[:, :, j, :], start=False,
                                     stop=(k == 1 and j == 3))
                        ins.then_inc(sem("piece_used"), 1)
                    pe.wait_ge(sem(f"xg_loaded{c}"), 16 * (i + b + 1))
                    turn(c, 0)
                    pe.wait_ge(sem("acte_ready"), u + 1)
                    rows = acte[b].rearrange("t (p m) -> t m p", m=2)
                    for m in range(2):
                        ins = nc.tensor.transpose(bank[3][:, tile_cols(m)], rows[:, m, :], ident[:, :])
                    ins.then_inc(sem("acte_turned"), 1)
                    turn(c, 1)
                    hi, lo = (w[b][2].rearrange("p (m n) -> p m n", m=2) for w in (w_hi, w_lo))
                    pe.wait_ge(sem("ae_hi_ready"), u + 1)
                    pe.wait_ge(sem("ae_lo_ready"), u + 1)
                    pe.wait_ge(sem("hi_ready"), 3 * u + 3)
                    pe.wait_ge(sem("lo_ready"), 3 * u + 3)
                    pe.wait_ge(sem("y_read"), 2 * u + 2)
                    for n in range(2):
                        terms = [(t[b][:, m, :], w[:, m, 512 * n:512 * n + 512]) for m in range(2)
                                 for t, w in ((ae_hi, hi), (ae_lo, hi), (ae_hi, lo))]
                        for q, (s_, w) in enumerate(terms):
                            ins = mm(bank[4 + 2 * b + n][:, :], s_, w, start=(q == 0), stop=(q == 5))
                        ins.then_inc(sem("piece_used" if n else "y_begun"), 1)

        @block.scalar
        def _(act):
            A = nc.scalar.activation
            chain = [0]

            def link(ins):
                chain[0] += 1
                ins.then_inc(sem("act_chain"), 1)
                act.wait_ge(sem("act_chain"), chain[0])

            act.wait_ge(sem("consts"), 1)
            act.wait_ge(sem("consts_loaded"), NCONST[0])
            A(cs[:, :], c_in[:, :], ACT.Silu).then_inc(sem("cs_ready"), 1)
            act.wait_ge(sem("x_loaded"), 16)
            for i in range(TT):
                link(A(junk, x[:, i, :], ACT.Square, accum_out=stat[:, i:i + 1]))
            A(stat[:, 4:8], stat[:, 0:4], ACT.Sqrt, scale=1.0 / D, bias=epsc[:, 0:1]).then_inc(sem("rms_ready"), 1)
            act.wait_ge(sem("mod1_ready"), 1)
            for j in range(8):
                b = done(act, f"xT{j}")
                A(hT[:, j, :], b[:, :], ACT.Identity, scale=mod1[:, j:j + 1], bias=mod1[:, 8 + j:9 + j]
                  ).then_inc(sem("hT_ready"), 1)
            b = done(act, "small")
            A(small[:, :], b[:, :], ACT.Copy).then_inc(sem("small_ready"), 1)
            for f in range(2):
                act.wait_ge(sem("z_ready"), f + 1)
                link(A(decay[:, f, :], arg[0][:, f, :], ACT.Abs))
                link(A(decay[:, f, :], decay[:, f, :], ACT.Exp, scale=-1.0))
                A(decay[:, f, :], decay[:, f, :], ACT.Ln, bias=1.0).then_inc(sem("lnz_ready"), 1)
            for f in range(2):
                b = done(act, f"qa{f}")
                A(qT[:, f, :], b[:, :], ACT.Copy, scale=0.125).then_inc(sem("qa_ready"), 1)
            act.wait_ge(sem("cum_ready"), 1)
            A(ecum, cum, ACT.Exp).then_inc(sem("ecum_ready"), 1)
            act.wait_ge(sem("kdarg_ready"), 1)
            A(decay, arg[0], ACT.Exp).then_inc(sem("kdE_ready"), 1)
            for f in range(2):
                b = done(act, f"kd{f}")
                A(kdr[:, :, f, :], b[:, :].rearrange("p (i k) -> p i k", i=TT), ACT.Copy).then_inc(sem("kdr_ready"), 1)
            for l in range(7):
                act.wait_ge(sem("arg_ready"), l + 1)
                if l:
                    act.wait_ge(sem("level_ready"), l)
                else:
                    act.wait_ge(sem("products_done"), number["kd1"] + 1)
                A(decay, arg[l % 2], ACT.Exp).then_inc(sem("E_ready"), 1)
            for m in range(4):
                b = done(act, f"ga{m}")
                A(sga[:, m, :], b[:, :], ACT.Silu).then_inc(sem("outgate_ready"), 1)
            for h in range(5):
                if h < 4:
                    b = done(act, f"oA{h}")
                    if h:
                        b1 = done(act, f"msA{h - 1}")
                        if h == 3:
                            act.wait_ge(sem("oA_read"), 1)
                        A(rsA[(h - 1) % 2], b1[:, :], ACT.Sqrt, scale=1.0 / P,
                          bias=epsc[:, 0:1]).then_inc(sem("root_ready"), 1)
                    A(sqA, b[:, :], ACT.Square).then_inc(sem("squares_ready"), 1)
                else:
                    b = done(act, "msA3")
                    act.wait_ge(sem("oA_read"), 2)
                    A(rsA[1], b[:, :], ACT.Sqrt, scale=1.0 / P, bias=epsc[:, 0:1]).then_inc(sem("root_ready"), 1)

            act.wait_ge(sem("oTA_ready"), 4)
            act.wait_ge(sem("fb_ready"), 1)
            link(A(g4[1], g4[0], ACT.Abs))
            link(A(g4[1], g4[1], ACT.Exp, scale=-1.0))
            A(g4[1], g4[1], ACT.Ln, bias=1.0).then_inc(sem("lnf_ready"), 1)
            for f in range(4):
                act.wait_ge(sem("conv_ready"), f + 1)
                A(qkc[:, f, :], qkc[:, f, :], ACT.Silu).then_inc(sem("qkc_ready"), 1)
            for m in range(4):
                b = done(act, f"oc{m}")
                A(soc[:, m, :], b[:, :], ACT.Sigmoid).then_inc(sem("outgate_ready"), 1)
            for h in range(4):
                b = done(act, f"bt{h}")
                if h:
                    act.wait_ge(sem("den_read"), h)
                A(floor_, b[:, :], ACT.Exp, scale=-1.0).then_inc(sem("floor_ready"), 1)
                for j in range(TT):
                    n = 4 * h + j
                    act.wait_ge(sem("argC_ready"), n + 1)
                    if n >= 2:
                        act.wait_ge(sem("SW_ready"), n - 1)
                    A(W[n % 2][:, 0:T - P * j], argC[n % 2][:, 0:T - P * j], ACT.Exp, scale=-1.0).then_inc(sem("W_ready"), 1)
                act.wait_ge(sem("hC_ready"), h + 1)
                if h:
                    act.wait_ge(sem("products_done"), number[f"msC{h - 1}"] + 1)
                A(sqC, hC, ACT.Square).then_inc(sem("squares_ready"), 1)
                b = done(act, f"msC{h}")
                A(rsC, b[:, :], ACT.Sqrt, scale=1.0 / P, bias=epsc[:, 0:1]).then_inc(sem("root_ready"), 1)

            act.wait_ge(sem("oTC_ready"), 4)
            b = done(act, "kidx")
            A(kidxT, b[:, :], ACT.Copy).then_inc(sem("kidx_ready"), 1)
            for n in range(3):
                act.wait_ge(sem("craw_ready"), n + 1)
                A(sqB[:, n, :], craw[:, n, :], ACT.Square).then_inc(sem("squares_ready"), 1)
            for n, name in enumerate(("msq", "mskv")):
                b = done(act, name)
                A(rsB[:, n, :], b[:, :], ACT.Sqrt, scale=1.0 / (256, 128)[n], bias=epsc[:, 0:1]).then_inc(sem("root_ready"), 1)
            b = done(act, "ckr")
            A(ckr, b[:, :].rearrange("p (i k) -> p i k", i=TT), ACT.Copy).then_inc(sem("ckr_ready"), 1)
            for m in range(2):
                b = done(act, f"qi{m}")
                A(qiT[:, m, :], b[:, :], ACT.Copy, scale=float(32 ** -0.5)).then_inc(sem("qi_ready"), 1)
            for i in range(1, TT):
                for h in range(8):
                    n = 8 * (i - 1) + h
                    b = done(act, f"ix{i}{h}")
                    if n >= 2:
                        act.wait_ge(sem("relu_used"), n - 1)
                    A(rl[n % 2][:, 0:P * (i + 1)], b[:, 0:P * (i + 1)], ACT.Relu).then_inc(sem("relu_ready"), 1)
            for m in range(4):
                b = done(act, f"q{m}")
                if m == 0:
                    act.wait_ge(sem("D_ready"), 4)
                A(qTb[:, m, :], b[:, :], ACT.Copy).then_inc(sem("q_ready"), 1)
            for h in range(8):
                b = done(act, f"ql{h}")
                A(qlT[:, h, :], b[:, :], ACT.Copy, scale=0.125).then_inc(sem("ql_ready"), 1)
            npt = 0
            for i in range(TT):
                for h in range(8):
                    n = 8 * i + h
                    act.wait_ge(sem("nmax_ready"), n + 1)
                    if i:
                        act.wait_ge(sem("products_done"), number[f"pt{i - 1}{h // 4}{i - 1}"] + 1)
                    A(Pn[:, h, 0:P * (i + 1)], L[n % 2][:, 0:P * (i + 1)], ACT.Exp, bias=nmax[:, n % 2:n % 2 + 1],
                      accum_out=nmax[:, 2 + n % 2:3 + n % 2]).then_inc(sem("exp_ready"), 1)
                for g in range(2):
                    for j in range(i + 1):
                        b = done(act, f"pt{i}{g}{j}")
                        if i or g:
                            act.wait_ge(sem("products_done"), number[f"ol{i - (g == 0)}{1 - g}"] + 1)
                        A(PT[:, j, :], b[:, :], ACT.Copy).then_inc(sem("PT_ready"), 1)
            for m in range(4):
                b = done(act, f"ob{m}")
                A(oT[1][:, m, :], b[:, :], ACT.Copy).then_inc(sem("oTB_ready"), 1)

            for n, (m, br) in enumerate(merge_steps()):
                b = done(act, f"gate{m}{br}")
                if n >= 2:
                    act.wait_ge(sem("up_read"), n - 1)
                A(sgate[n % 2], b[:, :], ACT.Sigmoid).then_inc(sem("gate_ready"), 1)
            for i in range(TT):
                act.wait_ge(sem("x2_ready"), i + 1)
                link(A(sqx, x[:, i, :], ACT.Square, accum_out=stat[:, 8 + i:9 + i]))
                A(stat[:, 12 + i:13 + i], stat[:, 8 + i:9 + i], ACT.Sqrt, scale=1.0 / D, bias=epsc[:, 0:1]).then_inc(sem("rms_ready"), 1)
            for j in range(8):
                b = done(act, f"hT2{j}")
                A(hT[:, j, :], b[:, :], ACT.Copy).then_inc(sem("h2T_ready"), 1)
            for i in range(TT):
                b = done(act, f"rt{i}")
                A(score[:, i, :], b[:, 0:E], ACT.Sigmoid).then_inc(sem("rt_ready"), 1)
            for m in range(2):
                b = done(act, f"sg{m}")
                A(sgS[m], b[:, :], ACT.Silu).then_inc(sem("sg_ready"), 1)

            act.wait_ge(sem("table_ready"), 1)
            act.wait_ge(sem("x_added"), 8)
            pairs = act.value_load(npair[0:1, 0:1], min_val=1, max_val=UNITS // 2)

            def weights_hi(v, c, k):
                act.wait_ge(sem(f"w_loaded{c}{k}"), v)
                A(w_hi[c][k], w_raw[c][k], ACT.Copy).then_inc(sem("hi_ready"), 1)

            def turned(u, c, half):
                act.wait_ge(sem("turned"), 2 * u + half + 4)
                A(xe_hi[c][:, 512 * half:512 * half + 512], bank[half][:, :], ACT.Copy).then_inc(sem("xe_hi_ready"), 1)

            for half in range(2):
                turned(-1, 0, half)
            for k in range(3):
                weights_hi(32 if k < 2 else 16, 0, k)
            with act.Fori(0, pairs) as i:
                for b in range(2):
                    c, u = 1 - b, 2 * i + b
                    for k in range(2):
                        weights_hi(32 * (i + b) + 32, c, k)
                    act.wait_ge(sem("piece_used"), 3 * u + 8)
                    A(sge[b], bank[2][:, 0:FF], ACT.Silu).then_inc(sem("sge_ready"), 1)
                    turned(u, c, 0)
                    act.wait_ge(sem("acte_turned"), u + 1)
                    A(ae_hi[b], bank[3][:, 0:FF].rearrange("p (m t) -> p m t", m=2), ACT.Copy
                      ).then_inc(sem("ae_hi_ready"), 1)
                    turned(u, c, 1)
                    weights_hi(16 * (i + b) + 16, c, 2)
                    act.wait_ge(sem(f"y_stored{b}"), 16 * i + 16)
                    for n in range(2):
                        if n:
                            act.wait_ge(sem("piece_used"), 3 * u + 9)
                        else:
                            act.wait_ge(sem("y_begun"), u + 1)
                        A(ys[b][:, 512 * n:512 * n + 512], bank[4 + 2 * b + n][:, :], ACT.Copy).then_inc(sem("y_read"), 1)
            for i in range(TT):
                act.wait_ge(sem("x4_ready"), i + 1)
                link(A(ring[:, 0, 0:D], x[:, i, :], ACT.Square, accum_out=stat[:, i:i + 1]))
                A(stat[:, 4 + i:5 + i], stat[:, i:i + 1], ACT.Sqrt, scale=1.0 / D, bias=epsc[:, 0:1]).then_inc(sem("rms_ready"), 1)

        @block.vector
        def _(dve):
            v = nc.vector
            chain = [0]

            def link(ins):
                chain[0] += 1
                ins.then_inc(sem("dve_chain"), 1)
                dve.wait_ge(sem("dve_chain"), chain[0])

            dve.wait_ge(sem("consts"), 1)
            link(v.tensor_tensor(level_mask[:, 7, :], level_mask[:, 0, :], level_mask[:, 1, :], ALU.bitwise_xor))
            b = level_mask[:, 0, :]
            link(v.tensor_copy(b, before[:, :]))
            link(v.memset(level_mask[:, 6, :], 1000))
            link(v.copy_predicated(level_mask[:, 6, :], b, level_mask[:, 7, :]))
            for l in range(6):
                v.tensor_scalar(level_mask[:, l, :], level_mask[:, 6, :], float(P >> l), None, ALU.is_lt)
            link(v.tensor_scalar(level_mask[:, 7, :], level_mask[:, 7, :], 0.0, None, ALU.is_equal))
            link(v.tensor_scalar(level_mask[:, 6, :], level_mask[:, 6, :], 2.0, None, ALU.is_lt))

            dve.wait_ge(sem("consts_loaded"), NCONST[0])
            b = done(dve, "params")
            v.tensor_copy(par[:, :], b[:, 0:53]).then_inc(sem("params_ready"), 1)
            dve.wait_ge(sem("params_ready"), 1)
            dve.wait_ge(sem("rms_ready"), 1)
            link(v.reciprocal(stat[:, 8:12], stat[:, 4:8]))
            for i in range(TT):
                v.tensor_scalar(xn[:, i, :], x[:, i, :], stat[:, 8 + i:9 + i], None, ALU.mult).then_inc(sem("xn_ready"), 1)
            def condition(c, name):
                loaded(dve, name)
                w = ring_view(name, 0, 8, 512)
                if c >= 2:
                    done(dve, f"mc{c - 2}" if c < 6 else f"mb{c - 6}")
                link(v.tensor_scalar(cond[c], w[:, 0, :], cs[:, 0:1], None, ALU.mult))
                for j in range(1, 8):
                    ins = v.scalar_tensor_tensor(out=cond[c], in0=w[:, j, :], scalar=cs[:, j:j + 1], in1=cond[c],
                                                 op0=ALU.mult, op1=ALU.add)
                    if j < 7:
                        link(ins)
                ins.then_inc(sem("cond_ready"), 1)

            dve.wait_ge(sem("cs_ready"), 1)
            for c in range(4):
                condition(c, f"ada{c}")
            for c in range(4):
                b = done(dve, f"mc{c}")
                d0 = (8, 12, 0, 4)[c]
                v.tensor_tensor(mod1[:, d0:d0 + 4], b[:, 0:4], par[:, 8 + 4 * c:12 + 4 * c], ALU.add
                                ).then_inc(sem("mc_ready"), 1)
            dve.wait_ge(sem("mc_ready"), 4)
            v.scalar_tensor_tensor(out=mod1[:, 0:8], in0=mod1[:, 0:8], scalar=1.0, in1=par[:, 0:8], op0=ALU.add,
                                   op1=ALU.mult).then_inc(sem("mod1_ready"), 1)

            dve.wait_ge(sem("small_ready"), 1)
            for f in range(2):
                b = done(dve, f"la{f}")
                v.tensor_scalar(arg[0][:, f, :], b[:, :], par[:, 24 + f:25 + f], None, ALU.add).then_inc(sem("z_ready"), 1)
            dve.wait_ge(sem("z_ready"), 2)
            for f in range(2):
                dve.wait_ge(sem("lnz_ready"), f + 1)
                link(v.scalar_tensor_tensor(out=arg[1][:, f, :], in0=arg[0][:, f, :], scalar=0.0, in1=decay[:, f, :],
                                            op0=ALU.min, op1=ALU.subtract))
                link(v.tensor_scalar(arg[1][:, f, :], arg[1][:, f, :], 1.0 / 16.0, None, ALU.mult))
                ins = v.tensor_tensor_scan(cum[:, f, :], resets, arg[1][:, f, :], 0.0, ALU.mult, ALU.add)
                if f == 0:
                    link(ins)
            ins.then_inc(sem("cum_ready"), 1)
            dve.wait_ge(sem("cum_ready"), 1)
            for f in range(2):
                b = done(dve, f"ka{f}")
                v.tensor_copy(kT[:, f, :], b[:, :]).then_inc(sem("ka_ready"), 1)
            c8 = cum.rearrange("p f (i t) -> p (f i) t", t=P)
            a8 = arg[0].rearrange("p f (i t) -> p (f i) t", t=P)
            v.tensor_tensor(a8, c8[:, :, P - 1:P].to_broadcast([P, 8, P]), c8, ALU.subtract).then_inc(sem("kdarg_ready"), 1)
            for i in range(TT):
                b = done(dve, f"va{i}")
                v.tensor_copy(va[:, i, :], b[:, :]).then_inc(sem("v_ready"), 1)
            dve.wait_ge(sem("cleared"), 1)
            dve.wait_ge(sem("ecum_ready"), 1)
            dve.wait_ge(sem("qa_ready"), 2)
            for p in range(2):
                r = slice(64 * p, 64 * p + 64)
                v.tensor_tensor(qcz[p][r], qT[r], ecum[r], ALU.mult)
            dve.wait_ge(sem("ka_ready"), 2)
            dve.wait_ge(sem("kdE_ready"), 1)
            v.tensor_tensor(decay, decay, kT, ALU.mult).then_inc(sem("kd_ready"), 1)

            def level_arg(l):
                h = (P // 2) >> l
                cv = cum.rearrange("p f t -> p (f t)").rearrange("p (n b) -> p n b", b=2 * h)
                av = arg[l % 2].rearrange("p f t -> p (f t)").rearrange("p (n b) -> p n b", b=2 * h)
                ref = cv[:, :, h - 1:h].to_broadcast([P, 1024 // (2 * h), h])
                if l == 0:
                    dve.wait_ge(sem("kdE_ready"), 1)
                v.tensor_tensor(av[:, :, 0:h], ref, cv[:, :, 0:h], ALU.subtract)
                v.tensor_tensor(av[:, :, h:2 * h], cv[:, :, h:2 * h], ref, ALU.subtract).then_inc(sem("arg_ready"), 1)

            def level_mul(l):
                h = (P // 2) >> l
                dve.wait_ge(sem("E_ready"), l + 1)
                if l >= 2:
                    dve.wait_ge(sem("products_done"), number[f"scA{l - 2}3"] + 1)

                def halves(t):
                    return t.rearrange("p f t -> p (f t)").rearrange("p (n b) -> p n b", b=2 * h)

                v.tensor_tensor(halves(kE[l % 2])[:, :, 0:h], halves(kT)[:, :, 0:h], halves(decay)[:, :, 0:h], ALU.mult)
                v.tensor_tensor(halves(qE[l % 2])[:, :, h:2 * h], halves(qT)[:, :, h:2 * h],
                                halves(decay)[:, :, h:2 * h], ALU.mult).then_inc(sem("level_ready"), 1)

            def level_merge(l):
                m = level_mask[:, l:l + 1, :].to_broadcast([P, 4, P])
                for g in range(4):
                    b = done(dve, f"scA{l}{g}")
                    if l:
                        dve.wait_ge(sem("intra_done"), 4 * (l - 1) + g + 1)
                    tp = g % 2
                    v.copy_predicated(S[:, g // 2, 2 * tp:2 * tp + 2, :, :].rearrange("p i f t -> p (i f) t"), m,
                                      b[:, :].rearrange("p (n t) -> p n t", t=P)).then_inc(sem("intra_done"), 1)

            level_arg(0)
            for i in range(3):
                for f in range(2):
                    b = done(dve, f"st{i}{f}")
                    for p in range(2):
                        r = slice(64 * p, 64 * p + 64)
                        if i == 0:
                            ins = v.tensor_copy(state[r, i, f, :], b[r, tile_cols(p)])
                        else:
                            ins = v.scalar_tensor_tensor(out=state[r, i, f, :], in0=state[r, i - 1, f, :],
                                                         scalar=ecum[r, f, P * i + P - 1:P * i + P],
                                                         in1=b[r, tile_cols(p)], op0=ALU.mult, op1=ALU.add)
                    ins.then_inc(sem("state_ready"), 1)
                dve.wait_ge(sem("state_ready"), 2 * i + 2)
            for l in range(7):
                level_mul(l)
                if l < 6:
                    level_arg(l + 1)
                if l:
                    level_merge(l - 1)
            level_merge(6)
            level_merge(7)
            dve.wait_ge(sem("outgate_ready"), 4)
            for h in range(4):
                dve.wait_ge(sem("root_ready"), h + 1)
                if h:
                    dve.wait_ge(sem("oTA_ready"), h)
                link(v.reciprocal(hA, rsA[h % 2]))
                b = done(dve, f"oA{h}")
                v.scalar_tensor_tensor(out=hA, in0=b[:, :], scalar=par[:, 26 + h:27 + h], in1=hA, op0=ALU.mult,
                                       op1=ALU.mult).then_inc(sem("oA_read"), 1)
                dve.wait_ge(sem("oA_read"), h + 1)
                v.tensor_tensor(oT[0][:, h, :], hA, sga[:, h, :], ALU.mult).then_inc(sem("oTA_ready"), 1)
            dve.wait_ge(sem("oTA_ready"), 4)

            fb, lnf, G, u, M, mt, ib, lf = g4
            link(v.tensor_copy(fb, small[96:100, :]))
            link(v.tensor_copy(ib, small[64:68, :]))
            v.tensor_scalar(fb, fb, bif[:, 1:2], None, ALU.add).then_inc(sem("fb_ready"), 1)
            dve.wait_ge(sem("fb_ready"), 1)
            link(v.tensor_scalar(ib, ib, bif[:, 0:1], None, ALU.add))
            dve.wait_ge(sem("cleared"), 2)
            dve.wait_ge(sem("lnf_ready"), 1)
            link(v.scalar_tensor_tensor(out=lf, in0=fb, scalar=0.0, in1=lnf, op0=ALU.min, op1=ALU.subtract))
            link(v.tensor_tensor_scan(G, ones4, lf, 0.0, ALU.mult, ALU.add))
            link(v.tensor_tensor(u, ib, G, ALU.subtract))
            link(v.tensor_tensor_scan(M, ones4, u, 0.0, ALU.mult, ALU.max))
            v.tensor_tensor(mt, G, M, ALU.add).then_inc(sem("scans_ready"), 1)
            for f in range(4):
                b = done(dve, f"qk{f}")
                v.tensor_copy(raw[:, f, 3:515], b[:, :]).then_inc(sem("qk_ready"), 1)
                dve.wait_ge(sem("qk_ready"), f + 1)
                link(v.tensor_scalar(qkc[:, f, :], raw[:, f, 0:512], par[:, 37 + f:38 + f], None, ALU.mult))
                for k in range(1, 4):
                    ins = v.scalar_tensor_tensor(out=qkc[:, f, :], in0=raw[:, f, k:k + 512],
                                                 scalar=par[:, 37 + 4 * k + f:38 + 4 * k + f], in1=qkc[:, f, :],
                                                 op0=ALU.mult, op1=ALU.add)
                    if k < 3:
                        link(ins)
                ins.then_inc(sem("conv_ready"), 1)
            b = done(dve, "uT")
            v.tensor_copy(ucol, b[:, 0:16].rearrange("p (i h) -> p i h", i=TT)).then_inc(sem("u_ready"), 1)
            for i in range(TT):
                b = done(dve, f"vc{i}")
                v.tensor_copy(vc[:, i, :], b[:, :]).then_inc(sem("v_ready"), 1)
            dve.wait_ge(sem("u_ready"), 1)
            for h in range(4):
                def arg_c(j):
                    n = 4 * h + j
                    bm = done(dve, f"bm{h}")
                    if n >= 2:
                        dve.wait_ge(sem("W_ready"), n - 1)
                    v.tensor_scalar(argC[n % 2][:, 0:T - P * j], bm[:, P * j:T], ucol[:, j, h:h + 1], 0.0,
                                    ALU.subtract, ALU.max).then_inc(sem("argC_ready"), 1)

                arg_c(0)
                if h:
                    dve.wait_ge(sem("products_done"), number[f"den{h - 1}"] + 1)
                for j in range(TT):
                    if j < 3:
                        arg_c(j + 1)
                    n = 4 * h + j
                    dve.wait_ge(sem("W_ready"), n + 1)
                    link(v.tensor_tensor(W[n % 2][:, 0:P], W[n % 2][:, 0:P], causal[:, :], ALU.mult))
                    b = done(dve, f"scC{h}{j}")
                    v.scalar_tensor_tensor(out=SW[:, j, P * j:T], in0=b[:, P * j:T], scalar=0.125,
                                           in1=W[n % 2][:, 0:T - P * j], op0=ALU.mult, op1=ALU.mult
                                           ).then_inc(sem("SW_ready"), 1)
                dve.wait_ge(sem("floor_ready"), h + 1)
                if h:
                    dve.wait_ge(sem("oTC_ready"), h)
                b = done(dve, f"den{h}")
                link(v.scalar_tensor_tensor(out=hD, in0=b[:, :], scalar=-1.0, in1=floor_, op0=ALU.mult, op1=ALU.max))
                v.tensor_tensor(hD, b[:, :], hD, ALU.max).then_inc(sem("den_read"), 1)
                dve.wait_ge(sem("den_read"), h + 1)
                link(v.reciprocal(hD, hD))
                b = done(dve, f"num{h}")
                v.tensor_tensor(hC, b[:, :], hD, ALU.mult).then_inc(sem("hC_ready"), 1)
                dve.wait_ge(sem("hC_ready"), h + 1)
                dve.wait_ge(sem("root_ready"), h + 5)
                link(v.reciprocal(hD, rsC))
                link(v.scalar_tensor_tensor(out=hD, in0=hC, scalar=par[:, 33 + h:34 + h], in1=hD, op0=ALU.mult,
                                            op1=ALU.mult))
                dve.wait_ge(sem("outgate_ready"), h + 5)
                v.tensor_tensor(oT[2][:, h, :], hD, soc[:, h, :], ALU.mult).then_inc(sem("oTC_ready"), 1)
            dve.wait_ge(sem("oTC_ready"), 4)

            v.tensor_copy(wki4, wki[:, :, :].rearrange("p j (o d) -> p j o d", o=1).to_broadcast([P, 8, 4, 32])
                          ).then_inc(sem("wki4_ready"), 1)
            v.tensor_copy(wi0[:, :], small[32:40, :]).then_inc(sem("wi0_ready"), 1)
            for n in range(3):
                b = done(dve, f"cl{n}")
                v.tensor_copy(craw[:, n, :], b[:, :]).then_inc(sem("craw_ready"), 1)
            b = done(dve, "wi")
            v.tensor_scalar(wcol[:, :, :], b[:, 0:32].rearrange("p (i h) -> p i h", i=TT), float(8 ** -0.5), None,
                            ALU.mult).then_inc(sem("wcol_ready"), 1)
            b = done(dve, "uk")
            v.tensor_copy(ukT, b[:, :].rearrange("p (i h) -> p i h", i=4)).then_inc(sem("ukT_ready"), 1)
            dve.wait_ge(sem("craw_ready"), 3)
            for n in range(2):
                dve.wait_ge(sem("root_ready"), n + 9)
                link(v.reciprocal(rsB[:, n, :], rsB[:, n, :]))
                for k in (0, 1) if n == 0 else (2,):
                    ins = v.scalar_tensor_tensor(out=cn[:, k, :], in0=craw[:, k, :], scalar=par[:, 30 + k:31 + k],
                                                 in1=rsB[:, n, :], op0=ALU.mult, op1=ALU.mult)
                ins.then_inc(sem("cn_ready"), 1)
            dve.wait_ge(sem("wcol_ready"), 1)
            dve.wait_ge(sem("cleared"), 3)
            link(v.tensor_scalar(selm[:, 0:P], future[:, :], 0.0, None, ALU.is_equal))
            v.copy_predicated(Dm[:, 0, 0:P], selm[:, 0:P], distv[:, 384:384 + P]).then_inc(sem("D_ready"), 1)
            for i in range(1, TT):
                N = P * (i + 1)
                for h in range(8):
                    n = 8 * (i - 1) + h
                    dve.wait_ge(sem("relu_ready"), n + 1)
                    if h == 0:
                        ins = v.tensor_scalar(I_s[:, 0:N], rl[n % 2][:, 0:N], wcol[:, i, 0:1], None, ALU.mult)
                    else:
                        ins = v.scalar_tensor_tensor(out=I_s[:, 0:N], in0=rl[n % 2][:, 0:N], scalar=wcol[:, i, h:h + 1],
                                                     in1=I_s[:, 0:N], op0=ALU.mult, op1=ALU.add)
                    ins.then_inc(sem("relu_used"), 1)
                    dve.wait_ge(sem("relu_used"), n + 1)
                link(v.copy_predicated(I_s[:, P * i:N], future[:, :], negc[:, :]))
                for _ in range(KEYS // 8):
                    link(v.max(top8[:, :], I_s[:, 0:N]))
                    link(v.match_replace(I_s[:, 0:N], top8[:, :], I_s[:, 0:N], NEG_TAKEN))
                link(v.tensor_scalar(selm[:, 0:N], I_s[:, 0:N], -2e38, None, ALU.is_lt))
                off = 384 - P * i
                v.copy_predicated(Dm[:, i, 0:N], selm[:, 0:N], distv[:, off:off + N]).then_inc(sem("D_ready"), 1)
            dve.wait_ge(sem("D_ready"), 4)
            def logits(i, h):
                n, N = 8 * i + h, P * (i + 1)
                b = done(dve, f"lg{i}{h}")
                if n >= 2:
                    dve.wait_ge(sem("exp_ready"), n - 1)
                v.scalar_tensor_tensor(out=L[n % 2][:, 0:N], in0=Dm[:, i, 0:N], scalar=float(2.0 ** -(h + 1)),
                                       in1=b[:, 0:N], op0=ALU.mult, op1=ALU.add).then_inc(sem("L_ready"), 1)
                dve.wait_ge(sem("L_ready"), n + 1)
                if n >= 2:
                    dve.wait_ge(sem("P_ready"), n - 1)
                v.tensor_reduce(nmax[:, n % 2:n % 2 + 1], L[n % 2][:, 0:N], AX, ALU.max, negate=True
                                ).then_inc(sem("nmax_ready"), 1)

            def normalise(i, h):
                n, N = 8 * i + h, P * (i + 1)
                dve.wait_ge(sem("exp_ready"), n + 1)
                link(v.reciprocal(top8[:, n % 2:n % 2 + 1], nmax[:, 2 + n % 2:3 + n % 2]))
                v.tensor_scalar(Pn[:, h, 0:N], Pn[:, h, 0:N], top8[:, n % 2:n % 2 + 1], None, ALU.mult
                                ).then_inc(sem("P_ready"), 1)

            for i in range(TT):
                for h in range(8):
                    logits(i, h)
                    if h:
                        normalise(i, h - 1)
                normalise(i, 7)
                for g in range(2):
                    b = done(dve, f"ol{i}{g}")
                    v.tensor_copy(olT[:, 4 * g:4 * g + 4, tile_cols(i)], b[:, :].rearrange("p (h t) -> p h t", h=4)
                                  ).then_inc(sem("ol_ready"), 1)

            dve.wait_ge(sem("extra_loaded"), 96)
            condition(4, "adr0")
            for n, (m, br) in enumerate(merge_steps()):
                dve.wait_ge(sem("gate_ready"), n + 1)
                b = done(dve, f"up{m}{br}")
                dst = mT[:, m, :] if br == 0 else mtmp[n % 2]
                v.tensor_tensor(dst, b[:, :], sgate[n % 2], ALU.mult).then_inc(sem("up_read"), 1)
                dve.wait_ge(sem("up_read"), n + 1)
                if br:
                    ins = v.tensor_tensor(mT[:, m, :], mT[:, m, :], mtmp[n % 2], ALU.add)
                    if br == 1:
                        link(ins)
                    else:
                        ins.then_inc(sem("mT_ready"), 1)
                if n % 2 and n // 2 < 8:
                    c = n // 2
                    b = done(dve, f"mb{c}")
                    dst = modB[:, c // 2, 512 * (c % 2):512 * (c % 2) + 512]
                    if c // 2 == 2:
                        ins = v.scalar_tensor_tensor(out=dst, in0=b[:, :], scalar=1.0,
                                                     in1=nffn[:, 512 * (c % 2):512 * (c % 2) + 512],
                                                     op0=ALU.add, op1=ALU.mult)
                    else:
                        ins = v.tensor_copy(dst, b[:, :])
                    ins.then_inc(sem("mb_ready"), 1)
                    if c < 7:
                        condition(5 + c, f"adr{c + 1}")
            dve.wait_ge(sem("mb_ready"), 8)
            for i in range(TT):
                for n in range(2):
                    b = done(dve, f"wo{i}{n}")
                    v.tensor_tensor(wtmp, b[:, :], modB[:, 0, 512 * n:512 * n + 512], ALU.mult).then_inc(sem("wo_read"), 1)
                    dve.wait_ge(sem("wo_read"), 2 * i + n + 1)
                    dst = x[:, i, 512 * n:512 * n + 512]
                    ins = v.tensor_tensor(dst, dst, wtmp, ALU.add)
                    if n:
                        ins.then_inc(sem("x2_ready"), 1)
                    else:
                        link(ins)
                dve.wait_ge(sem("x2_ready"), i + 1)
                dve.wait_ge(sem("rms_ready"), i + 2)
                link(v.reciprocal(stat[:, 12 + i:13 + i], stat[:, 12 + i:13 + i]))
                link(v.scalar_tensor_tensor(out=h2[:, i, :], in0=x[:, i, :], scalar=stat[:, 12 + i:13 + i],
                                            in1=modB[:, 2, :], op0=ALU.mult, op1=ALU.mult))
                v.tensor_tensor(h2[:, i, :], h2[:, i, :], modB[:, 1, :], ALU.add).then_inc(sem("h2_ready"), 1)

            for i in range(TT):
                dve.wait_ge(sem("rt_ready"), i + 1)
                sel = selr[:, i, :]
                link(v.tensor_tensor(sel, score[:, i, :], rbias[:, :], ALU.add))
                for g in range(GROUPS):
                    ins = v.max(gtop[:, g, :], sel[:, 8 * g:8 * g + 8])
                link(ins)
                link(v.tensor_tensor(gsc[:, :], gtop[:, :, 0], gtop[:, :, 1], ALU.add))
                link(v.max(gm8[:, :], gsc[:, :]))
                link(v.max_index(gidx[:, :], gm8[:, :], gsc[:, :]))
                link(v.tensor_copy(gidf[:, :], gidx[:, :]))
                link(v.tensor_scalar(gmask[:, :], iota_e[:, 0:8], gidf[:, 0:1], None, ALU.is_equal))
                for k in range(1, TOPG):
                    link(v.scalar_tensor_tensor(out=gmask[:, :], in0=iota_e[:, 0:8], scalar=gidf[:, k:k + 1],
                                                in1=gmask[:, :], op0=ALU.is_equal, op1=ALU.add))
                gb = gmask[:, :].rearrange("p (g o) -> p g o", o=1).to_broadcast([P, 8, 8])
                s3 = sel.rearrange("p (g e) -> p g e", g=8)
                link(v.tensor_tensor(s3, s3, gb, ALU.mult))
                link(v.tensor_scalar(gmask[:, :], gmask[:, :], 1.0, 1e30, ALU.subtract, ALU.mult))
                link(v.tensor_tensor(s3, s3, gb, ALU.add))
                link(v.max(gm8[:, :], sel))
                link(v.max_index(eidx[:, :], gm8[:, :], sel))
                link(v.tensor_copy(eidf[:, :], eidx[:, :]))
                for k in range(TOPK):
                    ins = v.tensor_scalar(onehot[:, k, :], iota_e[:, :], eidf[:, k:k + 1], None, ALU.is_equal)
                link(ins)
                for k in range(TOPK):
                    ins = v.tensor_tensor_reduce(rt_tmp, onehot[:, k, :], score[:, i, :], 1.0, 0.0, ALU.mult,
                                                 ALU.add, wk[:, i, k:k + 1])
                    link(ins)
                link(v.tensor_copy(eall[:, i, :], eidf[:, :]))
                link(v.tensor_reduce(wsum[:, :], wk[:, i, 0:TOPK], AX, ALU.add))
                link(v.reciprocal(wsum[:, :], wsum[:, :]))
                v.tensor_scalar(wk[:, i, 0:TOPK], wk[:, i, 0:TOPK], wsum[:, 0:1], 2.5, ALU.mult, ALU.mult)
                v.tensor_reduce(mall[:, i, :], onehot[:, 0:TOPK, :].rearrange("p k e -> p e k"), AX, ALU.add
                                ).then_inc(sem("mall_ready"), 1)
                dve.wait_ge(sem("mall_ready"), i + 1)
            b = done(dve, "tot")
            link(v.tensor_scalar(ntile, b[:, 0:E], 0.0, None, ALU.is_gt))
            for q in range(1, TT - 1):
                link(v.scalar_tensor_tensor(out=ntile, in0=b[:, 0:E], scalar=float(P * q), in1=ntile, op0=ALU.is_gt,
                                            op1=ALU.add))
            v.scalar_tensor_tensor(out=ntile, in0=b[:, 0:E], scalar=float(P * (TT - 1)), in1=ntile, op0=ALU.is_gt,
                                   op1=ALU.add).then_inc(sem("tot_read"), 1)
            dve.wait_ge(sem("tot_read"), 1)
            link(v.memset(rt_tmp, 1.0))
            link(v.tensor_tensor_scan(uend, rt_tmp, ntile, 0.0, ALU.mult, ALU.add))
            link(v.tensor_tensor(base, uend, ntile, ALU.subtract))
            v.tensor_scalar(base, base, float(P), None, ALU.mult).then_inc(sem("uend_ready"), 1)
            dve.wait_ge(sem("uend_ready"), 1)
            for i in range(TT):
                b = done(dve, f"pos{i}")
                v.tensor_tensor(slotA, b[:, 0:E], base, ALU.add).then_inc(sem("slot_done"), 1)
                dve.wait_ge(sem("slot_done"), i + 1)
                for k in range(TOPK):
                    link(v.tensor_scalar(rt_tmp2, iota_e[:, :], eall[:, i, k:k + 1], None, ALU.is_equal))
                    link(v.tensor_tensor_reduce(rt_tmp2, rt_tmp2, slotA, 1.0, 0.0, ALU.mult, ALU.add,
                                                slotf[:, i, k:k + 1]))
                v.tensor_copy(sloti[:, i, 0:TOPK], slotf[:, i, 0:TOPK]).then_inc(sem("slots_ready"), 1)
            b = done(dve, "ue")
            v.tensor_copy(ucolf[:, :], b[0:E, 0:1]).then_inc(sem("ue_ready"), 1)
            dve.wait_ge(sem("ue_ready"), 1)
            v.tensor_scalar(ucmp[:, :], iota_u[:, :], ucolf[:, 0:1], None, ALU.is_ge).then_inc(sem("ucmp_ready"), 1)
            b = done(dve, "uc")
            v.tensor_scalar(uexp[:, :], b[0:1, 0:96], float(E - 1), None, ALU.min).then_inc(sem("uc_ready"), 1)
            link(v.tensor_scalar(npf[:, :], iota_e[0:1, :], 2.0, uend[0:1, E - 1:E], ALU.mult, ALU.is_lt))
            link(v.tensor_reduce(npg[:, :], npf[:, :], AX, ALU.add))
            v.tensor_copy(npair[:, :], npg[:, :]).then_inc(sem("table_ready"), 1)
            for m in range(2):
                dve.wait_ge(sem("sg_ready"), m + 1)
                b = done(dve, f"su{m}")
                v.tensor_tensor(actS[:, m, :], b[:, :], sgS[m], ALU.mult).then_inc(sem("actS_ready"), 1)
            for i in range(TT):
                for n in range(2):
                    b = done(dve, f"sd{i}{n}")
                    v.tensor_tensor(wtmp2, b[:, :], modB[:, 3, 512 * n:512 * n + 512], ALU.mult).then_inc(sem("sd_read"), 1)
                    dve.wait_ge(sem("sd_read"), 2 * i + n + 1)
                    dst = x[:, i, 512 * n:512 * n + 512]
                    v.tensor_tensor(dst, dst, wtmp2, ALU.add).then_inc(sem("x_added"), 1)
                    dve.wait_ge(sem("x_added"), 2 * i + n + 1)
            dve.wait_ge(sem("table_ready"), 1)
            dve.wait_ge(sem("x_added"), 8)
            pairs = dve.value_load(npair[0:1, 0:1], min_val=1, max_val=UNITS // 2)

            def weights_lo(u, c, k, part=slice(0, 2048), last=True):
                dve.wait_ge(sem("hi_ready"), 3 * u + k + 1)
                ins = v.tensor_tensor(w_lo[c][k][:, part], w_raw[c][k][:, part], w_hi[c][k][:, part].bitcast(F32), ALU.subtract)
                if last:
                    ins.then_inc(sem("lo_ready"), 1)

            def turned(u, c, half):
                dve.wait_ge(sem("xe_hi_ready"), 2 * u + half + 1)
                s_ = slice(512 * half, 512 * half + 512)
                v.tensor_tensor(xe_lo[c][:, s_], bank[half][:, :], xe_hi[c][:, s_].bitcast(F32), ALU.subtract
                                ).then_inc(sem("xe_lo_ready"), 1)

            for half in range(2):
                turned(0, 0, half)
            for k in range(3):
                weights_lo(0, 0, k)
            with dve.Fori(0, pairs) as i:
                for b in range(2):
                    c, u = 1 - b, 2 * i + b
                    weights_lo(u + 1, c, 0)
                    weights_lo(u + 1, c, 1, slice(0, D), False)
                    dve.wait_ge(sem("sge_ready"), u + 1)
                    v.tensor_tensor(acte[b], bank[2][:, FF:2 * FF], sge[b], ALU.mult).then_inc(sem("acte_ready"), 1)
                    turned(u + 1, c, 0)
                    dve.wait_ge(sem("ae_hi_ready"), u + 1)
                    v.tensor_tensor(ae_lo[b], bank[3][:, 0:FF].rearrange("p (m t) -> p m t", m=2), ae_hi[b].bitcast(F32),
                                    ALU.subtract).then_inc(sem("ae_lo_ready"), 1)
                    turned(u + 1, c, 1)
                    weights_lo(u + 1, c, 1, slice(D, 2 * D))
                    weights_lo(u + 1, c, 2)
            dve.wait_ge(sem("extra_loaded"), 112)
            for i in range(TT):
                for k in range(TOPK):
                    n = TOPK * i + k
                    dve.wait_ge(sem(f"yk_loaded{i % 2}"), 16 * (i // 2 + 1))
                    if k == 0:
                        ins = v.tensor_scalar(routed, yk[i % 2][:, k, :], wk[:, i, 0:1], None, ALU.mult)
                    else:
                        ins = v.scalar_tensor_tensor(out=routed, in0=yk[i % 2][:, k, :], scalar=wk[:, i, k:k + 1], in1=routed,
                                                     op0=ALU.mult, op1=ALU.add)
                    ins.then_inc(sem("yk_used"), 1)
                    dve.wait_ge(sem("yk_used"), n + 1)
                link(v.tensor_tensor(routed, routed, modB[:, 3, :], ALU.mult))
                v.tensor_tensor(x[:, i, :], x[:, i, :], routed, ALU.add).then_inc(sem("x4_ready"), 1)
                dve.wait_ge(sem("x4_ready"), i + 1)
                dve.wait_ge(sem("rms_ready"), i + 6)
                link(v.reciprocal(stat[:, 4 + i:5 + i], stat[:, 4 + i:5 + i]))
                v.scalar_tensor_tensor(out=x[:, i, :], in0=x[:, i, :], scalar=stat[:, 4 + i:5 + i], in1=nfin,
                                       op0=ALU.mult, op1=ALU.mult).then_inc(sem("out_ready"), 1)


_INS = ['x', 'c', 'ada_w', 'ada_b', 'norm_mix', 'norm_ffn', 'w_in', 'gla_w_a2', 'gla_b_a', 'gla_norm',
        'dsa_norm_q', 'dsa_norm_kv', 'dsa_w_uq', 'dsa_w_uk', 'dsa_w_uv', 'dsa_w_qi', 'mlstm_conv', 'mlstm_b_i',
        'mlstm_b_f', 'mlstm_norm', 'w_up_a', 'w_up_b', 'w_up_c', 'w_o', 'router_w', 'router_bias', 'exp_w_gate',
        'exp_w_up', 'exp_w_down', 'sh_w_gate', 'sh_w_up', 'sh_w_down', 'norm_final']


def kernel(**inputs):
    import numpy as _np
    import concourse.bacc as _bacc
    from concourse import mybir as _mybir
    from concourse.bass_utils import run_bass_kernel_spmd as _run

    nc = _bacc.Bacc("TRN2", target_bir_lowering=False, num_devices=1)
    arrays, aps = {}, {}
    for name in _INS:
        v = _np.ascontiguousarray(inputs[name])
        arrays[f"in_{name}"] = v
        aps[name] = nc.dram_tensor(f"in_{name}", v.shape, _mybir.dt.from_np(v.dtype), kind="ExternalInput").ap()
    shape = inputs["x"].shape
    out = nc.dram_tensor("out_0", shape, _mybir.dt.float32, kind="ExternalOutput").ap()
    hybrid_kernel(nc, aps, out)
    r = _run(nc, [arrays], core_ids=[0])
    return r.results[0]["out_0"]
```

```python
from contextlib import ExitStack

import numpy as np

import concourse.bass as bass
from concourse import mybir

F32 = mybir.dt.float32
F32R = mybir.dt.float32r
I32 = mybir.dt.int32
U32 = mybir.dt.uint32
ALU = mybir.AluOpType
ACT = mybir.ActivationFunctionType
AX = mybir.AxisListType.X

P = 128
BANKS = 8
EPS = 1e-6
NEG_MASK = -1e30
NEG_FUTURE = -1e38
NEG_TAKEN = -3e38

IN_SIZES = dict(qa=256, ka=256, va=512, ga=512, a_lr=16, cq=256, ckv=128, k_idx=32, w_idx=8,
                qc=256, kc=256, vc=512, ic=4, fc=4, oc=512, gates=3072)
COL = {}
_at = 0
for _n, _w in IN_SIZES.items():
    COL[_n] = _at
    _at += _w


def tile_cols(i, n=P):
    return slice(i * n, (i + 1) * n)


def merge_steps():
    return [(m, b) for m in range(0, 8, 2) for b in range(3)]


def wo_order():
    return [(i, q) for q in range(2) for i in range(4)] + [(i, q) for i in range(4) for q in (2, 3)]


def product_order():
    out = [("params", "params_ready", 1)]
    out += [(f"mc{c}", "mc_ready", c + 1) for c in range(4)]
    out += [(f"xT{j}", "hT_ready", j + 1) for j in range(8)]
    out += [("small", "small_ready", 1)]
    out += [(f"la{f}", "z_ready", f + 1) for f in range(2)]
    out += [(f"qa{f}", "qa_ready", f + 1) for f in range(2)]
    out += [(f"ka{f}", "ka_ready", f + 1) for f in range(2)]
    out += [(f"va{q}{i}", "v_ready", 4 * q + i + 1) for q in range(2) for i in range(4)]
    out += [(f"kd{f}", "kdr_ready", f + 1) for f in range(2)]
    out += [(f"st{i}{f}", "state_ready", 2 * i + f + 1) for i in range(3) for f in range(2)]
    out += [(f"scA{l}{g}", "intra_done", 4 * l + g + 1) for l in range(8) for g in range(4)]
    out += [(f"ga{m}", "outgate_ready", m + 1) for m in range(4)]
    for h in range(5):
        out += [(f"oA{h}", "oA_read", h + 1)] if h < 4 else []
        out += [(f"msA{h - 1}", "root_ready", h)] if h >= 1 else []
    out += [(f"mb{c}", "mb_ready", c + 1) for c in range(3)]
    out += [(f"qk{f}", "qk_ready", f + 1) for f in range(4)]
    out += [("uT", "u_ready", 1)]
    out += [(f"vc{q}{i}", "v_ready", 4 * q + i + 9) for q in range(2) for i in range(4)]
    out += [(f"oc{m}", "outgate_ready", m + 5) for m in range(4)]
    for h in range(4):
        out += [(f"bm{h}", "SW_ready", 4 * h + 4), (f"bt{h}", "floor_ready", h + 1)]
        out += [(f"scC{h}{j}", "SW_ready", 4 * h + j + 1) for j in range(4)]
        out += [(f"msC{h - 1}", "root_ready", h + 4)] if h else []
        out += [(f"cl{h - 1}", "craw_ready", h) if h else ("kidx", "kidx_ready", 1)]
        out += [(f"num{h}", "hC_ready", h + 1), (f"den{h}", "den_read", h + 1)]
    out += [("msC3", "root_ready", 8)]
    out += [("msq", "root_ready", 9), ("mskv", "root_ready", 10)]
    out += [("wi", "wcol_ready", 1), ("uk", "ukT_ready", 1)]
    out += [("ckr", "ckr_ready", 1)]
    out += [(f"qi{m}", "qi_ready", m + 1) for m in range(2)]
    out += [(f"ix{i}{h}", "relu_ready", 8 * (i - 1) + h + 1) for i in range(1, 4) for h in range(8)]
    out += [(f"q{m}", "q_ready", m + 1) for m in range(4)]
    out += [(f"mb{c}", "mb_ready", c + 1) for c in range(3, 8)]
    out += [(f"ql{h}", "ql_ready", h + 1) for h in range(8)]
    for n in range(-1, 8):
        if n < 7:
            i, g = divmod(n + 1, 2)
            out += [(f"lg{i}{h}", "L_ready", 8 * i + h + 1) for h in range(4 * g, 4 * g + 4)]
        if n >= 0:
            i, g = divmod(n, 2)
            k = i * (i + 1) + g * (i + 1)
            out += [(f"pt{i}{g}{j}", "PT_ready", k + j + 1) for j in range(i + 1)]
            out += [(f"ol{i}{g}", "ol_ready", n + 1)]
    out += [(f"ob{m}", "oTB_ready", m + 1) for m in range(4)]
    for n, (m, b) in enumerate(merge_steps()):
        out += [(f"gate{m + r}{b}", "gate_ready", 2 * n + r + 1) for r in range(2)]
        out += [(f"up{m + r}{b}", "up_read", 2 * n + r + 1) for r in range(2)]
        out += [(f"mr{n}", "mr_ready", n + 1)] if n < 8 else []
    out += [(f"wo{i}{q}", "wo_read", n + 1) for n, (i, q) in enumerate(wo_order())]
    out += [(f"hT2{j}", "h2T_ready", j + 1) for j in range(8)]
    out += [(f"rt{i}", "rt_ready", i + 1) for i in range(4)]
    out += [("sg0", "sg_ready", 1), ("su0", "actS_ready", 1)]
    out += [("tot", "tot_read", 1), ("sg1", "sg_ready", 2), ("ue", "ue_ready", 1), ("uc", "uc_ready", 1)]
    out += [(f"pos{i}", "slot_done", i + 1) for i in range(4)]
    out += [("lists", "lists_ready", 1), ("su1", "actS_ready", 2)]
    out += [(f"sd{i}{n}", "sd_read", 2 * i + n + 1) for i in range(4) for n in range(2)]
    return out


def hybrid_kernel(nc, a, out):
    T, D = a["x"].shape[1:]
    TT, KT = T // P, D // P
    E = a["router_w"].shape[2]
    FF = a["exp_w_gate"].shape[3]
    TOPK, GROUPS, TOPG = 6, 8, 4
    KEYS = T // 4
    UNITS = E + T * TOPK // P
    assert (T, D, TT, KT, E, FF) == (512, 1024, 4, 8, 64, 256)

    products = product_order()
    number = {name: n for n, (name, _, _) in enumerate(products)}
    assert len(number) == len(products)

    ctx = ExitStack()
    with ctx:
        sems = {}

        def sem(name):
            if name not in sems:
                sems[name] = ctx.enter_context(nc.semaphore(name))
            return sems[name]

        def sb(name, shape, dt=F32):
            return ctx.enter_context(nc.sbuf_tensor(name, shape, dt))

        def sb_two(name, shape):
            with nc.sbuf_tensor(name, shape, F32) as plain:
                pass
            parts = sb(name + "_parts", shape, F32R)
            return plain, parts

        bank = [ctx.enter_context(nc.psum_tensor(f"bank{i}", [P, 512], F32)) for i in range(BANKS)]

        x, hT_lo = sb_two("x", [P, TT, D])
        hT_lo = hT_lo[:].rearrange("p i (k t) -> p (i k) t", t=T)
        hT, hT_hi = sb_two("hT", [P, KT, T])
        oT, oTp = zip(*[sb_two(f"oT{b}", [P, 4, T]) for b in "ABC"])
        RING = 3
        ring, ringp = sb_two("ring", [P, 2 * RING, 2048])
        arena, arenap = sb_two("arena", [P, 22528])
        ident = sb("ident", [P, P])
        ones = sb("ones", [P, P])
        causal = sb("causal", [P, P])
        before = sb("before", [P, P])
        future = sb("future", [P, P], I32)
        negc = sb("negc", [P, P])
        small = sb("small", [P, T])
        prow = sb("prow", [53, P])
        par = sb("par", [P, 53])
        stat = sb("stat", [P, 16])
        epsc = sb("epsc", [P, 1])
        cs = sb("cs", [P, 8])
        c_in = sb("c_in", [P, 8])
        mod1 = sb("mod1", [P, 16])
        modcol = sb("modcol", [P, 32])
        bif = sb("bif", [4, 2])
        iota = sb("iota", [P, P])
        iota_e = iota[:, 0:E]
        wcol = sb("wcol", [P, TT, 8])

        class Region:
            def __init__(self, tensor, start=0, end=None):
                self.t, self.at, self.end = tensor, start, end

            def take(self, *shape, dt=F32, parts=P):
                n = int(np.prod(shape))
                assert self.end is None or self.at + n <= self.end, (self.at, n, self.end)
                v = self.t[0:parts, self.at:self.at + n]
                if dt not in (F32, F32R):
                    v = v.bitcast(dt)
                self.at += n
                if len(shape) == 2:
                    v = v.rearrange("p (a b) -> p a b", a=shape[0])
                elif len(shape) == 3:
                    v = v.rearrange("p (a b c) -> p a b c", a=shape[0], b=shape[1])
                elif len(shape) == 4:
                    v = v.rearrange("p (a b c d) -> p a b c d", a=shape[0], b=shape[1], c=shape[2])
                return v

        END = 22528
        r0 = Region(arena, 0, END)
        xn = r0.take(TT, D)
        junk = r0.take(D)
        ra = Region(arena, 0, END)
        qT, kT, cum = ra.take(2, T), ra.take(2, T), ra.take(2, T)
        arg = [ra.take(2, T) for _ in range(2)]
        decay = ra.take(2, T)
        qE = [ra.take(2, T) for _ in range(2)]
        kE = [ra.take(2, T) for _ in range(2)]
        va = ra.take(TT, T)
        S = ra.take(2, TT, 2, P)
        sga = ra.take(4, T)
        qcz = [ra.take(2, T) for _ in range(2)]
        state = ra.take(3, 2, P)
        rsA = [ra.take(T) for _ in range(2)]
        hA = ra.take(T)
        condA = [ra.take(T) for _ in range(3)]
        ra2 = Region(oT[1][:].rearrange("p a b -> p (a b)"), 0, 2048)
        ecum, kdr = ra2.take(2, T), ra2.take(TT, 2, P)
        ra3 = Region(oT[2][:].rearrange("p a b -> p (a b)"), 0, 2048)
        level_mask = ra3.take(8, P, dt=I32)
        resets = ra3.take(T)
        sqA = ra3.take(T)
        w_a2 = sb("w_a2", [16, 256])
        rc = Region(arena, 0, END)
        raw = rc.take(4, 516)
        qkc = rc.take(4, T)
        vc, soc = rc.take(TT, T), rc.take(4, T)
        floor_, hC, sqC, rsC = rc.take(T), rc.take(T), rc.take(T), rc.take(T)
        argC = [rc.take(T) for _ in range(2)]
        W = [rc.take(T) for _ in range(2)]
        SW = rc.take(TT, T)
        sel4 = rc.take(4, P, parts=4)
        g4 = [rc.take(T, parts=4) for _ in range(8)]
        ones4 = rc.take(T, parts=4)
        ucol = rc.take(TT, 4)
        hD = rc.take(T)
        condC = [rc.take(T) for _ in range(3)]
        rb = Region(arena, 0, END)
        cn, qlT, qiT = rb.take(3, T), rb.take(8, T), rb.take(2, T)
        rb0 = Region(oT[1][:].rearrange("p a b -> p (a b)"), 0, 2048)
        craw, kidxT = rb0.take(3, T), rb0.take(T)
        Dm, ckr, w_uv = rb.take(TT, T), rb.take(TT, P), rb.take(T)
        distv = rb.take(896)
        rb1 = Region(arena, rb.at, END)
        sqB, rsB, qTb = rb1.take(3, T), rb1.take(2, T), rb1.take(4, T)
        w_uq, w_uk, w_qi, ukT = rb1.take(2, T), rb1.take(T), rb1.take(2, 256), rb1.take(4, P)
        rl = [rb1.take(T) for _ in range(2)]
        I_s = rb1.take(T)
        selm = craw[:, 0, :].bitcast(I32)
        wi0 = sb("wi0", [8, T])
        top8 = sb("top8", [P, 8])
        rb2 = Region(arena, rb.at, END)
        Pn, PT, olT = rb2.take(8, T), rb2.take(TT, T), rb2.take(8, T)
        L = [rb2.take(T) for _ in range(2)]
        nmax, psum = sb("nmax", [P, 8]), sb("psum", [P, 8])
        modB = arena[:, 18432:22528].rearrange("p (a b) -> p a b", a=4)
        mT = arena[:, 14336:18432].rearrange("p (a b) -> p a b", a=8)
        rm = Region(arena, 0, 14336)
        oT_hi = [arenap[:, 2048 * b:2048 * b + 2048].rearrange("p (a b) -> p a b", a=4) for b in range(3)]
        oT_lo = oTp
        rm.at = 6144
        nffn = rm.take(D)
        sgate = [rm.take(T) for _ in range(2)]
        mtmp = [rm.take(T) for _ in range(2)]
        cond_merge = [rm.take(T) for _ in range(2)]
        mT_hi = arenap[:, rm.at:rm.at + 4096].rearrange("p (a b) -> p a b", a=8)
        mT_lo = arenap[:, 14336:18432].rearrange("p (a b) -> p a b", a=8)
        wtmp = mtmp[0]
        rm = Region(arena, 0, 6144)
        h2 = rm.take(TT, D)
        sqx = rm.take(D)
        re = Region(arena, 0, 14336)
        ringf = ring[:].rearrange("p s n -> p (s n)")
        rw_ = Region(ringf, 0, 12288)
        w_at = [None, None]
        for b in (1, 0):
            w_at[b] = rw_.at
            rw_.at += 6144

        def pieces(t, at):
            return [t[:, at + 2048 * k:at + 2048 * k + 2048] for k in range(3)]

        w_raw = [pieces(ringf, w_at[b]) for b in range(2)]
        w_lo = [pieces(ringp[:].rearrange("p s n -> p (s n)"), w_at[b]) for b in range(2)]
        w_hi = [pieces(arenap, 6144 * b) for b in range(2)]
        re.at = 12288
        nfin = re.take(D)
        rx = Region(arena, 14336, 18432)
        xg = [rx.take(D) for _ in range(2)]
        ys = [rx.take(D) for _ in range(2)]
        xe_hi, xe_lo = ([t[:].rearrange("p a b -> p (a b)")[:, D * b:D * b + D]
                         for b in range(2)] for t in (oTp[0], oTp[2]))
        ro = Region(oT[1][:].rearrange("p a b -> p (a b)"), 0, 2048)
        sge = [ro.take(FF) for _ in range(2)]
        acte = [ro.take(FF) for _ in range(2)]
        rp = Region(oTp[1][:].rearrange("p a b -> p (a b)"), ro.at, 2048)
        ae_hi = [rp.take(2, P, dt=F32R) for _ in range(2)]
        ae_lo = [rp.take(2, P, dt=F32R) for _ in range(2)]
        rr = Region(oT[2][:].rearrange("p a b -> p (a b)"), 0, 2048)
        score, selr, mall = rr.take(TT, E), rr.take(TT, E), rr.take(TT, E)
        rt_tmp = rr.take(E)
        rk = Region(arena, 6144, 12288)
        onehot, picked = rk.take(TT, TOPK, E), rk.take(TT, TOPK, E)
        gtop, ghot = rk.take(TT * GROUPS, 8), rk.take(TT, GROUPS, TOPG)
        gsc, gm8, gmask, gidf, em8 = (rk.take(TT, 8) for _ in range(5))
        gidx, eidx = rk.take(TT, 8, dt=U32), rk.take(TT, 8, dt=U32)
        wsum = rk.take(TT)
        base, ntile, uend = rr.take(E), rr.take(E), rr.take(E)
        slotA = rr.take(E)
        rbias = sb("rbias", [P, E])
        wk = sb("wk", [P, TT, 8])
        slotf, sloti = sb("slotf", [P, TOPK]), sb("sloti", [P, 3, TOPK], I32)
        placef = sb("placef", [P, 2, TOPK])
        row1 = sb("row1", [P, TT, TOPK])
        LISTS = UNITS + 2
        toks, rows_y, absent = (sb(n, [P, LISTS], I32) for n in ("toks", "rows_y", "absent"))
        is_row = [arena[:, at:at + TOPK * P].rearrange("p (k r) -> p k r", k=TOPK) for at in (14336, 15104)]
        is_unit = [v.rearrange("p (k u) -> p k u", k=TOPK)
                   for v in (arena[:, 13312:13312 + TOPK * LISTS], rr.take(TOPK * LISTS))]
        ucolf = sb("ucolf", [E, 1])
        ucmp = sb("ucmp", [E, 96])
        uexp = sb("uexp", [1, 96], I32)
        npair = sb("npair", [1, 1], I32)
        npf = sb("npf", [1, 64])
        npg = sb("npg", [1, 1])
        iota_u = iota[0:E, 0:96]
        tok_of = [sb(f"tok_of{b}", [P, 1], I32) for b in range(2)]
        row_of = [sb(f"row_of{b}", [P, 1], I32) for b in range(2)]
        eall = sb("eall", [P, TT, 8])
        sgS = [oT[1][:, 2 + m, :] for m in range(2)]
        rs = Region(arena, 16384, 18432)
        actS, wtmp2 = rs.take(2, T), rs.take(T)
        yk = [arena[:, 6144 * b:6144 * b + 6144].rearrange("p (k n) -> p k n", k=TOPK) for b in range(2)]
        routed = [hT[:, 2 * b:2 * b + 2, :].rearrange("p a b -> p (a b)") for b in range(2)]

        sq_out = ring[:, 0:1, 0:D].rearrange("p a b -> p (a b)")

        h_dram = nc.dram_tensor("h_dram", [T, D], F32).ap()
        y_dram = nc.dram_tensor("y_dram", [T * TOPK, D], F32).ap()

        w_in = a["w_in"][0].rearrange("(j p) n -> p j n", p=P)
        ada = a["ada_w"][0].rearrange("(p j) n -> p j n", j=8)
        loads = []
        splits = []

        def slot_view(n, off, *shape, t=ring, at=0):
            v = t[:, at + n % RING, off:off + int(np.prod(shape))]
            return v.rearrange("p (a b) -> p a b", a=shape[0])

        def load(name, parts, last, split=True):
            n = len(loads)
            loads.append((name, [(slot_view(n, off, *shape), src) for off, shape, src in parts], last))
            if split:
                splits.append(name)

        def load_cols(name, c, last, n=256):
            load(name, [(0, (8, n), w_in[:, :, c:c + n])], last)

        def load_cond(c):
            for h in range(2):
                load(f"adr{c}{h}", [(0, (4, 512), ada[:, 4 * h:4 * h + 4, 2048 + 512 * c:2560 + 512 * c])],
                     ("further_ready", 1 + 2 * c + h), split=False)

        load_cols("w_qa", COL["qa"], "qa1")
        load_cols("w_ka", COL["ka"], "ka1")
        for q in range(2):
            load_cols(f"w_va{q}", COL["va"] + 256 * q, f"va{q}3")
        for c in range(3):
            load_cond(c)
        for q in range(2):
            load_cols(f"w_ga{q}", COL["ga"] + 256 * q, f"ga{2 * q + 1}")
        for q in range(2):
            load_cols(f"w_qkc{q}", COL["qc"] + 256 * q, f"qk{2 * q + 1}")
        for q in range(2):
            load_cols(f"w_vc{q}", COL["vc"] + 256 * q, f"vc{q}3")
        for q in range(2):
            load_cols(f"w_oc{q}", COL["oc"] + 256 * q, f"oc{2 * q + 1}")
        load_cols("w_cl0", COL["cq"], "cl1")
        load_cols("w_cl1", COL["ckv"], "cl2", 128)
        for c in range(3, 8):
            load_cond(c)
        ups = [a[n][0].rearrange("(j p) n -> p j n", p=P) for n in ("w_up_a", "w_up_b", "w_up_c")]
        for n, (m, b) in enumerate(merge_steps()):
            load_cols(f"wg{n}", COL["gates"] + D * b + P * m, f"gate{m + 1}{b}")
            load(f"wu{n}", [(0, (4, 256), ups[b][:, :, P * m:P * m + 256])], f"up{m + 1}{b}")
        wo_d = a["w_o"][0].rearrange("(j p) n -> p j n", p=P)
        for q in range(4):
            load(f"wo{q}", [(0, (8, 256), wo_d[:, :, 256 * q:256 * q + 256])], f"wo3{q}")
        load("w_rt", [(0, (8, E), a["router_w"][0].rearrange("(p j) e -> p j e", j=8))], "rt3", split=False)
        load("w_shg", [(0, (8, 256), a["sh_w_gate"][0].rearrange("(p j) f -> p j f", j=8))], "sg1", split=False)
        load("w_shu", [(0, (8, 256), a["sh_w_up"][0].rearrange("(p j) f -> p j f", j=8))], "su1", split=False)
        load("w_shd", [(0, (2, D), a["sh_w_down"][0].rearrange("(p m) n -> p m n", m=2))], "sd31", split=False)
        load_at = {name: n for n, (name, _, _) in enumerate(loads)}
        landed = {}
        count = [0] * RING
        for n, (name, parts, _) in enumerate(loads):
            count[n % RING] += 16 * len(parts)
            landed[name] = (n % RING, count[n % RING])

        def loaded(eng, name):
            s, v = landed[name]
            eng.wait_ge(sem(f"ring_loaded{s}"), v)

        def ring_view(name, off, *shape):
            return slot_view(load_at[name], off, *shape)

        def hi_view(name, *shape):
            return slot_view(load_at[name], 0, *shape, t=ringp, at=RING)

        def lo_view(name, *shape):
            return slot_view(load_at[name], 0, *shape, t=ringp)

        def size_of(name):
            return int(np.prod(loads[load_at[name]][1][0][0].shape[1:]))

        def split_wait(eng, name, part):
            eng.wait_ge(sem(part), splits.index(name) + 1)

        def done(eng, name):
            n = number[name]
            eng.wait_ge(sem("products_done"), n + 1)
            return bank[n % BANKS]

        wsm = r0.take(8, P)
        cond0 = [r0.take(T) for _ in range(2)]
        h32 = [r0.take(T) for _ in range(2)]
        adaw = [r0.take(8, 512) for _ in range(3)]
        wsm_lo = arenap[:, 5120:6144].rearrange("p (j n) -> p j n", j=8)
        wsm_hi = arenap[:, r0.at:r0.at + D].rearrange("p (j n) -> p j n", j=8)
        r0.take(D)
        cond = [*condA, *condC, qlT[:, 0, :], qlT[:, 1, :]]
        wki, wki_lo = sb_two("wki", [P, 8, 32])
        wki_hi = sb("wki_hi", [P, 8, 32], F32R)
        GAPS = {"a_lr": 0, "w_idx": 32, "ic": 64, "fc": 96}

        for n in ("consts", "consts_loaded", "products_done", "dve_chain", "act_chain", "pool_chain",
                  *[f"ring_loaded{i}" for i in range(RING)], *sorted({s for _, s, _ in products})):
            sem(n)

        block = ctx.enter_context(nc.Block())
        NCONST = [0]

        @block.sync
        def _(sp):
            def const(dst, src):
                sp.dma_start(dst, src).then_inc(sem("consts_loaded"), 16)
                NCONST[0] += 16

            for name, n in (("piece_used", 6), ("turned", 1), ("y_read", 4)):
                sp.sem_inc(sem(name), n)

            def rows(v, n):
                return v.rearrange("(r p) -> r p", p=P)[0:n]

            const(c_in[:, :], a["c"].rearrange("o (p j) -> (o p) j", j=8))
            sp.dma_start(x[:, :, :], a["x"][0].rearrange("(i p) d -> p i d", p=P)).then_inc(sem("x_loaded"), 16)
            const(prow[0:8, :], rows(a["norm_mix"][0], 8))
            const(prow[8:24, :], rows(a["ada_b"][0], 16))
            const(prow[24:26, :], rows(a["gla_b_a"][0], 2))
            const(prow[26:30, :], rows(a["gla_norm"][0], 4))
            const(prow[30:32, :], rows(a["dsa_norm_q"][0], 2))
            const(prow[32:33, :], rows(a["dsa_norm_kv"][0], 1))
            const(prow[33:37, :], rows(a["mlstm_norm"][0], 4))
            const(prow[37:53, :], a["mlstm_conv"][0].rearrange("k (r p) -> (k r) p", p=P))
            const(w_a2[:, :], a["gla_w_a2"][0])
            with nc.allow_non_contiguous_dma(reason="eight numbers"):
                const(bif[:, 0:1], a["mlstm_b_i"].rearrange("o h -> h o"))
                const(bif[:, 1:2], a["mlstm_b_f"].rearrange("o h -> h o"))
            sp.wait_ge(sem("small_cleared"), 1)
            for name, g in GAPS.items():
                const(wsm[:, :, g:g + IN_SIZES[name]], w_in[:, :, COL[name]:COL[name] + IN_SIZES[name]])
            const(wki[:, :, :], w_in[:, :, COL["k_idx"]:COL["k_idx"] + 32])
            const(rbias[:, :], a["router_bias"].to_broadcast([P, E]))

            for c in range(4):
                if c == 3:
                    done(sp, "mc0")
                sp.dma_start(adaw[c % 3], ada[:, :, 512 * c:512 * c + 512]).then_inc(sem(f"ada_loaded{c % 3}"), 16)

            def ring_load(n):
                name, parts, last = loads[n]
                if n >= RING:
                    last = loads[n - RING][2]
                    if isinstance(last, str):
                        sp.wait_ge(sem("products_done"), number[last] + 1)
                    else:
                        sp.wait_ge(sem(last[0]), last[1])
                for dst, src in parts:
                    sp.dma_start(dst, src).then_inc(sem(f"ring_loaded{n % RING}"), 16)

            n = 0
            while n < len(loads):
                name = loads[n][0]
                if name == "adr60":
                    sp.wait_ge(sem("oTC_ready"), 4)
                    sp.dma_start(w_uq, a["dsa_w_uq"][0].rearrange("(k p) h d -> p k (h d)", p=P)).then_inc(sem("extra_loaded"), 16)
                    sp.dma_start(w_uk, a["dsa_w_uk"][0].rearrange("c h d -> c (h d)")).then_inc(sem("extra_loaded"), 16)
                    sp.dma_start(w_uv, a["dsa_w_uv"][0].rearrange("c h d -> c (h d)")).then_inc(sem("extra_loaded"), 16)
                    sp.dma_start(w_qi, a["dsa_w_qi"][0].rearrange("(k p) h d -> p k (h d)", p=P)).then_inc(sem("extra_loaded"), 16)
                if name == "wg1":
                    sp.wait_ge(sem("oTB_ready"), 4)
                    sp.dma_start(nffn, a["norm_ffn"].to_broadcast([P, D])).then_inc(sem("extra_loaded"), 16)
                    sp.dma_start(modB, a["ada_b"][0:1, 2048:6144].to_broadcast([P, 4096]).rearrange("p (a b) -> p a b", a=4)
                                 ).then_inc(sem("extra_loaded"), 16)
                if name == "wo2":
                    done(sp, "gate72")
                    sp.dma_start(x[:, :, :], a["x"][0].rearrange("(i p) d -> p i d", p=P)).then_inc(sem("x_loaded"), 16)
                ring_load(n)
                n += 1

            for i in range(TT):
                sp.wait_ge(sem("h2_ready"), i + 1)
                sp.dma_start(h_dram[P * i:P * i + P, :], h2[:, i, :]).then_inc(sem("h_stored"), 16)
            sp.wait_ge(sem("h_stored"), 16 * TT)
            sp.wait_ge(sem("h2T_ready"), 8)
            sp.dma_start(nfin, a["norm_final"].rearrange("(o d) -> o d", o=1).to_broadcast([P, D])).then_inc(sem("extra_loaded"), 16)

            sp.wait_ge(sem("table_ready"), 1)
            pairs = sp.value_load(npair[0:1, 0:1], min_val=1, max_val=UNITS // 2)
            def load_piece(e, b, k):
                if k < 2:
                    dst = w_raw[b][k].rearrange("p (g j f) -> p g j f", g=2, j=4)
                    for g, w in enumerate(("exp_w_gate", "exp_w_up")):
                        src = a[w][0][bass.ds(e, 1)].rearrange("e (p j) f -> (e p) j f", j=8)[:, 4 * k:4 * k + 4, :]
                        sp.dma_start(dst[:, g, :, :], src).then_inc(sem(f"w_loaded{b}{k}"), 16)
                else:
                    src = a["exp_w_down"][0][bass.ds(e, 1)].rearrange("e (p m) n -> (e p) m n", m=2)
                    sp.dma_start(w_raw[b][2].rearrange("p (m n) -> p m n", m=2), src).then_inc(sem(f"w_loaded{b}2"), 16)

            e = sp.value_load(uexp[0:1, 0:1], min_val=0, max_val=E - 1)
            for k in range(3):
                load_piece(e, 0, k)
            sp.wait_ge(sem("products_done"), len(products))
            with sp.Fori(0, pairs) as i:
                for b in range(2):
                    c, u = 1 - b, 2 * i + b
                    e = sp.value_load(uexp[0:1, bass.ds(u + 1, 1)], min_val=0, max_val=E - 1)
                    for k in range(3):
                        sp.wait_ge(sem("piece_used"), 3 * u + k + 4)
                        load_piece(e, c, k)

            for b in range(2):
                sp.wait_ge(sem(f"y_stored{b}"), 16 * pairs + 16)
            sp.wait_ge(sem("lo_ready"), 6 * pairs + 3)
            for i in range(TT):
                if i >= 2:
                    sp.wait_ge(sem("yk_used"), (TOPK - 1) * (i - 1))
                rows_ = y_dram.rearrange("(k t) n -> t k n", k=TOPK)[P * i:P * (i + 1)]
                for h in range(2):
                    k = slice(3 * h, 3 * h + 3)
                    sp.dma_start(yk[i % 2][:, k, :], rows_[:, k, :]).then_inc(sem(f"yk_loaded{i % 2}{h}"), 16)
            for i in range(TT):
                sp.wait_ge(sem("out_ready"), i + 1)
                sp.dma_start(out[0, P * i:P * i + P, :], x[:, i, :]).then_inc(sem("out_stored"), 16)
            sp.wait_ge(sem("out_stored"), 16 * TT)

        @block.gpsimd
        def _(pool):
            g = nc.gpsimd
            chain = [0]

            def link(ins):
                chain[0] += 1
                ins.then_inc(sem("pool_chain"), 1)
                pool.wait_ge(sem("pool_chain"), chain[0])

            g.memset(wsm, 0.0).then_inc(sem("small_cleared"), 1)
            g.memset(epsc[:], EPS)
            link(g.memset(ident[:], 0.0))
            link(g.affine_select(out=ident[:], in_=ident[:], compare_op=ALU.not_equal, fill=1.0, base=0,
                                 pattern=[[-1, P]], channel_multiplier=1))
            link(g.memset(ones[:], 1.0))
            link(g.affine_select(out=causal[:], in_=ones[:], compare_op=ALU.is_ge, fill=0.0, base=0,
                                 pattern=[[1, P]], channel_multiplier=-1))
            link(g.affine_select(out=before[:], in_=ones[:], compare_op=ALU.is_gt, fill=0.0, base=0,
                                 pattern=[[1, P]], channel_multiplier=-1))
            link(g.memset(future[:], 1))
            link(g.affine_select(out=future[:], in_=future[:], compare_op=ALU.is_gt, fill=0.0, base=0,
                                 pattern=[[1, P]], channel_multiplier=-1))
            g.memset(negc[:], NEG_FUTURE)
            g.iota(iota[:], pattern=[[1, P]], base=0, channel_multiplier=0, allow_small_or_imprecise_dtypes=True)
            g.iota(row1[:], pattern=[[P, TT], [T, TOPK]], base=1, channel_multiplier=1,
                   allow_small_or_imprecise_dtypes=True)
            link(g.iota(level_mask[:, 0, :], pattern=[[1, P]], base=0, channel_multiplier=0))
            link(g.iota(level_mask[:, 1, :], pattern=[[0, P]], base=0, channel_multiplier=1))
            link(g.memset(resets, 1.0))
            link(g.memset(resets.rearrange("p (i t) -> p i t", i=TT)[:, :, 0:1], 0.0))
            g.memset(stat[:], 0.0).then_inc(sem("consts"), 1)

            def further_condition(c):
                for h in range(2):
                    loaded(pool, f"adr{c}{h}")
                    w = ring_view(f"adr{c}{h}", 0, 4, 512)
                    weights = cs[:, 4 * h:4 * h + 4].rearrange("p (j o) -> p j o", o=1).to_broadcast([P, 4, 512])
                    link(g.tensor_tensor(w, w, weights, ALU.mult))
                    link(g.tensor_tensor(w[:, 0:2, :], w[:, 0:2, :], w[:, 2:4, :], ALU.add))
                    if h == 0:
                        ins = g.tensor_tensor(cond[c], w[:, 0, :], w[:, 1, :], ALU.add)
                    else:
                        link(g.tensor_tensor(w[:, 0, :], w[:, 0, :], w[:, 1, :], ALU.add))
                        ins = g.tensor_tensor(cond[c], cond[c], w[:, 0, :], ALU.add)
                    ins.then_inc(sem("further_ready"), 1)
                    pool.wait_ge(sem("further_ready"), 2 * c + h + 1)

            pool.wait_ge(sem("hT_ready"), 8)
            pool.wait_ge(sem("small_ready"), 1)
            for t in (qE[0], qE[1], kE[0], kE[1], qcz[0], qcz[1], S):
                ins = g.memset(t, 0.0)
            ins.then_inc(sem("cleared"), 1)
            pool.wait_ge(sem("cs_ready"), 1)
            for c in range(3):
                further_condition(c)

            pool.wait_ge(sem("oTA_ready"), 4)
            pool.wait_ge(sem("mb_ready"), 3)
            g.memset(raw, 0.0)
            g.memset(ones4, 1.0)
            link(g.memset(sel4, 0.0))
            g.affine_select(out=sel4, in_=sel4, compare_op=ALU.not_equal, fill=1.0, base=0,
                            pattern=[[-1, 4], [0, P]], channel_multiplier=1).then_inc(sem("cleared"), 1)
            for c in range(3, 6):
                further_condition(c)

            pool.wait_ge(sem("oTC_ready"), 4)
            g.iota(distv, pattern=[[1, 896]], base=-384, channel_multiplier=-1,
                   allow_small_or_imprecise_dtypes=True)
            g.memset(Dm, NEG_MASK).then_inc(sem("cleared"), 1)
            for c in range(6, 8):
                further_condition(c)

            pool.wait_ge(sem("x2_ready"), 4)
            pool.wait_ge(sem("lists_ready"), 1)
            for b in range(2):
                g.memset(row_of[b][:, :], T * TOPK)
                ins = g.memset(xg[b], 0.0)
            link(ins)
            pool.wait_ge(sem("h_stored"), 16 * TT)
            pool.wait_ge(sem("table_ready"), 1)
            pairs = pool.value_load(npair[0:1, 0:1], min_val=1, max_val=UNITS // 2)

            def gather(b):
                pool.sem_inc(sem("gathers_begun"), 1)
                g.indirect_dma_start(out=xg[b], out_offset=None, in_=h_dram[:, :],
                                     in_offset=bass.IndirectOffsetOnAxis(ap=tok_of[b][:, 0:1], axis=0),
                                     bounds_check=T - 1, oob_is_err=False).then_inc(sem(f"xg_loaded{b}"), 16)

            for b in range(2):
                g.indirect_dma_start(out=y_dram[:, :], out_offset=bass.IndirectOffsetOnAxis(ap=row_of[b][:, 0:1], axis=0),
                                     in_=xg[b], in_offset=None, bounds_check=T * TOPK - 1, oob_is_err=False
                                     ).then_inc(sem(f"y_stored{b}"), 16)
            def copy_list(dst, lists, u, n):
                g.tensor_copy(dst[:, :], lists[:, bass.ds(u, 1)]).then_inc(sem("list_copied"), 1)
                pool.wait_ge(sem("list_copied"), n)

            for b in range(2):
                copy_list(tok_of[b], toks, b, b + 1)
                gather(b)
            with pool.Fori(0, pairs) as i:
                for b in range(2):
                    pool.wait_ge(sem("turned"), 4 * i + 2 * b + 3)
                    copy_list(tok_of[b], toks, 2 * i + b + 2, 4 * i + 2 * b + 3)
                    gather(b)
                    pool.wait_ge(sem(f"y_stored{b}"), 16 * i + 16)
                    copy_list(row_of[b], rows_y, 2 * i + b, 4 * i + 2 * b + 4)
                    pool.wait_ge(sem("y_read"), 4 * i + 2 * b + 6)
                    pool.sem_inc(sem("gathers_begun"), 1)
                    g.indirect_dma_start(out=y_dram[:, :], out_offset=bass.IndirectOffsetOnAxis(ap=row_of[b][:, 0:1], axis=0),
                                         in_=ys[b], in_offset=None, bounds_check=T * TOPK - 1, oob_is_err=False
                                         ).then_inc(sem(f"y_stored{b}"), 16)

        @block.tensor
        def _(pe):
            mm = nc.tensor.matmul
            nxt = [0]

            def begin(name):
                n = nxt[0]
                assert products[n][0] == name, (products[n][0], name)
                nxt[0] += 1
                if n >= BANKS:
                    _, s, v = products[n - BANKS]
                    pe.wait_ge(sem(s), v)
                return bank[n % BANKS]

            def end(ins):
                ins.then_inc(sem("products_done"), 1)

            pe.wait_ge(sem("consts"), 1)
            pe.wait_ge(sem("consts_loaded"), NCONST[0])
            b = begin("params")
            end(nc.tensor.transpose(b[:, 0:53], prow[0:53, :], ident[0:53, 0:53]))
            def column_sums(name, c, sums):
                b = begin(name)
                pe.wait_ge(sem("cond_ready" if c < 4 else "further_ready"), 2 * (c % 4 if c < 4 else c - 4) + 2)
                for m in range(4):
                    ins = mm(b[:, m:m + 1], sums[:, tile_cols(m)], ones[:, 0:1], start=True, stop=True)
                end(ins)

            for c in range(4):
                column_sums(f"mc{c}", c, cond0[c % 2])
            for j in range(8):
                pe.wait_ge(sem("xn_ready"), TT)
                b = begin(f"xT{j}")
                for i in range(TT):
                    ins = nc.tensor.transpose(b[:, tile_cols(i)], xn[:, i, tile_cols(j)], ident[:, :])
                end(ins)

            def triple(out, n, weights, tokens, weights_left=True, name=None):
                if name:
                    split_wait(pe, name, "hi_split")
                for j in range(n):
                    for k in range(2):
                        w, t = weights(j)[0], tokens(j)[k]
                        mm(out, w if weights_left else t, t if weights_left else w, start=(j == 0 and k == 0), stop=False)
                if name:
                    split_wait(pe, name, "lo_split")
                for j in range(n):
                    w, t = weights(j)[1], tokens(j)[0]
                    ins = mm(out, w if weights_left else t, t if weights_left else w, start=False, stop=(j == n - 1))
                end(ins)

            def project(name, piece, m, hi=None, lo=None):
                b = begin(name)
                if piece:
                    n = size_of(piece) // 8
                    hi, lo = hi_view(piece, 8, n), lo_view(piece, 8, n)

                def tokens(j):
                    if name == "small":
                        pe.wait_ge(sem("hT_lo_ready"), j + 1)
                    return hT_hi[:, j, :], hT_lo[:, j, :]

                triple(b[:, :], 8, lambda j: (hi[:, j, tile_cols(m)], lo[:, j, tile_cols(m)]), tokens, name=piece)

            def project_rows(name, piece, i):
                b = begin(name)
                hi, lo = hi_view(piece, 8, 256), lo_view(piece, 8, 256)
                triple(b[:, 0:256], 8, lambda j: (hi[:, j, :], lo[:, j, :]),
                       lambda j: (hT_hi[:, j, tile_cols(i)], hT_lo[:, j, tile_cols(i)]), False, piece)

            pe.wait_ge(sem("wsm_ready"), 1)
            project("small", None, 0, wsm_hi, wsm_lo)
            pe.wait_ge(sem("small_ready"), 1)
            for f in range(2):
                b = begin(f"la{f}")
                end(mm(b[:, :], w_a2[:, tile_cols(f)], small[0:16, :], start=True, stop=True))
            for f in range(2):
                project(f"qa{f}", "w_qa", f)
            for f in range(2):
                project(f"ka{f}", "w_ka", f)
            for q in range(2):
                for i in range(TT):
                    project_rows(f"va{q}{i}", f"w_va{q}", i)
            pe.wait_ge(sem("kd_ready"), 1)
            kd = decay
            for f in range(2):
                b = begin(f"kd{f}")
                for i in range(TT):
                    ins = nc.tensor.transpose(b[:, tile_cols(i)], kd[:, f, tile_cols(i)], ident[:, :])
                end(ins)
            pe.wait_ge(sem("kdr_ready"), 2)
            pe.wait_ge(sem("v_ready"), 8)
            for i in range(3):
                for f in range(2):
                    b = begin(f"st{i}{f}")
                    end(mm(b[:, 0:256], kdr[:, i, f, :], va[:, i, 256 * f:256 * f + 256], start=True, stop=True))
            for l in range(8):
                if l < 7:
                    pe.wait_ge(sem("level_ready"), l + 1)
                    ksrc, qsrc = kE[l % 2], qE[l % 2]
                else:
                    ksrc, qsrc = kT, qT
                for g in range(4):
                    p0, tp = 64 * (g // 2), g % 2
                    b = begin(f"scA{l}{g}")
                    for ii in range(2):
                        for f in range(2):
                            t = tile_cols(2 * tp + ii)
                            ins = mm(b[:, tile_cols(2 * ii + f)], ksrc[p0:p0 + 64, f, t], qsrc[p0:p0 + 64, f, t],
                                     start=True, stop=True)
                    end(ins)
            for m in range(4):
                project(f"ga{m}", f"w_ga{m // 2}", m % 2)
            pe.wait_ge(sem("state_ready"), 6)
            pe.wait_ge(sem("intra_done"), 32)
            for h in range(5):
                if h < 4:
                    b = begin(f"oA{h}")
                    for i in range(TT):
                        if i:
                            mm(b[:, tile_cols(i)], state[:, i - 1, h // 2, :], qcz[h % 2][:, h // 2, tile_cols(i)],
                               start=True, stop=False)
                        ins = mm(b[:, tile_cols(i)], va[:, i, tile_cols(h)], S[:, h % 2, i, h // 2, :],
                                 start=(i == 0), stop=True)
                    end(ins)
                if h:
                    pe.wait_ge(sem("squares_ready"), h)
                    b = begin(f"msA{h - 1}")
                    end(mm(b[:, :], ones[:, :], sqA, start=True, stop=True))

            for c in range(3):
                column_sums(f"mb{c}", 4 + c, cond[c])
            for f in range(4):
                project(f"qk{f}", f"w_qkc{f // 2}", f % 2)
            pe.wait_ge(sem("scans_ready"), 1)
            b = begin("uT")
            for i in range(TT):
                ins = nc.tensor.transpose(b[:, 4 * i:4 * i + 4], g4[3][:, tile_cols(i)], ident[0:4, 0:4])
            end(ins)
            for q in range(2):
                for i in range(TT):
                    project_rows(f"vc{q}{i}", f"w_vc{q}", i)
            for m in range(4):
                project(f"oc{m}", f"w_oc{m // 2}", m % 2)
            pe.wait_ge(sem("cleared"), 2)
            pe.wait_ge(sem("qkc_ready"), 4)
            pe.wait_ge(sem("v_ready"), 16)
            def mean_square(h):
                pe.wait_ge(sem("squares_ready"), h + 5)
                b = begin(f"msC{h}")
                end(mm(b[:, :], ones[:, :], sqC, start=True, stop=True))

            for h in range(4):
                p0, f = 64 * (h % 2), h // 2
                b = begin(f"bm{h}")
                end(mm(b[:, :], sel4[:, h, :], g4[4], start=True, stop=True))
                b = begin(f"bt{h}")
                end(mm(b[:, :], sel4[:, h, :], g4[5], start=True, stop=True))
                for j in range(TT):
                    b = begin(f"scC{h}{j}")
                    end(mm(b[:, P * j:T], qkc[p0:p0 + 64, 2 + f, tile_cols(j)], qkc[p0:p0 + 64, f, P * j:T],
                           start=True, stop=True))
                if h:
                    mean_square(h - 1)
                if h == 0:
                    pe.wait_ge(sem("wki_ready"), 1)
                    b = begin("kidx")
                    triple(b[0:32, :], 8, lambda j: (wki_hi[:, j, :], wki_lo[:, j, :]),
                           lambda j: (hT_hi[:, j, :], hT_lo[:, j, :]))
                else:
                    project(f"cl{h - 1}", f"w_cl{(h - 1) // 2}", (h - 1) % 2)
                b = begin(f"num{h}")
                for j in range(TT):
                    pe.wait_ge(sem("SW_ready"), 4 * h + j + 1)
                    ins = mm(b[:, P * j:T], vc[:, j, tile_cols(h)], SW[:, j, P * j:T], start=(j == 0), stop=(j == 3))
                end(ins)
                b = begin(f"den{h}")
                for j in range(TT):
                    ins = mm(b[:, P * j:T], ones[:, :], SW[:, j, P * j:T], start=(j == 0), stop=(j == 3))
                end(ins)
            mean_square(3)

            pe.wait_ge(sem("squares_ready"), 11)
            b = begin("msq")
            for k in range(2):
                ins = mm(b[:, :], ones[:, :], sqB[:, k, :], start=(k == 0), stop=(k == 1))
            end(ins)
            b = begin("mskv")
            end(mm(b[:, :], ones[:, :], sqB[:, 2, :], start=True, stop=True))
            pe.wait_ge(sem("wi0_ready"), 1)
            b = begin("wi")
            for i in range(TT):
                ins = nc.tensor.transpose(b[:, 8 * i:8 * i + 8], wi0[:, tile_cols(i)], ident[0:8, 0:8])
            end(ins)
            pe.wait_ge(sem("extra_loaded"), 64)
            b = begin("uk")
            for m in range(4):
                ins = nc.tensor.transpose(b[:, tile_cols(m)], w_uk[:, tile_cols(m)], ident[:, :])
            end(ins)
            pe.wait_ge(sem("cn_ready"), 2)
            b = begin("ckr")
            for i in range(TT):
                ins = nc.tensor.transpose(b[:, tile_cols(i)], cn[:, 2, tile_cols(i)], ident[:, :])
            end(ins)
            for m in range(2):
                b = begin(f"qi{m}")
                for k in range(2):
                    ins = mm(b[:, :], w_qi[:, k, tile_cols(m)], cn[:, k, :], start=(k == 0), stop=(k == 1))
                end(ins)
            pe.wait_ge(sem("qi_ready"), 2)
            pe.wait_ge(sem("kidx_ready"), 1)
            for i in range(1, TT):
                for h in range(8):
                    p0 = 32 * (h % 4)
                    b = begin(f"ix{i}{h}")
                    end(mm(b[:, 0:P * (i + 1)], qiT[p0:p0 + 32, h // 4, tile_cols(i)],
                           kidxT[p0:p0 + 32, 0:P * (i + 1)], start=True, stop=True))
            for m in range(4):
                b = begin(f"q{m}")
                for k in range(2):
                    ins = mm(b[:, :], w_uq[:, k, tile_cols(m)], cn[:, k, :], start=(k == 0), stop=(k == 1))
                end(ins)
            for c in range(3, 8):
                column_sums(f"mb{c}", 4 + c, cond[c])
            pe.wait_ge(sem("ukT_ready"), 1)
            for h in range(8):
                p0 = 64 * (h % 2)
                pe.wait_ge(sem("q_ready"), h // 2 + 1)
                b = begin(f"ql{h}")
                end(mm(b[:, :], ukT[p0:p0 + 64, h // 2, :], qTb[p0:p0 + 64, h // 2, :], start=True, stop=True))
            npt = 0
            for n in range(-1, 8):
                if n < 7:
                    i, g = divmod(n + 1, 2)
                    for h in range(4 * g, 4 * g + 4):
                        pe.wait_ge(sem("ql_ready"), h + 1)
                        b = begin(f"lg{i}{h}")
                        end(mm(b[:, 0:P * (i + 1)], qlT[:, h, tile_cols(i)], cn[:, 2, 0:P * (i + 1)],
                               start=True, stop=True))
                if n < 0:
                    continue
                i, g = divmod(n, 2)
                pe.wait_ge(sem("P_ready"), n + 1)
                for j in range(i + 1):
                    b = begin(f"pt{i}{g}{j}")
                    for h in range(4):
                        ins = nc.tensor.transpose(b[:, tile_cols(h)], Pn[:, 4 * g + h, tile_cols(j)], ident[:, :])
                    end(ins)
                b = begin(f"ol{i}{g}")
                for j in range(i + 1):
                    npt += 1
                    pe.wait_ge(sem("PT_ready"), npt)
                    ins = mm(b[:, :], ckr[:, j, :], PT[:, j, :], start=(j == 0), stop=(j == i))
                end(ins)
            pe.wait_ge(sem("ol_ready"), 8)
            for m in range(4):
                b = begin(f"ob{m}")
                for q in range(2):
                    h = 2 * m + q
                    ins = mm(b[64 * q:64 * q + 64, :], w_uv[:, 64 * h:64 * h + 64], olT[:, h, :], start=True, stop=True)
                end(ins)

            for n, (m, br) in enumerate(merge_steps()):
                for r in range(2):
                    project(f"gate{m + r}{br}", f"wg{n}", r)
                hi, lo = hi_view(f"wu{n}", 4, 256), lo_view(f"wu{n}", 4, 256)
                pe.wait_ge(sem("oT_lo_ready"), br + 1)
                for r in range(2):
                    b = begin(f"up{m + r}{br}")
                    triple(b[:, :], 4, lambda j: (hi[:, j, tile_cols(r)], lo[:, j, tile_cols(r)]),
                           lambda j: (oT_hi[br][:, j, :], oT_lo[br][:, j, :]), name=f"wu{n}")
                if n < 8:
                    b = begin(f"mr{n}")
                    pe.wait_ge(sem("diag_ready"), n + 1)
                    end(mm(b[:, :], ones[:, :], cond_merge[n % 2], start=True, stop=True))
            pe.wait_ge(sem("mT_lo_ready"), 8)
            for i, q in wo_order():
                b = begin(f"wo{i}{q}")
                hi, lo = hi_view(f"wo{q}", 8, 256), lo_view(f"wo{q}", 8, 256)
                triple(b[:, 0:256], 8, lambda j: (hi[:, j, :], lo[:, j, :]),
                       lambda j: (mT_hi[:, j, tile_cols(i)], mT_lo[:, j, tile_cols(i)]), False, f"wo{q}")

            pe.wait_ge(sem("h2_ready"), TT)
            for j in range(8):
                b = begin(f"hT2{j}")
                for i in range(TT):
                    src = h2[:, i, :].rearrange("t (p j) -> t j p", j=8)[:, j, :]
                    ins = nc.tensor.transpose(b[:, tile_cols(i)], src, ident[:, :])
                end(ins)
            loaded(pe, "w_rt")
            rw = ring_view("w_rt", 0, 8, E)
            pe.wait_ge(sem("h2T_ready"), 8)
            for i in range(TT):
                b = begin(f"rt{i}")
                for j in range(8):
                    ins = mm(b[:, 0:E], hT[:, j, tile_cols(i)], rw[:, j, :], start=(j == 0), stop=(j == 7))
                end(ins)
            loaded(pe, "w_shg")
            loaded(pe, "w_shu")
            wg, wu = ring_view("w_shg", 0, 8, 256), ring_view("w_shu", 0, 8, 256)

            def shared_up(name, w, m):
                b = begin(name)
                for j in range(8):
                    ins = mm(b[:, :], w[:, j, :].rearrange("p (f m) -> p m f", m=2)[:, m, :], hT[:, j, :],
                             start=(j == 0), stop=(j == 7))
                end(ins)

            shared_up("sg0", wg, 0)
            shared_up("su0", wu, 0)
            pe.wait_ge(sem("mall_ready"), TT)
            b = begin("tot")
            for q in range(TT):
                ins = mm(b[:, 0:E], ones[:, :], mall[:, q, :], start=(q == 0), stop=(q == TT - 1))
            end(ins)
            shared_up("sg1", wg, 1)
            pe.wait_ge(sem("uend_ready"), 1)
            b = begin("ue")
            end(nc.tensor.transpose(b[0:E, 0:P], uend, ident[:, :]))
            pe.wait_ge(sem("ucmp_ready"), 1)
            b = begin("uc")
            end(mm(b[0:1, 0:96], ones[0:E, 0:1], ucmp[:, :], start=True, stop=True))
            for i in range(TT):
                pe.wait_ge(sem("mall_ready"), TT)
                b = begin(f"pos{i}")
                for q in range(i + 1):
                    ins = mm(b[:, 0:E], before[:, :] if q == i else ones[:, :], mall[:, q, :],
                             start=(q == 0), stop=(q == i))
                end(ins)
            b = begin("lists")
            for i in range(TT):
                pe.wait_ge(sem("place_ready"), i + 1)
                for k in range(TOPK):
                    ins = mm(b[:, 0:LISTS], is_row[i % 2][:, k, :], is_unit[i % 2][:, k, :], start=(i == 0 and k == 0),
                             stop=(i == TT - 1 and k == TOPK - 1))
                ins.then_inc(sem("place_used"), 1) if i < TT - 1 else end(ins)
            shared_up("su1", wu, 1)
            loaded(pe, "w_shd")
            wd = ring_view("w_shd", 0, 2, D)
            pe.wait_ge(sem("actS_ready"), 2)
            for i in range(TT):
                for n in range(2):
                    b = begin(f"sd{i}{n}")
                    for m in range(2):
                        ins = mm(b[:, :], actS[:, m, tile_cols(i)], wd[:, m, 512 * n:512 * n + 512],
                                 start=(m == 0), stop=(m == 1))
                    end(ins)
            assert nxt[0] == len(products)

            for _, s, v in products[-BANKS:]:
                pe.wait_ge(sem(s), v)
            pe.wait_ge(sem("table_ready"), 1)
            pairs = pe.value_load(npair[0:1, 0:1], min_val=1, max_val=UNITS // 2)

            def turn(c, half):
                rows = xg[c].rearrange("t (p j) -> t j p", j=8)
                for q in range(4):
                    ins = nc.tensor.transpose(bank[half][:, tile_cols(q)], rows[:, 4 * half + q, :], ident[:, :])
                ins.then_inc(sem("turned"), 1)

            pe.wait_ge(sem("xg_loaded0"), 16)
            turn(0, 0)
            turn(0, 1)
            with pe.Fori(0, pairs) as i:
                for b in range(2):
                    c, u = 1 - b, 2 * i + b
                    out_gu = bank[2][:, :].rearrange("p (g f) -> p g f", g=2)
                    for k in range(2):
                        hi, lo = (w[b][k].rearrange("p (g j f) -> p g j f", g=2, j=4) for w in (w_hi, w_lo))
                        pe.wait_ge(sem("xe_hi_ready"), 2 * u + k + 1)
                        pe.wait_ge(sem("xe_lo_ready"), 2 * u + k + 1)
                        pe.wait_ge(sem("hi_ready"), 3 * u + k + 1)
                        for j in range(4):
                            for x_, t in enumerate((xe_hi, xe_lo)):
                                mm(out_gu, t[b][:, tile_cols(4 * k + j)], hi[:, :, j, :],
                                   start=(k == 0 and j == 0 and x_ == 0), stop=False)
                        pe.wait_ge(sem("lo_ready"), 3 * u + k + 1)
                        for j in range(4):
                            ins = mm(out_gu, xe_hi[b][:, tile_cols(4 * k + j)], lo[:, :, j, :], start=False,
                                     stop=(k == 1 and j == 3))
                        ins.then_inc(sem("piece_used"), 1)
                    pe.wait_ge(sem(f"xg_loaded{c}"), 16 * (i + b + 1))
                    turn(c, 0)
                    pe.wait_ge(sem("acte_ready"), u + 1)
                    rows = acte[b].rearrange("t (p m) -> t m p", m=2)
                    for m in range(2):
                        ins = nc.tensor.transpose(bank[3][:, tile_cols(m)], rows[:, m, :], ident[:, :])
                    ins.then_inc(sem("acte_turned"), 1)
                    turn(c, 1)
                    hi, lo = (w[b][2].rearrange("p (m n) -> p m n", m=2) for w in (w_hi, w_lo))
                    pe.wait_ge(sem("ae_hi_ready"), u + 1)
                    pe.wait_ge(sem("ae_lo_ready"), u + 1)
                    pe.wait_ge(sem("hi_ready"), 3 * u + 3)
                    pe.wait_ge(sem("lo_ready"), 3 * u + 3)
                    pe.wait_ge(sem("y_read"), 2 * u + 2)
                    for n in range(2):
                        terms = [(t[b][:, m, :], w[:, m, 512 * n:512 * n + 512]) for m in range(2)
                                 for t, w in ((ae_hi, hi), (ae_lo, hi), (ae_hi, lo))]
                        for q, (s_, w) in enumerate(terms):
                            ins = mm(bank[4 + 2 * b + n][:, :], s_, w, start=(q == 0), stop=(q == 5))
                        ins.then_inc(sem("piece_used" if n else "y_begun"), 1)

        @block.scalar
        def _(act):
            A = nc.scalar.activation
            chain = [0]

            def link(ins):
                chain[0] += 1
                ins.then_inc(sem("act_chain"), 1)
                act.wait_ge(sem("act_chain"), chain[0])

            act.wait_ge(sem("consts"), 1)
            act.wait_ge(sem("consts_loaded"), NCONST[0])
            A(cs[:, :], c_in[:, :], ACT.Silu).then_inc(sem("cs_ready"), 1)
            act.wait_ge(sem("x_loaded"), 16)
            for i in range(TT):
                link(A(junk, x[:, i, :], ACT.Square, accum_out=stat[:, i:i + 1]))
            A(stat[:, 4:8], stat[:, 0:4], ACT.Sqrt, scale=1.0 / D, bias=epsc[:, 0:1]).then_inc(sem("rms_ready"), 1)
            act.wait_ge(sem("rstd_ready"), 1)
            for i in range(TT):
                A(xn[:, i, :], x[:, i, :], ACT.Copy, scale=stat[:, 8 + i:9 + i]).then_inc(sem("xn_ready"), 1)

            def split_hi(name):
                loaded(act, name)
                n = size_of(name)
                A(hi_view(name, 1, n), ring_view(name, 0, 1, n), ACT.Copy).then_inc(sem("hi_split"), 1)

            act.wait_ge(sem("consts_loaded"), NCONST[0])
            A(wsm_hi, wsm, ACT.Copy).then_inc(sem("wsm_hi_ready"), 1)
            for name in ("w_qa", "w_ka", "w_va0"):
                split_hi(name)
            act.wait_ge(sem("mod1_ready"), 1)
            for j in range(8):
                b = done(act, f"xT{j}")
                if j >= 2:
                    act.wait_ge(sem("hT_lo_ready"), j - 1)
                A(h32[j % 2], b[:, :], ACT.Identity, scale=mod1[:, j:j + 1], bias=mod1[:, 8 + j:9 + j]
                  ).then_inc(sem("h32_ready"), 1)
                A(hT_hi[:, j, :], b[:, :], ACT.Identity, scale=mod1[:, j:j + 1], bias=mod1[:, 8 + j:9 + j]
                  ).then_inc(sem("hT_ready"), 1)
            b = done(act, "small")
            A(small[:, :], b[:, :], ACT.Copy).then_inc(sem("small_ready"), 1)
            for f in range(2):
                act.wait_ge(sem("z_ready"), f + 1)
                link(A(decay[:, f, :], arg[0][:, f, :], ACT.Abs))
                link(A(decay[:, f, :], decay[:, f, :], ACT.Exp, scale=-1.0))
                A(decay[:, f, :], decay[:, f, :], ACT.Ln, bias=1.0).then_inc(sem("lnz_ready"), 1)
            for f in range(2):
                b = done(act, f"qa{f}")
                A(qT[:, f, :], b[:, :], ACT.Copy, scale=0.125).then_inc(sem("qa_ready"), 1)
            split_hi("w_va1")
            act.wait_ge(sem("cum_ready"), 1)
            A(ecum, cum, ACT.Exp).then_inc(sem("ecum_ready"), 1)
            act.wait_ge(sem("kdarg_ready"), 1)
            A(decay, arg[0], ACT.Exp).then_inc(sem("kdE_ready"), 1)
            for f in range(2):
                b = done(act, f"kd{f}")
                A(kdr[:, :, f, :], b[:, :].rearrange("p (i k) -> p i k", i=TT), ACT.Copy).then_inc(sem("kdr_ready"), 1)
            for l in range(7):
                act.wait_ge(sem("arg_ready"), l + 1)
                if l:
                    act.wait_ge(sem("level_ready"), l)
                else:
                    act.wait_ge(sem("products_done"), number["kd1"] + 1)
                A(decay, arg[l % 2], ACT.Exp).then_inc(sem("E_ready"), 1)
                if l in (2, 3):
                    split_hi(f"w_ga{l - 2}")
            for m in range(4):
                b = done(act, f"ga{m}")
                A(sga[:, m, :], b[:, :], ACT.Silu).then_inc(sem("outgate_ready"), 1)
            split_hi("w_qkc0")
            split_hi("w_qkc1")
            for h in range(5):
                if h < 4:
                    b = done(act, f"oA{h}")
                    if h:
                        b1 = done(act, f"msA{h - 1}")
                        if h == 3:
                            act.wait_ge(sem("oA_read"), 1)
                        A(rsA[(h - 1) % 2], b1[:, :], ACT.Sqrt, scale=1.0 / P,
                          bias=epsc[:, 0:1]).then_inc(sem("root_ready"), 1)
                    A(sqA, b[:, :], ACT.Square).then_inc(sem("squares_ready"), 1)
                else:
                    b = done(act, "msA3")
                    act.wait_ge(sem("oA_read"), 2)
                    A(rsA[1], b[:, :], ACT.Sqrt, scale=1.0 / P, bias=epsc[:, 0:1]).then_inc(sem("root_ready"), 1)

            act.wait_ge(sem("oTA_ready"), 4)
            act.wait_ge(sem("fb_ready"), 1)
            link(A(g4[1], g4[0], ACT.Abs))
            link(A(g4[1], g4[1], ACT.Exp, scale=-1.0))
            A(g4[1], g4[1], ACT.Ln, bias=1.0).then_inc(sem("lnf_ready"), 1)
            split_hi("w_vc0")
            split_hi("w_vc1")
            for f in range(4):
                act.wait_ge(sem("conv_ready"), f + 1)
                A(qkc[:, f, :], qkc[:, f, :], ACT.Silu).then_inc(sem("qkc_ready"), 1)
            split_hi("w_oc0")
            split_hi("w_oc1")
            for m in range(4):
                b = done(act, f"oc{m}")
                A(soc[:, m, :], b[:, :], ACT.Sigmoid).then_inc(sem("outgate_ready"), 1)
            A(wki_hi[:, :, :], wki[:, :, :], ACT.Copy).then_inc(sem("wki_hi_ready"), 1)
            split_hi("w_cl0")

            def root_c(h):
                b = done(act, f"msC{h}")
                if h:
                    act.wait_ge(sem("oTC_ready"), h)
                A(rsC, b[:, :], ACT.Sqrt, scale=1.0 / P, bias=epsc[:, 0:1]).then_inc(sem("root_ready"), 1)

            for h in range(4):
                b = done(act, f"bt{h}")
                if h:
                    act.wait_ge(sem("den_read"), h)
                A(floor_, b[:, :], ACT.Exp, scale=-1.0).then_inc(sem("floor_ready"), 1)
                for j in range(TT):
                    n = 4 * h + j
                    act.wait_ge(sem("argC_ready"), n + 1)
                    if n >= 2:
                        act.wait_ge(sem("SW_ready"), n - 1)
                    A(W[n % 2][:, 0:T - P * j], argC[n % 2][:, 0:T - P * j], ACT.Exp, scale=-1.0).then_inc(sem("W_ready"), 1)
                    if h and j == 1:
                        root_c(h - 1)
                act.wait_ge(sem("hC_ready"), h + 1)
                if h:
                    act.wait_ge(sem("products_done"), number[f"msC{h - 1}"] + 1)
                A(sqC, hC, ACT.Square).then_inc(sem("squares_ready"), 1)
                if h == 0:
                    split_hi("w_cl1")
                    b = done(act, "kidx")
                    for q in range(4):
                        ins = A(kidxT[32 * q:32 * q + 32, :], b[0:32, :], ACT.Copy)
                    ins.then_inc(sem("kidx_ready"), 1)
            root_c(3)

            act.wait_ge(sem("oTC_ready"), 4)
            for n in range(3):
                act.wait_ge(sem("craw_ready"), n + 1)
                A(sqB[:, n, :], craw[:, n, :], ACT.Square).then_inc(sem("squares_ready"), 1)
            for n, name in enumerate(("msq", "mskv")):
                b = done(act, name)
                A(rsB[:, n, :], b[:, :], ACT.Sqrt, scale=1.0 / (256, 128)[n], bias=epsc[:, 0:1]).then_inc(sem("root_ready"), 1)
            b = done(act, "ckr")
            A(ckr, b[:, :].rearrange("p (i k) -> p i k", i=TT), ACT.Copy).then_inc(sem("ckr_ready"), 1)
            for m in range(2):
                b = done(act, f"qi{m}")
                A(qiT[:, m, :], b[:, :], ACT.Copy, scale=float(32 ** -0.5)).then_inc(sem("qi_ready"), 1)
            for i in range(1, TT):
                for h in range(8):
                    n = 8 * (i - 1) + h
                    b = done(act, f"ix{i}{h}")
                    if n >= 2:
                        act.wait_ge(sem("relu_used"), n - 1)
                    A(rl[n % 2][:, 0:P * (i + 1)], b[:, 0:P * (i + 1)], ACT.Relu).then_inc(sem("relu_ready"), 1)
            for m in range(4):
                b = done(act, f"q{m}")
                A(qTb[:, m, :], b[:, :], ACT.Copy).then_inc(sem("q_ready"), 1)
            for h in range(8):
                b = done(act, f"ql{h}")
                A(qlT[:, h, :], b[:, :], ACT.Copy, scale=0.125).then_inc(sem("ql_ready"), 1)
            for n in range(-1, 8):
                for k in range(4):
                    if n < 7:
                        i, g = divmod(n + 1, 2)
                        h, e = 4 * g + k, 4 * n + 4 + k
                        act.wait_ge(sem("nmax_ready"), e + 1)
                        if i:
                            act.wait_ge(sem("products_done"), number[f"pt{i - 1}{g}{i - 1}"] + 1)
                        A(Pn[:, h, 0:P * (i + 1)], L[e % 2][:, 0:P * (i + 1)], ACT.Exp, bias=nmax[:, h:h + 1],
                          accum_out=psum[:, h:h + 1]).then_inc(sem("exp_ready"), 1)
                    i, g = divmod(n, 2)
                    if n >= 0 and k <= i:
                        b = done(act, f"pt{i}{g}{k}")
                        if n:
                            act.wait_ge(sem("products_done"), number[f"ol{(n - 1) // 2}{1 - g}"] + 1)
                        A(PT[:, k, :], b[:, :], ACT.Copy).then_inc(sem("PT_ready"), 1)
                if n == 4:
                    split_hi("wg0")
                    split_hi("wu0")
            for m in range(4):
                b = done(act, f"ob{m}")
                A(oT[1][:, m, :], b[:, :], ACT.Copy).then_inc(sem("oTB_ready"), 1)

            act.wait_ge(sem("oTB_ready"), 4)
            for br in range(3):
                A(oT_hi[br], oT[br][:, :, :], ACT.Copy).then_inc(sem("oT_hi_ready"), 1)
            for n, (m, br) in enumerate(merge_steps()):
                names = (f"wg{n + 1}", f"wu{n + 1}") if n < 11 else ("wo0", "wo1")
                split_hi(names[0])
                for r in range(2):
                    b = done(act, f"gate{m + r}{br}")
                    if n:
                        act.wait_ge(sem("up_read"), 2 * n + r - 1)
                    A(sgate[r], b[:, :], ACT.Sigmoid).then_inc(sem("gate_ready"), 1)
                split_hi(names[1])
                if br == 2:
                    for r in range(2):
                        act.wait_ge(sem("mT_ready"), m + r + 1)
                        A(mT_hi[:, m + r, :], mT[:, m + r, :], ACT.Copy).then_inc(sem("mT_hi_ready"), 1)
            split_hi("wo2")
            split_hi("wo3")
            for i in range(TT):
                act.wait_ge(sem("x2_ready"), i + 1)
                link(A(sqx, x[:, i, :], ACT.Square, accum_out=stat[:, 8 + i:9 + i]))
                A(stat[:, 12 + i:13 + i], stat[:, 8 + i:9 + i], ACT.Sqrt, scale=1.0 / D, bias=epsc[:, 0:1]).then_inc(sem("rms_ready"), 1)
            for j in range(8):
                b = done(act, f"hT2{j}")
                A(hT[:, j, :], b[:, :], ACT.Copy).then_inc(sem("h2T_ready"), 1)
            for i in range(TT):
                b = done(act, f"rt{i}")
                A(score[:, i, :], b[:, 0:E], ACT.Sigmoid).then_inc(sem("rt_ready"), 1)
            for m in range(2):
                b = done(act, f"sg{m}")
                A(sgS[m], b[:, :], ACT.Silu).then_inc(sem("sg_ready"), 1)

            act.wait_ge(sem("table_ready"), 1)
            pairs = act.value_load(npair[0:1, 0:1], min_val=1, max_val=UNITS // 2)

            def weights_hi(v, c, k):
                act.wait_ge(sem(f"w_loaded{c}{k}"), v)
                A(w_hi[c][k], w_raw[c][k], ACT.Copy).then_inc(sem("hi_ready"), 1)

            def turned(u, c, half):
                act.wait_ge(sem("turned"), 2 * u + half + 4)
                A(xe_hi[c][:, 512 * half:512 * half + 512], bank[half][:, :], ACT.Copy).then_inc(sem("xe_hi_ready"), 1)

            for k in range(3):
                weights_hi(32 if k < 2 else 16, 0, k)
            act.wait_ge(sem("x_added"), 8)
            for half in range(2):
                turned(-1, 0, half)
            with act.Fori(0, pairs) as i:
                for b in range(2):
                    c, u = 1 - b, 2 * i + b
                    for k in range(2):
                        weights_hi(32 * (i + b) + 32, c, k)
                    act.wait_ge(sem("piece_used"), 3 * u + 8)
                    A(sge[b], bank[2][:, 0:FF], ACT.Silu).then_inc(sem("sge_ready"), 1)
                    turned(u, c, 0)
                    act.wait_ge(sem("acte_turned"), u + 1)
                    A(ae_hi[b], bank[3][:, 0:FF].rearrange("p (m t) -> p m t", m=2), ACT.Copy
                      ).then_inc(sem("ae_hi_ready"), 1)
                    turned(u, c, 1)
                    weights_hi(16 * (i + b) + 16, c, 2)
                    act.wait_ge(sem(f"y_stored{b}"), 16 * i + 16)
                    for n in range(2):
                        if n:
                            act.wait_ge(sem("piece_used"), 3 * u + 9)
                        else:
                            act.wait_ge(sem("y_begun"), u + 1)
                        A(ys[b][:, 512 * n:512 * n + 512], bank[4 + 2 * b + n][:, :], ACT.Copy).then_inc(sem("y_read"), 1)
            def first_choice(i):
                act.wait_ge(sem(f"yk_loaded{i % 2}0"), 16 * (i // 2 + 1))
                if i >= 2:
                    act.wait_ge(sem("x4_ready"), i - 1)
                A(routed[i % 2], yk[i % 2][:, 0, :], ACT.Copy, scale=wk[:, i, 0:1]).then_inc(sem("first_ready"), 1)

            first_choice(0)
            for i in range(TT):
                if i < TT - 1:
                    first_choice(i + 1)
                act.wait_ge(sem("x4_ready"), i + 1)
                link(A(sq_out, x[:, i, :], ACT.Square, accum_out=stat[:, i:i + 1]))
                A(stat[:, 4 + i:5 + i], stat[:, i:i + 1], ACT.Sqrt, scale=1.0 / D, bias=epsc[:, 0:1]).then_inc(sem("rms_ready"), 1)

        @block.vector
        def _(dve):
            v = nc.vector
            chain = [0]

            def link(ins):
                chain[0] += 1
                ins.then_inc(sem("dve_chain"), 1)
                dve.wait_ge(sem("dve_chain"), chain[0])

            dve.wait_ge(sem("consts"), 1)
            link(v.tensor_tensor(level_mask[:, 7, :], level_mask[:, 0, :], level_mask[:, 1, :], ALU.bitwise_xor))
            b = level_mask[:, 0, :]
            link(v.tensor_copy(b, before[:, :]))
            link(v.memset(level_mask[:, 6, :], 1000))
            link(v.copy_predicated(level_mask[:, 6, :], b, level_mask[:, 7, :]))
            for l in range(6):
                v.tensor_scalar(level_mask[:, l, :], level_mask[:, 6, :], float(P >> l), None, ALU.is_lt)
            link(v.tensor_scalar(level_mask[:, 7, :], level_mask[:, 7, :], 0.0, None, ALU.is_equal))
            link(v.tensor_scalar(level_mask[:, 6, :], level_mask[:, 6, :], 2.0, None, ALU.is_lt))

            dve.wait_ge(sem("consts_loaded"), NCONST[0])
            b = done(dve, "params")
            v.tensor_copy(par[:, :], b[:, 0:53]).then_inc(sem("params_ready"), 1)
            dve.wait_ge(sem("params_ready"), 1)
            dve.wait_ge(sem("rms_ready"), 1)
            v.reciprocal(stat[:, 8:12], stat[:, 4:8]).then_inc(sem("rstd_ready"), 1)
            def condition(halves, out):
                for h in range(2):
                    w = halves(h)
                    for j in range(4):
                        k = 4 * h + j
                        if k == 0:
                            ins = v.tensor_scalar(out, w[:, 0, :], cs[:, 0:1], None, ALU.mult)
                        else:
                            ins = v.scalar_tensor_tensor(out=out, in0=w[:, j, :], scalar=cs[:, k:k + 1], in1=out,
                                                         op0=ALU.mult, op1=ALU.add)
                        if j < 3:
                            link(ins)
                    cond_count[0] += 1
                    ins.then_inc(sem("cond_ready"), 1)
                    dve.wait_ge(sem("cond_ready"), cond_count[0])

            cond_count = [0]

            def further_columns(c):
                b = done(dve, f"mb{c}")
                v.tensor_copy(modcol[:, 4 * c:4 * c + 4], b[:, 0:4]).then_inc(sem("mb_ready"), 1)

            def split_lo(name):
                n = size_of(name)
                split_wait(dve, name, "hi_split")
                v.tensor_tensor(lo_view(name, 1, n), ring_view(name, 0, 1, n), hi_view(name, 1, n).bitcast(F32),
                                ALU.subtract).then_inc(sem("lo_split"), 1)

            dve.wait_ge(sem("cs_ready"), 1)
            for c in range(4):
                dve.wait_ge(sem(f"ada_loaded{c % 3}"), 32 if c == 3 else 16)
                if c >= 2:
                    done(dve, f"mc{c - 2}")
                condition(lambda h: adaw[c % 3][:, 4 * h:4 * h + 4, :], cond0[c % 2])
            for c in range(4):
                b = done(dve, f"mc{c}")
                d0 = (8, 12, 0, 4)[c]
                v.tensor_tensor(mod1[:, d0:d0 + 4], b[:, 0:4], par[:, 8 + 4 * c:12 + 4 * c], ALU.add
                                ).then_inc(sem("mc_ready"), 1)
            dve.wait_ge(sem("mc_ready"), 4)
            v.scalar_tensor_tensor(out=mod1[:, 0:8], in0=mod1[:, 0:8], scalar=1.0, in1=par[:, 0:8], op0=ALU.add,
                                   op1=ALU.mult).then_inc(sem("mod1_ready"), 1)
            dve.wait_ge(sem("wsm_hi_ready"), 1)
            v.tensor_tensor(wsm_lo, wsm, wsm_hi.bitcast(F32), ALU.subtract).then_inc(sem("wsm_ready"), 1)
            for j in range(8):
                dve.wait_ge(sem("h32_ready"), j + 1)
                dve.wait_ge(sem("hT_ready"), j + 1)
                v.tensor_tensor(hT_lo[:, j, :], h32[j % 2], hT_hi[:, j, :].bitcast(F32), ALU.subtract
                                ).then_inc(sem("hT_lo_ready"), 1)
            split_lo("w_qa")
            split_lo("w_ka")

            dve.wait_ge(sem("small_ready"), 1)
            for f in range(2):
                b = done(dve, f"la{f}")
                v.tensor_scalar(arg[0][:, f, :], b[:, :], par[:, 24 + f:25 + f], None, ALU.add).then_inc(sem("z_ready"), 1)
            dve.wait_ge(sem("z_ready"), 2)
            for f in range(2):
                dve.wait_ge(sem("lnz_ready"), f + 1)
                link(v.scalar_tensor_tensor(out=arg[1][:, f, :], in0=arg[0][:, f, :], scalar=0.0, in1=decay[:, f, :],
                                            op0=ALU.min, op1=ALU.subtract))
                link(v.tensor_scalar(arg[1][:, f, :], arg[1][:, f, :], 1.0 / 16.0, None, ALU.mult))
                ins = v.tensor_tensor_scan(cum[:, f, :], resets, arg[1][:, f, :], 0.0, ALU.mult, ALU.add)
                if f == 0:
                    link(ins)
            ins.then_inc(sem("cum_ready"), 1)
            dve.wait_ge(sem("cum_ready"), 1)
            for f in range(2):
                b = done(dve, f"ka{f}")
                v.tensor_copy(kT[:, f, :], b[:, :]).then_inc(sem("ka_ready"), 1)
            split_lo("w_va0")
            split_lo("w_va1")
            c8 = cum.rearrange("p f (i t) -> p (f i) t", t=P)
            a8 = arg[0].rearrange("p f (i t) -> p (f i) t", t=P)
            v.tensor_tensor(a8, c8[:, :, P - 1:P].to_broadcast([P, 8, P]), c8, ALU.subtract).then_inc(sem("kdarg_ready"), 1)
            for q in range(2):
                for i in range(TT):
                    b = done(dve, f"va{q}{i}")
                    v.tensor_copy(va[:, i, 256 * q:256 * q + 256], b[:, 0:256]).then_inc(sem("v_ready"), 1)
            dve.wait_ge(sem("cleared"), 1)
            dve.wait_ge(sem("ecum_ready"), 1)
            dve.wait_ge(sem("qa_ready"), 2)
            for p in range(2):
                r = slice(64 * p, 64 * p + 64)
                v.tensor_tensor(qcz[p][r], qT[r], ecum[r], ALU.mult)
            dve.wait_ge(sem("ka_ready"), 2)
            dve.wait_ge(sem("kdE_ready"), 1)
            v.tensor_tensor(decay, decay, kT, ALU.mult).then_inc(sem("kd_ready"), 1)

            def level_arg(l):
                h = (P // 2) >> l
                cv = cum.rearrange("p f t -> p (f t)").rearrange("p (n b) -> p n b", b=2 * h)
                av = arg[l % 2].rearrange("p f t -> p (f t)").rearrange("p (n b) -> p n b", b=2 * h)
                ref = cv[:, :, h - 1:h].to_broadcast([P, 1024 // (2 * h), h])
                if l == 0:
                    dve.wait_ge(sem("kdE_ready"), 1)
                v.tensor_tensor(av[:, :, 0:h], ref, cv[:, :, 0:h], ALU.subtract)
                v.tensor_tensor(av[:, :, h:2 * h], cv[:, :, h:2 * h], ref, ALU.subtract).then_inc(sem("arg_ready"), 1)

            def level_mul(l):
                h = (P // 2) >> l
                dve.wait_ge(sem("E_ready"), l + 1)
                if l >= 2:
                    dve.wait_ge(sem("products_done"), number[f"scA{l - 2}3"] + 1)

                def halves(t):
                    return t.rearrange("p f t -> p (f t)").rearrange("p (n b) -> p n b", b=2 * h)

                v.tensor_tensor(halves(kE[l % 2])[:, :, 0:h], halves(kT)[:, :, 0:h], halves(decay)[:, :, 0:h], ALU.mult)
                v.tensor_tensor(halves(qE[l % 2])[:, :, h:2 * h], halves(qT)[:, :, h:2 * h],
                                halves(decay)[:, :, h:2 * h], ALU.mult).then_inc(sem("level_ready"), 1)

            def level_merge(l):
                m = level_mask[:, l:l + 1, :].to_broadcast([P, 4, P])
                for g in range(4):
                    b = done(dve, f"scA{l}{g}")
                    if l:
                        dve.wait_ge(sem("intra_done"), 4 * (l - 1) + g + 1)
                    tp = g % 2
                    v.copy_predicated(S[:, g // 2, 2 * tp:2 * tp + 2, :, :].rearrange("p i f t -> p (i f) t"), m,
                                      b[:, :].rearrange("p (n t) -> p n t", t=P)).then_inc(sem("intra_done"), 1)

            level_arg(0)
            for i in range(3):
                for f in range(2):
                    b = done(dve, f"st{i}{f}")
                    for p in range(2):
                        r = slice(64 * p, 64 * p + 64)
                        if i == 0:
                            ins = v.tensor_copy(state[r, i, f, :], b[r, tile_cols(p)])
                        else:
                            ins = v.scalar_tensor_tensor(out=state[r, i, f, :], in0=state[r, i - 1, f, :],
                                                         scalar=ecum[r, f, P * i + P - 1:P * i + P],
                                                         in1=b[r, tile_cols(p)], op0=ALU.mult, op1=ALU.add)
                    ins.then_inc(sem("state_ready"), 1)
                dve.wait_ge(sem("state_ready"), 2 * i + 2)
            for l in range(7):
                level_mul(l)
                if l < 6:
                    level_arg(l + 1)
                if l:
                    level_merge(l - 1)
                if l in (4, 5):
                    split_lo(f"w_ga{l - 4}")
            level_merge(6)
            level_merge(7)
            split_lo("w_qkc0")
            split_lo("w_qkc1")
            dve.wait_ge(sem("outgate_ready"), 4)
            for h in range(4):
                dve.wait_ge(sem("root_ready"), h + 1)
                if h:
                    dve.wait_ge(sem("oTA_ready"), h)
                link(v.reciprocal(hA, rsA[h % 2]))
                b = done(dve, f"oA{h}")
                v.scalar_tensor_tensor(out=hA, in0=b[:, :], scalar=par[:, 26 + h:27 + h], in1=hA, op0=ALU.mult,
                                       op1=ALU.mult).then_inc(sem("oA_read"), 1)
                dve.wait_ge(sem("oA_read"), h + 1)
                v.tensor_tensor(oT[0][:, h, :], hA, sga[:, h, :], ALU.mult).then_inc(sem("oTA_ready"), 1)
            dve.wait_ge(sem("oTA_ready"), 4)
            for c in range(3):
                further_columns(c)

            fb, lnf, G, u, M, mt, ib, lf = g4
            link(v.tensor_copy(fb, small[96:100, :]))
            link(v.tensor_copy(ib, small[64:68, :]))
            v.tensor_scalar(fb, fb, bif[:, 1:2], None, ALU.add).then_inc(sem("fb_ready"), 1)
            dve.wait_ge(sem("fb_ready"), 1)
            link(v.tensor_scalar(ib, ib, bif[:, 0:1], None, ALU.add))
            dve.wait_ge(sem("cleared"), 2)
            dve.wait_ge(sem("lnf_ready"), 1)
            link(v.scalar_tensor_tensor(out=lf, in0=fb, scalar=0.0, in1=lnf, op0=ALU.min, op1=ALU.subtract))
            link(v.tensor_tensor_scan(G, ones4, lf, 0.0, ALU.mult, ALU.add))
            link(v.tensor_tensor(u, ib, G, ALU.subtract))
            link(v.tensor_tensor_scan(M, ones4, u, 0.0, ALU.mult, ALU.max))
            v.tensor_tensor(mt, G, M, ALU.add).then_inc(sem("scans_ready"), 1)
            for f in range(4):
                b = done(dve, f"qk{f}")
                v.tensor_copy(raw[:, f, 3:515], b[:, :]).then_inc(sem("qk_ready"), 1)
                dve.wait_ge(sem("qk_ready"), f + 1)
                link(v.tensor_scalar(qkc[:, f, :], raw[:, f, 0:512], par[:, 37 + f:38 + f], None, ALU.mult))
                for k in range(1, 4):
                    ins = v.scalar_tensor_tensor(out=qkc[:, f, :], in0=raw[:, f, k:k + 512],
                                                 scalar=par[:, 37 + 4 * k + f:38 + 4 * k + f], in1=qkc[:, f, :],
                                                 op0=ALU.mult, op1=ALU.add)
                    if k < 3:
                        link(ins)
                ins.then_inc(sem("conv_ready"), 1)
                if f >= 2:
                    split_lo(f"w_vc{f - 2}")
            b = done(dve, "uT")
            v.tensor_copy(ucol, b[:, 0:16].rearrange("p (i h) -> p i h", i=TT)).then_inc(sem("u_ready"), 1)
            for q in range(2):
                for i in range(TT):
                    b = done(dve, f"vc{q}{i}")
                    v.tensor_copy(vc[:, i, 256 * q:256 * q + 256], b[:, 0:256]).then_inc(sem("v_ready"), 1)
                split_lo(f"w_oc{q}")
            dve.wait_ge(sem("u_ready"), 1)

            dve.wait_ge(sem("wki_hi_ready"), 1)
            v.tensor_tensor(wki_lo[:, :, :], wki[:, :, :], wki_hi[:, :, :].bitcast(F32), ALU.subtract).then_inc(sem("wki_ready"), 1)
            split_lo("w_cl0")

            def latent(n):
                b = done(dve, f"cl{n}")
                v.tensor_copy(craw[:, n, :], b[:, :]).then_inc(sem("craw_ready"), 1)

            def finish_c(h):
                dve.wait_ge(sem("root_ready"), h + 5)
                link(v.reciprocal(hD, rsC))
                link(v.scalar_tensor_tensor(out=hD, in0=hC, scalar=par[:, 33 + h:34 + h], in1=hD, op0=ALU.mult,
                                            op1=ALU.mult))
                dve.wait_ge(sem("outgate_ready"), h + 5)
                v.tensor_tensor(oT[2][:, h, :], hD, soc[:, h, :], ALU.mult).then_inc(sem("oTC_ready"), 1)
                dve.wait_ge(sem("oTC_ready"), h + 1)

            for h in range(4):
                def arg_c(j):
                    n = 4 * h + j
                    bm = done(dve, f"bm{h}")
                    if n >= 2:
                        dve.wait_ge(sem("W_ready"), n - 1)
                    v.tensor_scalar(argC[n % 2][:, 0:T - P * j], bm[:, P * j:T], ucol[:, j, h:h + 1], 0.0,
                                    ALU.subtract, ALU.max).then_inc(sem("argC_ready"), 1)

                arg_c(0)
                if h:
                    dve.wait_ge(sem("products_done"), number[f"den{h - 1}"] + 1)
                for j in range(TT):
                    if j < 3:
                        arg_c(j + 1)
                    n = 4 * h + j
                    dve.wait_ge(sem("W_ready"), n + 1)
                    link(v.tensor_tensor(W[n % 2][:, 0:P], W[n % 2][:, 0:P], causal[:, :], ALU.mult))
                    b = done(dve, f"scC{h}{j}")
                    v.scalar_tensor_tensor(out=SW[:, j, P * j:T], in0=b[:, P * j:T], scalar=0.125,
                                           in1=W[n % 2][:, 0:T - P * j], op0=ALU.mult, op1=ALU.mult
                                           ).then_inc(sem("SW_ready"), 1)
                if h:
                    finish_c(h - 1)
                dve.wait_ge(sem("floor_ready"), h + 1)
                b = done(dve, f"den{h}")
                link(v.scalar_tensor_tensor(out=hD, in0=b[:, :], scalar=-1.0, in1=floor_, op0=ALU.mult, op1=ALU.max))
                v.tensor_tensor(hD, b[:, :], hD, ALU.max).then_inc(sem("den_read"), 1)
                dve.wait_ge(sem("den_read"), h + 1)
                link(v.reciprocal(hD, hD))
                b = done(dve, f"num{h}")
                v.tensor_tensor(hC, b[:, :], hD, ALU.mult).then_inc(sem("hC_ready"), 1)
                dve.wait_ge(sem("hC_ready"), h + 1)
                if h == 0:
                    split_lo("w_cl1")
                else:
                    latent(h - 1)
            finish_c(3)
            dve.wait_ge(sem("oTC_ready"), 4)

            v.tensor_copy(wi0[:, :], small[32:40, :]).then_inc(sem("wi0_ready"), 1)
            b = done(dve, "wi")
            v.tensor_scalar(wcol[:, :, :], b[:, 0:32].rearrange("p (i h) -> p i h", i=TT), float(8 ** -0.5), None,
                            ALU.mult).then_inc(sem("wcol_ready"), 1)
            b = done(dve, "uk")
            v.tensor_copy(ukT, b[:, :].rearrange("p (i h) -> p i h", i=4)).then_inc(sem("ukT_ready"), 1)
            dve.wait_ge(sem("craw_ready"), 3)
            for n in range(2):
                dve.wait_ge(sem("root_ready"), n + 9)
                link(v.reciprocal(rsB[:, n, :], rsB[:, n, :]))
                for k in (0, 1) if n == 0 else (2,):
                    ins = v.scalar_tensor_tensor(out=cn[:, k, :], in0=craw[:, k, :], scalar=par[:, 30 + k:31 + k],
                                                 in1=rsB[:, n, :], op0=ALU.mult, op1=ALU.mult)
                ins.then_inc(sem("cn_ready"), 1)
            dve.wait_ge(sem("wcol_ready"), 1)
            dve.wait_ge(sem("cleared"), 3)
            link(v.tensor_scalar(selm[:, 0:P], future[:, :], 0.0, None, ALU.is_equal))
            v.copy_predicated(Dm[:, 0, 0:P], selm[:, 0:P], distv[:, 384:384 + P]).then_inc(sem("D_ready"), 1)
            for i in range(1, TT):
                N = P * (i + 1)
                for h in range(8):
                    n = 8 * (i - 1) + h
                    dve.wait_ge(sem("relu_ready"), n + 1)
                    if h == 0:
                        ins = v.tensor_scalar(I_s[:, 0:N], rl[n % 2][:, 0:N], wcol[:, i, 0:1], None, ALU.mult)
                    else:
                        ins = v.scalar_tensor_tensor(out=I_s[:, 0:N], in0=rl[n % 2][:, 0:N], scalar=wcol[:, i, h:h + 1],
                                                     in1=I_s[:, 0:N], op0=ALU.mult, op1=ALU.add)
                    ins.then_inc(sem("relu_used"), 1)
                    dve.wait_ge(sem("relu_used"), n + 1)
                link(v.copy_predicated(I_s[:, P * i:N], future[:, :], negc[:, :]))
                if i == TT - 1:
                    for c in range(3, 8):
                        further_columns(c)
                for _ in range(KEYS // 8):
                    link(v.max(top8[:, :], I_s[:, 0:N]))
                    link(v.match_replace(I_s[:, 0:N], top8[:, :], I_s[:, 0:N], NEG_TAKEN))
                link(v.tensor_scalar(selm[:, 0:N], I_s[:, 0:N], -2e38, None, ALU.is_lt))
                off = 384 - P * i
                v.copy_predicated(Dm[:, i, 0:N], selm[:, 0:N], distv[:, off:off + N]).then_inc(sem("D_ready"), 1)
            dve.wait_ge(sem("D_ready"), 4)
            for n in range(-1, 8):
                if n >= 0:
                    i, g = divmod(n, 2)
                    r_ = slice(4 * g, 4 * g + 4)
                    dve.wait_ge(sem("exp_ready"), 4 * n + 4)
                    link(v.reciprocal(top8[:, r_], psum[:, r_]))
                    v.tensor_tensor(Pn[:, r_, 0:P * (i + 1)], Pn[:, r_, 0:P * (i + 1)],
                                    top8[:, r_].rearrange("p (h o) -> p h o", o=1).to_broadcast([P, 4, P * (i + 1)]),
                                    ALU.mult).then_inc(sem("P_ready"), 1)
                if n < 7:
                    i, g = divmod(n + 1, 2)
                    N = P * (i + 1)
                    for h in range(4 * g, 4 * g + 4):
                        e = 8 * i + h
                        b = done(dve, f"lg{i}{h}")
                        if e >= 2:
                            dve.wait_ge(sem("exp_ready"), e - 1)
                        v.scalar_tensor_tensor(out=L[e % 2][:, 0:N], in0=Dm[:, i, 0:N], scalar=float(2.0 ** -(h + 1)),
                                               in1=b[:, 0:N], op0=ALU.mult, op1=ALU.add).then_inc(sem("L_ready"), 1)
                        dve.wait_ge(sem("L_ready"), e + 1)
                        v.tensor_reduce(nmax[:, h:h + 1], L[e % 2][:, 0:N], AX, ALU.max, negate=True
                                        ).then_inc(sem("nmax_ready"), 1)
                if n >= 0:
                    i, g = divmod(n, 2)
                    b = done(dve, f"ol{i}{g}")
                    v.tensor_copy(olT[:, 4 * g:4 * g + 4, tile_cols(i)], b[:, :].rearrange("p (h t) -> p h t", h=4)
                                  ).then_inc(sem("ol_ready"), 1)
                if n == 4:
                    split_lo("wg0")
                    split_lo("wu0")

            dve.wait_ge(sem("oTB_ready"), 4)
            dve.wait_ge(sem("mb_ready"), 8)

            def diagonals(c):
                cols_ = modcol[:, 4 * c:4 * c + 4].rearrange("p (m o) -> p m o", o=1).to_broadcast([P, 4, P])
                if c >= 2:
                    done(dve, f"mr{c - 2}")
                v.tensor_tensor(cond_merge[c % 2].rearrange("p (m t) -> p m t", m=4),
                                ident[:, :].rearrange("p (o t) -> p o t", o=1).to_broadcast([P, 4, P]), cols_,
                                ALU.mult).then_inc(sem("diag_ready"), 1)

            for n, (m, br) in enumerate(merge_steps()):
                if n < 3:
                    dve.wait_ge(sem("oT_hi_ready"), n + 1)
                    v.tensor_tensor(oT_lo[n][:, :, :], oT[n][:, :, :], oT_hi[n].bitcast(F32), ALU.subtract
                                    ).then_inc(sem("oT_lo_ready"), 1)
                if n < 8:
                    diagonals(n)
                names = (f"wg{n + 1}", f"wu{n + 1}") if n < 11 else ("wo0", "wo1")
                split_lo(names[0])
                for r in range(2):
                    dve.wait_ge(sem("gate_ready"), 2 * n + r + 1)
                    b = done(dve, f"up{m + r}{br}")
                    dst = mT[:, m + r, :] if br == 0 else mtmp[r]
                    v.tensor_tensor(dst, b[:, :], sgate[r], ALU.mult).then_inc(sem("up_read"), 1)
                    dve.wait_ge(sem("up_read"), 2 * n + r + 1)
                    if br:
                        ins = v.tensor_tensor(mT[:, m + r, :], mT[:, m + r, :], mtmp[r], ALU.add)
                        if br == 1:
                            link(ins)
                        else:
                            ins.then_inc(sem("mT_ready"), 1)
                split_lo(names[1])
                if br == 2:
                    for r in range(2):
                        dve.wait_ge(sem("mT_ready"), m + r + 1)
                        dve.wait_ge(sem("mT_hi_ready"), m + r + 1)
                        v.tensor_tensor(mT_lo[:, m + r, :], mT[:, m + r, :], mT_hi[:, m + r, :].bitcast(F32), ALU.subtract
                                        ).then_inc(sem("mT_lo_ready"), 1)
                if n < 8:
                    b = done(dve, f"mr{n}")
                    s_ = slice(512 * (n % 2), 512 * (n % 2) + 512)
                    dst = modB[:, n // 2, s_]
                    dve.wait_ge(sem("extra_loaded"), 96)
                    v.tensor_tensor(dst, dst, b[:, :], ALU.add).then_inc(sem("mr_ready"), 1)
                    dve.wait_ge(sem("mr_ready"), n + 1)
                    if n // 2 == 2:
                        link(v.scalar_tensor_tensor(out=dst, in0=dst, scalar=1.0, in1=nffn[:, s_], op0=ALU.add,
                                                    op1=ALU.mult))
            dve.wait_ge(sem("x_loaded"), 32)
            split_lo("wo2")
            for k, (i, q) in enumerate(wo_order()):
                if k == 4:
                    split_lo("wo3")
                b = done(dve, f"wo{i}{q}")
                s_ = slice(256 * q, 256 * q + 256)
                v.tensor_tensor(wtmp[:, 0:256], b[:, 0:256], modB[:, 0, s_], ALU.mult).then_inc(sem("wo_read"), 1)
                dve.wait_ge(sem("wo_read"), k + 1)
                ins = v.tensor_tensor(x[:, i, s_], x[:, i, s_], wtmp[:, 0:256], ALU.add)
                if q < 3:
                    link(ins)
                    continue
                ins.then_inc(sem("x2_ready"), 1)
                dve.wait_ge(sem("x2_ready"), i + 1)
                dve.wait_ge(sem("rms_ready"), i + 2)
                link(v.reciprocal(stat[:, 12 + i:13 + i], stat[:, 12 + i:13 + i]))
                link(v.scalar_tensor_tensor(out=h2[:, i, :], in0=x[:, i, :], scalar=stat[:, 12 + i:13 + i],
                                            in1=modB[:, 2, :], op0=ALU.mult, op1=ALU.mult))
                v.tensor_tensor(h2[:, i, :], h2[:, i, :], modB[:, 1, :], ALU.add).then_inc(sem("h2_ready"), 1)

            dve.wait_ge(sem("rt_ready"), TT)
            bias = rbias[:, :].rearrange("p (o e) -> p o e", o=1).to_broadcast([P, TT, E])
            link(v.tensor_tensor(selr, score, bias, ALU.add))
            by_group = selr.rearrange("p i (g e) -> p (i g) e", g=GROUPS)
            for q in range(TT * GROUPS):
                ins = v.max(gtop[:, q, :], by_group[:, q, :])
            link(ins)
            link(v.tensor_tensor(gsc.rearrange("p i g -> p (i g)"), gtop[:, :, 0], gtop[:, :, 1], ALU.add))
            for i in range(TT):
                ins = v.max(gm8[:, i, :], gsc[:, i, :])
            link(ins)
            for i in range(TT):
                ins = v.max_index(gidx[:, i, :], gm8[:, i, :], gsc[:, i, :])
            link(ins)
            link(v.tensor_copy(gidf, gidx))
            link(v.tensor_tensor(ghot, iota_e[:, 0:8].rearrange("p (a g b) -> p a g b", a=1, b=1).to_broadcast([P, TT, GROUPS, TOPG]),
                                 gidf[:, :, 0:TOPG].rearrange("p i (o k) -> p i o k", o=1).to_broadcast([P, TT, GROUPS, TOPG]),
                                 ALU.is_equal))
            link(v.tensor_reduce(gmask, ghot, AX, ALU.add))
            gb = gmask.rearrange("p i (g o) -> p (i g) o", o=1).to_broadcast([P, TT * GROUPS, 8])
            link(v.tensor_tensor(by_group, by_group, gb, ALU.mult))
            link(v.tensor_scalar(gmask, gmask, 1.0, 1e30, ALU.subtract, ALU.mult))
            link(v.tensor_tensor(by_group, by_group, gb, ALU.add))
            for i in range(TT):
                ins = v.max(em8[:, i, :], selr[:, i, :])
            link(ins)
            for i in range(TT):
                ins = v.max_index(eidx[:, i, :], em8[:, i, :], selr[:, i, :])
            link(ins)
            link(v.tensor_copy(eall[:, :, :], eidx))
            for i in range(TT):
                ins = v.tensor_tensor(onehot[:, i], iota_e.rearrange("p (o e) -> p o e", o=1).to_broadcast([P, TOPK, E]),
                                      eall[:, i, 0:TOPK].rearrange("p (k o) -> p k o", o=1).to_broadcast([P, TOPK, E]),
                                      ALU.is_equal)
            link(ins)
            for i in range(TT):
                v.tensor_reduce(mall[:, i, :], onehot[:, i].rearrange("p k e -> p e k"), AX, ALU.add
                                ).then_inc(sem("mall_ready"), 1)
            for i in range(TT):
                ins = v.tensor_tensor(picked[:, i], onehot[:, i], score[:, i:i + 1, :].to_broadcast([P, TOPK, E]), ALU.mult)
            link(ins)
            link(v.tensor_reduce(wk[:, :, 0:TOPK], picked, AX, ALU.add))
            link(v.tensor_reduce(wsum, wk[:, :, 0:TOPK], AX, ALU.add))
            link(v.reciprocal(wsum, wsum))
            for i in range(TT):
                v.tensor_scalar(wk[:, i, 0:TOPK], wk[:, i, 0:TOPK], wsum[:, i:i + 1], 2.5, ALU.mult, ALU.mult)

            def shared_act(m):
                dve.wait_ge(sem("sg_ready"), m + 1)
                b = done(dve, f"su{m}")
                v.tensor_tensor(actS[:, m, :], b[:, :], sgS[m], ALU.mult).then_inc(sem("actS_ready"), 1)

            shared_act(0)
            b = done(dve, "tot")
            link(v.tensor_scalar(ntile, b[:, 0:E], 0.0, None, ALU.is_gt))
            for q in range(1, TT - 1):
                link(v.scalar_tensor_tensor(out=ntile, in0=b[:, 0:E], scalar=float(P * q), in1=ntile, op0=ALU.is_gt,
                                            op1=ALU.add))
            v.scalar_tensor_tensor(out=ntile, in0=b[:, 0:E], scalar=float(P * (TT - 1)), in1=ntile, op0=ALU.is_gt,
                                   op1=ALU.add).then_inc(sem("tot_read"), 1)
            dve.wait_ge(sem("tot_read"), 1)
            link(v.memset(rt_tmp, 1.0))
            link(v.tensor_tensor_scan(uend, rt_tmp, ntile, 0.0, ALU.mult, ALU.add))
            link(v.tensor_tensor(base, uend, ntile, ALU.subtract))
            v.tensor_scalar(base, base, float(P), None, ALU.mult).then_inc(sem("uend_ready"), 1)
            dve.wait_ge(sem("uend_ready"), 1)
            b = done(dve, "ue")
            v.tensor_copy(ucolf[:, :], b[0:E, 0:1]).then_inc(sem("ue_ready"), 1)
            dve.wait_ge(sem("ue_ready"), 1)
            v.tensor_scalar(ucmp[:, :], iota_u, ucolf[:, 0:1], None, ALU.is_ge).then_inc(sem("ucmp_ready"), 1)
            b = done(dve, "uc")
            v.tensor_scalar(uexp[:, :], b[0:1, 0:96], float(E - 1), None, ALU.min).then_inc(sem("uc_ready"), 1)
            link(v.tensor_scalar(npf[:, :], iota_e[0:1], 2.0, uend[0:1, E - 1:E], ALU.mult, ALU.is_lt))
            link(v.tensor_reduce(npg[:, :], npf[:, :], AX, ALU.add))
            v.tensor_copy(npair[:, :], npg[:, :]).then_inc(sem("table_ready"), 1)
            for i in range(TT):
                b = done(dve, f"pos{i}")
                v.tensor_tensor(slotA, b[:, 0:E], base, ALU.add).then_inc(sem("slot_done"), 1)
                dve.wait_ge(sem("slot_done"), i + 1)
                link(v.tensor_tensor(picked[:, i], onehot[:, i], slotA.rearrange("p (o e) -> p o e", o=1).to_broadcast([P, TOPK, E]),
                                     ALU.mult))
                link(v.tensor_reduce(slotf[:, :], picked[:, i], AX, ALU.add))
                link(v.tensor_copy(sloti[:, 0, :], slotf[:, :]))
                v.tensor_scalar(sloti[:, 1, :], sloti[:, 0, :], 7, None, ALU.logical_shift_right)
                link(v.tensor_scalar(sloti[:, 2, :], sloti[:, 0, :], P - 1, None, ALU.bitwise_and))
                link(v.tensor_copy(placef[:, :, :], sloti[:, 1:3, :]))

                def spread(v_, n):
                    return v_.rearrange("p (k o) -> p k o", o=1).to_broadcast([P, TOPK, n])

                if i >= 2:
                    dve.wait_ge(sem("place_used"), i - 1)
                u_, r_ = is_unit[i % 2], is_row[i % 2]
                v.tensor_tensor(r_, iota[:, :].rearrange("p (o r) -> p o r", o=1).to_broadcast([P, TOPK, P]),
                                spread(placef[:, 1, :], P), ALU.is_equal)
                link(v.tensor_tensor(u_, iota[:, 0:LISTS].rearrange("p (o u) -> p o u", o=1).to_broadcast([P, TOPK, LISTS]),
                                     spread(placef[:, 0, :], LISTS), ALU.is_equal))
                v.tensor_tensor(u_, u_, spread(row1[:, i, :], LISTS), ALU.mult).then_inc(sem("place_ready"), 1)
                dve.wait_ge(sem("place_ready"), i + 1)
            b = done(dve, "lists")
            link(v.tensor_scalar(absent[:, :], b[:, 0:LISTS], 0.0, float(T * TOPK + 1), ALU.is_equal, ALU.mult))
            link(v.scalar_tensor_tensor(out=rows_y[:, :], in0=b[:, 0:LISTS], scalar=-1.0, in1=absent[:, :], op0=ALU.add,
                                        op1=ALU.add))
            link(v.tensor_scalar(toks[:, :], rows_y[:, :], T - 1, None, ALU.bitwise_and))
            v.tensor_tensor(toks[:, :], toks[:, :], absent[:, :], ALU.add).then_inc(sem("lists_ready"), 1)
            shared_act(1)
            def weights_lo(u, c, k, part=slice(0, 2048), last=True):
                dve.wait_ge(sem("hi_ready"), 3 * u + k + 1)
                ins = v.tensor_tensor(w_lo[c][k][:, part], w_raw[c][k][:, part], w_hi[c][k][:, part].bitcast(F32), ALU.subtract)
                if last:
                    ins.then_inc(sem("lo_ready"), 1)

            for k in range(3):
                weights_lo(0, 0, k)
            for i in range(TT):
                for n in range(2):
                    b = done(dve, f"sd{i}{n}")
                    v.tensor_tensor(wtmp2, b[:, :], modB[:, 3, 512 * n:512 * n + 512], ALU.mult).then_inc(sem("sd_read"), 1)
                    dve.wait_ge(sem("sd_read"), 2 * i + n + 1)
                    dst = x[:, i, 512 * n:512 * n + 512]
                    v.tensor_tensor(dst, dst, wtmp2, ALU.add).then_inc(sem("x_added"), 1)
                    dve.wait_ge(sem("x_added"), 2 * i + n + 1)
            dve.wait_ge(sem("table_ready"), 1)
            dve.wait_ge(sem("x_added"), 8)
            pairs = dve.value_load(npair[0:1, 0:1], min_val=1, max_val=UNITS // 2)

            def turned(u, c, half):
                dve.wait_ge(sem("xe_hi_ready"), 2 * u + half + 1)
                s_ = slice(512 * half, 512 * half + 512)
                v.tensor_tensor(xe_lo[c][:, s_], bank[half][:, :], xe_hi[c][:, s_].bitcast(F32), ALU.subtract
                                ).then_inc(sem("xe_lo_ready"), 1)

            for half in range(2):
                turned(0, 0, half)
            with dve.Fori(0, pairs) as i:
                for b in range(2):
                    c, u = 1 - b, 2 * i + b
                    weights_lo(u + 1, c, 0)
                    weights_lo(u + 1, c, 1, slice(0, D), False)
                    dve.wait_ge(sem("sge_ready"), u + 1)
                    v.tensor_tensor(acte[b], bank[2][:, FF:2 * FF], sge[b], ALU.mult).then_inc(sem("acte_ready"), 1)
                    turned(u + 1, c, 0)
                    dve.wait_ge(sem("ae_hi_ready"), u + 1)
                    v.tensor_tensor(ae_lo[b], bank[3][:, 0:FF].rearrange("p (m t) -> p m t", m=2), ae_hi[b].bitcast(F32),
                                    ALU.subtract).then_inc(sem("ae_lo_ready"), 1)
                    turned(u + 1, c, 1)
                    weights_lo(u + 1, c, 1, slice(D, 2 * D))
                    weights_lo(u + 1, c, 2)
            dve.wait_ge(sem("extra_loaded"), 112)
            def final_norm(i):
                dve.wait_ge(sem("rms_ready"), i + 6)
                link(v.reciprocal(stat[:, 4 + i:5 + i], stat[:, 4 + i:5 + i]))
                v.scalar_tensor_tensor(out=x[:, i, :], in0=x[:, i, :], scalar=stat[:, 4 + i:5 + i], in1=nfin,
                                       op0=ALU.mult, op1=ALU.mult).then_inc(sem("out_ready"), 1)

            n = 0
            for i in range(TT):
                r_ = routed[i % 2]
                dve.wait_ge(sem("first_ready"), i + 1)
                for k in range(1, TOPK):
                    n += 1
                    dve.wait_ge(sem(f"yk_loaded{i % 2}{k // 3}"), 16 * (i // 2 + 1))
                    v.scalar_tensor_tensor(out=r_, in0=yk[i % 2][:, k, :], scalar=wk[:, i, k:k + 1], in1=r_,
                                           op0=ALU.mult, op1=ALU.add).then_inc(sem("yk_used"), 1)
                    dve.wait_ge(sem("yk_used"), n)
                link(v.tensor_tensor(r_, r_, modB[:, 3, :], ALU.mult))
                v.tensor_tensor(x[:, i, :], x[:, i, :], r_, ALU.add).then_inc(sem("x4_ready"), 1)
                dve.wait_ge(sem("x4_ready"), i + 1)
                if i:
                    final_norm(i - 1)
            final_norm(TT - 1)


_INS = ['x', 'c', 'ada_w', 'ada_b', 'norm_mix', 'norm_ffn', 'w_in', 'gla_w_a2', 'gla_b_a', 'gla_norm',
        'dsa_norm_q', 'dsa_norm_kv', 'dsa_w_uq', 'dsa_w_uk', 'dsa_w_uv', 'dsa_w_qi', 'mlstm_conv', 'mlstm_b_i',
        'mlstm_b_f', 'mlstm_norm', 'w_up_a', 'w_up_b', 'w_up_c', 'w_o', 'router_w', 'router_bias', 'exp_w_gate',
        'exp_w_up', 'exp_w_down', 'sh_w_gate', 'sh_w_up', 'sh_w_down', 'norm_final']


def kernel(**inputs):
    import numpy as _np
    import concourse.bacc as _bacc
    from concourse import mybir as _mybir
    from concourse.bass_utils import run_bass_kernel_spmd as _run

    nc = _bacc.Bacc("TRN2", target_bir_lowering=False, num_devices=1)
    arrays, aps = {}, {}
    for name in _INS:
        v = _np.ascontiguousarray(inputs[name])
        arrays[f"in_{name}"] = v
        aps[name] = nc.dram_tensor(f"in_{name}", v.shape, _mybir.dt.from_np(v.dtype), kind="ExternalInput").ap()
    shape = inputs["x"].shape
    out = nc.dram_tensor("out_0", shape, _mybir.dt.float32, kind="ExternalOutput").ap()
    hybrid_kernel(nc, aps, out)
    r = _run(nc, [arrays], core_ids=[0])
    return r.results[0]["out_0"]
```
